# Optimizing a Trainium2 kernel written in Bass

```python
import jax, jax.numpy as jnp
from jax import lax
import numpy as np

D_MODEL = 1024
BATCH = 1
SEQ = 1024
DEPTH = 2
DEC_BATCH = 8
DEC_SEQ = 16
PAST_LEN = 512

CHUNK = 64
HEAD_DIM = 64
D_MIX = D_MODEL
H_M = 4
GROUP_HEADS = (D_MIX // HEAD_DIM - H_M) // 3
H_A = GROUP_HEADS
H_B = GROUP_HEADS
H_C = GROUP_HEADS
W_A = H_A * HEAD_DIM
W_B = H_B * HEAD_DIM
W_C = H_C * HEAD_DIM
W_M = H_M * HEAD_DIM
ROT_DIM = HEAD_DIM // 4
ROPE_THETA = 500000.0
H_IDX = 4
D_IDX = HEAD_DIM
TOPK_MAX = 256
Q_BLOCK = 128
BAND_CHUNKS = 8
BAND = BAND_CHUNKS * CHUNK
REL_CLIP = 128
N_MEM = 256
EPS = 1e-6
F32 = jnp.float32

IN_SPLITS = (('a_q', W_A), ('a_k', HEAD_DIM), ('a_v', HEAD_DIM), ('a_qi', H_IDX * D_IDX), ('a_ki', D_IDX),
             ('a_wi', H_IDX), ('a_g', W_A),
             ('b_q', W_B), ('b_k', W_B), ('b_v', W_B), ('b_f', H_B), ('b_g', W_B),
             ('c_q', W_C), ('c_k', W_C), ('c_v', W_C), ('c_g', W_C),
             ('m_q', W_M), ('m_g', W_M))
D_IN = sum(size for _, size in IN_SPLITS)

kernel_name = 'hybrid_streaming_encoder_step'

def rmsnorm(x, g):
    xf = x.astype(F32)
    y = xf * lax.rsqrt(jnp.mean(xf * xf, axis=-1, keepdims=True) + EPS)
    return (y * g.astype(F32)).astype(x.dtype)

def rope_partial(x, pos):
    half = ROT_DIM // 2
    inv = ROPE_THETA ** (-jnp.arange(half, dtype=F32) / half)
    ang = pos.astype(F32)[:, None] * inv[None, :]
    shape = (ang.shape[0],) + (1,) * (x.ndim - 3) + (half,)
    cos = jnp.cos(ang).reshape(shape)
    sin = jnp.sin(ang).reshape(shape)
    xr = x[..., :ROT_DIM].astype(F32)
    x1, x2 = xr[..., :half], xr[..., half:]
    rot = jnp.concatenate([x1 * cos - x2 * sin, x2 * cos + x1 * sin], axis=-1).astype(x.dtype)
    return jnp.concatenate([rot, x[..., ROT_DIM:]], axis=-1)

def split_proj(p):
    offs = np.cumsum([s for _, s in IN_SPLITS])[:-1].tolist()
    return dict(zip([n for n, _ in IN_SPLITS], jnp.split(p, offs, axis=-1)))

def a_inputs(p, pos):
    lead = p['a_q'].shape[:2]
    qa = rope_partial(p['a_q'].reshape(lead + (H_A, HEAD_DIM)), pos)
    ka = rope_partial(p['a_k'], pos)
    qi = rope_partial(p['a_qi'].reshape(lead + (H_IDX, D_IDX)), pos)
    ki = rope_partial(p['a_ki'], pos)
    return qa, ka, p['a_v'], qi, ki, p['a_wi']

def b_inputs(p, bf):
    lead = p['b_q'].shape[:2]
    heads = lambda t: t.reshape(lead + (H_B, HEAD_DIM))
    lf = jax.nn.log_sigmoid(p['b_f'].astype(F32) + bf.astype(F32))
    return heads(p['b_q']), heads(p['b_k']), heads(p['b_v']), lf

def c_inputs(p):
    lead = p['c_q'].shape[:2]
    heads = lambda t: t.reshape(lead + (H_C, HEAD_DIM))
    return heads(p['c_q']), heads(p['c_k']), heads(p['c_v'])

def m_query(p):
    return p['m_q'].reshape(p['m_q'].shape[:2] + (H_M, HEAD_DIM))

def mem_kv(mem, g, w):
    kv = rmsnorm(mem, g) @ w
    lead = kv.shape[:2]
    mk, mv = jnp.split(kv, 2, axis=-1)
    return mk.reshape(lead + (H_M, HEAD_DIM)), mv.reshape(lead + (H_M, HEAD_DIM))

def dsa_attend(q, qi, wi, lim, k, v, ki, topk):
    L = k.shape[1]
    dots = jnp.einsum('bqhd,bld->bqhl', qi.astype(F32), ki.astype(F32)) * D_IDX ** -0.5
    score = jnp.einsum('bqh,bqhl->bql', wi.astype(F32) * H_IDX ** -0.5, jax.nn.relu(dots))
    admissible = jnp.arange(L)[None, :] < lim[:, None]
    score = jnp.where(admissible[None], score, -jnp.inf)
    top_s, top_i = lax.top_k(score, topk)
    valid = jnp.isfinite(top_s)
    ks = jax.vmap(lambda kk, ii: kk[ii])(k, top_i)
    vs = jax.vmap(lambda vv, ii: vv[ii])(v, top_i)
    logits = jnp.einsum('bqhd,bqkd->bqhk', q.astype(F32), ks.astype(F32)) * HEAD_DIM ** -0.5
    logits = jnp.where(valid[:, :, None, :], logits, -jnp.inf)
    prob = jax.nn.softmax(logits, axis=-1)
    return jnp.einsum('bqhk,bqkd->bqhd', prob, vs.astype(F32)).astype(q.dtype)

def dsa_prompt(q, qi, wi, k, v, ki):
    B, S = q.shape[:2]
    nb = S // Q_BLOCK
    pos = jnp.arange(S)
    lim = jnp.minimum((pos // CHUNK + 1) * CHUNK, S)
    topk = min(TOPK_MAX, S // 4)
    blk = lambda t: t.reshape((B, nb, Q_BLOCK) + t.shape[2:]).swapaxes(0, 1)
    o = lax.map(lambda a: dsa_attend(a[0], a[1], a[2], a[3], k, v, ki, topk),
                (blk(q), blk(qi), blk(wi), lim.reshape(nb, Q_BLOCK)))
    return o.swapaxes(0, 1).reshape(q.shape)

def fox_attend(q, k, v, fq, fk, qpos, kpos):
    logits = jnp.einsum('bqhd,bkhd->bhqk', q.astype(F32), k.astype(F32)) * HEAD_DIM ** -0.5
    logits = logits + jnp.swapaxes(fq, 1, 2)[..., :, None] - jnp.swapaxes(fk, 1, 2)[..., None, :]
    logits = jnp.where((kpos[None, :] <= qpos[:, None])[None, None], logits, -jnp.inf)
    prob = jax.nn.softmax(logits, axis=-1)
    return jnp.einsum('bhqk,bkhd->bqhd', prob, v.astype(F32)).astype(q.dtype)

def fox_prompt(q, k, v, F):
    B, S, H, D = q.shape
    nb = S // Q_BLOCK
    pos = jnp.arange(S)
    blk = lambda t: t.reshape((B, nb, Q_BLOCK) + t.shape[2:]).swapaxes(0, 1)
    o = lax.map(lambda a: fox_attend(a[0], k, v, a[1], F, a[2], pos),
                (blk(q), blk(F), pos.reshape(nb, Q_BLOCK)))
    return o.swapaxes(0, 1).reshape(q.shape)

def band_bias_mask(tab, qpos, kpos):
    rel = qpos[..., :, None] - kpos[..., None, :]
    idx = jnp.clip(rel, -REL_CLIP, REL_CLIP) + REL_CLIP
    bias = jnp.moveaxis(tab.astype(F32)[:, idx], 0, -3)
    qc = qpos[..., :, None] // CHUNK
    kc = kpos[..., None, :] // CHUNK
    mask = (kpos[..., None, :] >= 0) & (kc <= qc) & (kc >= qc - BAND_CHUNKS)
    return bias, mask

def band_attend(q, k, v, bias, mask):
    logits = jnp.einsum('...qhd,...khd->...hqk', q.astype(F32), k.astype(F32)) * HEAD_DIM ** -0.5 + bias
    logits = jnp.where(mask[..., None, :, :], logits, -jnp.inf)
    prob = jax.nn.softmax(logits, axis=-1)
    return jnp.einsum('...hqk,...khd->...qhd', prob, v.astype(F32)).astype(q.dtype)

def band_prompt(q, k, v, tab):
    B, S, H, D = q.shape
    nc = S // CHUNK
    def bands(t):
        tp = jnp.pad(t, ((0, 0), (BAND, 0), (0, 0), (0, 0))).reshape(B, nc + BAND_CHUNKS, CHUNK, H, D)
        return jnp.concatenate([tp[:, j:j + nc] for j in range(BAND_CHUNKS + 1)], axis=2)
    cidx = jnp.arange(nc)
    qpos = cidx[:, None] * CHUNK + jnp.arange(CHUNK)[None, :]
    kpos = (cidx[:, None] - BAND_CHUNKS) * CHUNK + jnp.arange((BAND_CHUNKS + 1) * CHUNK)[None, :]
    bias, mask = band_bias_mask(tab, qpos, kpos)
    o = band_attend(q.reshape(B, nc, CHUNK, H, D), bands(k), bands(v), bias, mask)
    return o.reshape(B, S, H, D)

def mem_attend(q, mk, mv):
    logits = jnp.einsum('bshd,bnhd->bhsn', q.astype(F32), mk.astype(F32)) * HEAD_DIM ** -0.5
    prob = jax.nn.softmax(logits, axis=-1)
    return jnp.einsum('bhsn,bnhd->bshd', prob, mv.astype(F32)).astype(q.dtype)

def merge(p, o_a, o_b, o_c, o_m, w_o):
    lead = o_a.shape[:2]
    parts = [o.reshape(lead + (-1,)) * jax.nn.silu(p[g])
             for o, g in ((o_a, 'a_g'), (o_b, 'b_g'), (o_c, 'c_g'), (o_m, 'm_g'))]
    return jnp.concatenate(parts, axis=-1) @ w_o

def setup_inputs(seed: int = 0) -> dict:
    key = jax.random.key(seed)
    ks = jax.random.split(key, 24)
    nrm = lambda k, shape, s=1.0: s * jax.random.normal(k, shape, F32)
    c_keep = min(BAND, PAST_LEN)
    return {
        'x_prompt': nrm(ks[0], (BATCH, SEQ, D_MODEL)),
        'x_sample': nrm(ks[1], (DEC_BATCH, DEC_SEQ, D_MODEL)),
        'cache_a_k': nrm(ks[2], (DEPTH, DEC_BATCH, PAST_LEN, HEAD_DIM)),
        'cache_a_v': nrm(ks[3], (DEPTH, DEC_BATCH, PAST_LEN, HEAD_DIM)),
        'cache_a_kidx': nrm(ks[4], (DEPTH, DEC_BATCH, PAST_LEN, D_IDX)),
        'cache_b_k': nrm(ks[5], (DEPTH, DEC_BATCH, PAST_LEN, H_B, HEAD_DIM)),
        'cache_b_v': nrm(ks[6], (DEPTH, DEC_BATCH, PAST_LEN, H_B, HEAD_DIM)),
        'cache_b_logf': jax.nn.log_sigmoid(nrm(ks[7], (DEPTH, DEC_BATCH, PAST_LEN, H_B))),
        'cache_c_k': nrm(ks[8], (DEPTH, DEC_BATCH, c_keep, H_C, HEAD_DIM)),
        'cache_c_v': nrm(ks[9], (DEPTH, DEC_BATCH, c_keep, H_C, HEAD_DIM)),
        'cache_mem_k': nrm(ks[10], (DEPTH, DEC_BATCH, N_MEM, H_M, HEAD_DIM)),
        'cache_mem_v': nrm(ks[11], (DEPTH, DEC_BATCH, N_MEM, H_M, HEAD_DIM)),
        'mem_prompt': nrm(ks[12], (BATCH, N_MEM, D_MODEL)),
        'w_in': nrm(ks[13], (DEPTH, D_MODEL, D_IN), D_MODEL ** -0.5),
        'w_out': nrm(ks[14], (DEPTH, D_MIX, D_MODEL), D_MIX ** -0.5),
        'g_norm': 1.0 + nrm(ks[15], (DEPTH, D_MODEL), 0.01),
        'b_f': nrm(ks[16], (DEPTH, H_B), 0.1),
        'c_bias': nrm(ks[17], (DEPTH, H_C, 2 * REL_CLIP + 1), 0.1),
        'g_mem': 1.0 + nrm(ks[18], (DEPTH, D_MODEL), 0.01),
        'w_mem_kv': nrm(ks[19], (DEPTH, D_MODEL, 2 * W_M), D_MODEL ** -0.5),
        'g_final': 1.0 + nrm(ks[20], (D_MODEL,), 0.01),
    }

def reference(x_prompt, x_sample, cache_a_k, cache_a_v, cache_a_kidx, cache_b_k, cache_b_v, cache_b_logf,
              cache_c_k, cache_c_v, cache_mem_k, cache_mem_v, mem_prompt,
              w_in, w_out, g_norm, b_f, c_bias, g_mem, w_mem_kv, g_final):
    x = x_prompt
    S = x.shape[1]
    pos = jnp.arange(S)
    c_keep_p = min(BAND, S)
    pa_k, pa_v, pa_ki, pb_k, pb_v, pb_lf, pc_k, pc_v, pm_k, pm_v = [], [], [], [], [], [], [], [], [], []
    for l in range(DEPTH):
        p = split_proj(rmsnorm(x, g_norm[l]) @ w_in[l])
        qa, ka, va, qi, ki, wi = a_inputs(p, pos)
        o_a = dsa_prompt(qa, qi, wi, ka, va, ki)
        qb, kb, vb, lf = b_inputs(p, b_f[l])
        o_b = fox_prompt(qb, kb, vb, jnp.cumsum(lf, axis=1))
        qc, kc, vc = c_inputs(p)
        o_c = band_prompt(qc, kc, vc, c_bias[l])
        mk, mv = mem_kv(mem_prompt, g_mem[l], w_mem_kv[l])
        o_m = mem_attend(m_query(p), mk, mv)
        x = x + merge(p, o_a, o_b, o_c, o_m, w_out[l])
        pa_k.append(ka); pa_v.append(va); pa_ki.append(ki)
        pb_k.append(kb); pb_v.append(vb); pb_lf.append(lf)
        pc_k.append(kc[:, S - c_keep_p:]); pc_v.append(vc[:, S - c_keep_p:])
        pm_k.append(mk); pm_v.append(mv)
    y_prompt = rmsnorm(x, g_final)

    x = x_sample
    T = x.shape[1]
    P = cache_a_k.shape[2]
    L = P + T
    qpos = P + jnp.arange(T)
    kpos_all = jnp.arange(L)
    c_keep = cache_c_k.shape[2]
    kpos_c = jnp.concatenate([P - c_keep + jnp.arange(c_keep), qpos])
    lim = jnp.minimum((qpos // CHUNK + 1) * CHUNK, L)
    topk = min(TOPK_MAX, L // 4)
    cat = lambda a, b: jnp.concatenate([a, b.astype(a.dtype)], axis=1)
    sa_k, sa_v, sa_ki, sb_k, sb_v, sb_lf, sc_k, sc_v = [], [], [], [], [], [], [], []
    for l in range(DEPTH):
        p = split_proj(rmsnorm(x, g_norm[l]) @ w_in[l])
        qa, ka, va, qi, ki, wi = a_inputs(p, qpos)
        o_a = dsa_attend(qa, qi, wi, lim, cat(cache_a_k[l], ka), cat(cache_a_v[l], va),
                         cat(cache_a_kidx[l], ki), topk)
        qb, kb, vb, lf = b_inputs(p, b_f[l])
        F = jnp.cumsum(jnp.concatenate([cache_b_logf[l].astype(F32), lf], axis=1), axis=1)
        o_b = fox_attend(qb, cat(cache_b_k[l], kb), cat(cache_b_v[l], vb), F[:, P:], F, qpos, kpos_all)
        qc, kc, vc = c_inputs(p)
        bias, mask = band_bias_mask(c_bias[l], qpos, kpos_c)
        o_c = band_attend(qc, cat(cache_c_k[l], kc), cat(cache_c_v[l], vc), bias, mask)
        o_m = mem_attend(m_query(p), cache_mem_k[l], cache_mem_v[l])
        x = x + merge(p, o_a, o_b, o_c, o_m, w_out[l])
        sa_k.append(ka); sa_v.append(va); sa_ki.append(ki)
        sb_k.append(kb); sb_v.append(vb); sb_lf.append(lf)
        sc_k.append(kc); sc_v.append(vc)
    y_sample = rmsnorm(x, g_final)

    return (y_prompt, y_sample,
            jnp.stack(pa_k), jnp.stack(pa_v), jnp.stack(pa_ki),
            jnp.stack(pb_k), jnp.stack(pb_v), jnp.stack(pb_lf),
            jnp.stack(pc_k), jnp.stack(pc_v), jnp.stack(pm_k), jnp.stack(pm_v),
            jnp.stack(sa_k), jnp.stack(sa_v), jnp.stack(sa_ki),
            jnp.stack(sb_k), jnp.stack(sb_v), jnp.stack(sb_lf),
            jnp.stack(sc_k), jnp.stack(sc_v))


_drawn_inputs = setup_inputs


def setup_inputs(seed=0):
    import zlib

    import numpy as np

    out = dict(_drawn_inputs(seed))
    spreads = {}
    factors = {'cache_b_logf': 3.803, 'g_norm': 5.109, 'c_bias': 8.0, 'g_mem': 5.677, 'g_final': 5.894}
    for name, (base, spread) in spreads.items():
        noise = np.random.default_rng([zlib.crc32(name.encode()), seed]).standard_normal(out[name].shape)
        drawn = base * np.exp(spread * noise) if base else spread * noise
        out[name] = __import__('jax').numpy.asarray(drawn.astype(out[name].dtype))
    for name, factor in factors.items():
        out[name] = (out[name] * factor).astype(out[name].dtype)
    return out
```

```python
from contextlib import ExitStack

import numpy as np

import concourse.bass as bass
from concourse import mybir

F32 = mybir.dt.float32
ALU = mybir.AluOpType
ACT = mybir.ActivationFunctionType

P = 128
D = 1024
KT = D // P
SEQ = 1024
NT = SEQ // P
ST_ = NT
TILES = list(range(NT + 1))
TOK = SEQ + P
DEPTH = 2
R, STEPS = 8, 16
PAIRS = R // 2
PAST = 512
H, HD = 4, 64
W = H * HD
MEM = 256
TOPK_P = min(256, SEQ // 4)
TOPK_S = min(256, (PAST + STEPS) // 4)
ROT = 8
EPS = 1e-6
NEG = -1.0e30
TAKEN = -3.0e38
SKEYS = PAST + P
CHUNKS = ["A1", "mm", "B1", "B2", "C1", "C2", "M1", "A2", "O0", "O1"]
BRANCHES = "BCMA"
GCOL = {"A": 0, "B": W, "C": 2 * W, "M": 3 * W}
XL = 767

C_ID, C_TRI, C_CM, C_FULL, C_CAUS, C_SELT, C_SEL, C_PM, C_HM, C_ROPE = np.cumsum(
    [0, 128, 128, 256, 224, 224, 128, 32, 4, 4]).tolist()
NCONST = C_ROPE + 9 * 16

SEL_TILES = [t for t in range(NT) if (t + 1) * P > TOPK_P]
SC_OFF, _n = {}, 0
for _t in SEL_TILES:
    SC_OFF[_t] = _n
    _n += (_t + 1) * P
SC_OFF[ST_] = _n
FILL = -TOPK_S % 8
SC_W = _n + SKEYS + FILL


def chunk_tiles(c):
    return [0, 1] if c == "mm" else TILES


def key_tiles(br, t):
    return {"A": range(t + 1), "B": range(t + 1), "C": range(max(0, t - 4), t + 1), "M": range(2)}[br]


def attention_items():
    return [(br, h, t) for br in BRANCHES for h in range(H) for t in list(range(NT)) + [f"s{h}"]]


def is_sample(item):
    return isinstance(item[2], str)


def blocks(item):
    if is_sample(item):
        return 2 if item[0] == "M" else 5
    return len(key_tiles(item[0], item[2]))


def topk_rounds():
    out = []
    for t in [ST_] + SEL_TILES:
        n = (TOPK_S + FILL if t == ST_ else TOPK_P) // 8
        out += [(t, i, i == n - 1) for i in range(n)]
    return out


def layer_order():
    o = []
    rounds = topk_rounds()
    cost = lambda t: 2 * ((SKEYS + FILL if t == ST_ else (t + 1) * P) + 70) / 960

    def project(c, fill=0.0):
        prev = None
        for t in chunk_tiles(c):
            o.append(("P", c, t))
            if prev is not None:
                o.append(("TR", c, prev))
            prev = t
            spent = 0.0
            while rounds and fill and spent < fill:
                o.append(("K",) + rounds[0])
                spent += cost(rounds[0][0])
                rounds.pop(0)
        o.append(("TR", c, prev))

    def attend(items):
        n = len(items)
        for i in range(-2, n + 2):
            if 0 <= i < n:
                o.append(("T", items[i]))
            if i + 2 < n:
                o.append(("S", items[i + 2]))
            if 0 <= i - 1 < n:
                o.append(("V", items[i - 1]))
            if 0 <= i - 2 < n and is_sample(items[i - 2]):
                o.append(("R", items[i - 2]))

    all_items = attention_items()
    o.append(("norm", 0))
    for n in range(12):
        if n < 10:
            o.append(("norm", n + 1))
        if n < 11:
            o.append(("turn", n))
        if n < 9:
            o.append(("P", "A1", n))
        if 1 <= n < 10:
            o.append(("TR", "A1", n - 1))
    project("mm")
    o.append(("F",))
    index = [("ip", t, h) for t in SEL_TILES for h in range(H)]
    for n, x in enumerate(index):
        o.append(x)
    o.append(("wrow",))
    for j in range(PAIRS):
        o.append(("is", j))
        if j:
            o.append(("iw", j - 1))
    o.append(("iw", PAIRS - 1))
    for c in ("B1", "B2"):
        project(c, 6.0)
    attend([x for x in all_items if x[0] == "B"])
    for c in ("C1", "C2"):
        project(c, 6.0)
    attend([x for x in all_items if x[0] == "C"])
    project("M1", 6.0)
    attend([x for x in all_items if x[0] == "M"])
    project("A2", 6.0)
    o += [("K",) + x for x in rounds]
    o += [("OT", t) for t in TILES]
    attend([x for x in all_items if x[0] == "A"])
    o += [("OA", t) for t in TILES]
    for c in ("O0", "O1"):
        for t in TILES:
            o.append(("P", c, t))
    return o


class Signal:

    def __init__(self, sem, events, worth=lambda e: 1, credit=0):
        self.sem, self.credit, self.upto = sem, credit, {}
        n = 0
        for e in events:
            assert e not in self.upto, e
            n += worth(e)
            self.upto[e] = n
        self.layer = n
        self.list = list(events)

    def at(self, event):
        return self.credit + self.upto[event]

    def before(self, n):
        return self.credit + (self.upto[self.list[n - 1]] if n else 0)


class Units:

    def __init__(self, sem, name, aps, uses):
        n = len(aps)
        self.aps, self.slot = aps, {u: i % n for i, u in enumerate(uses)}
        self.filled = [Signal(sem(f"{name}{k}_filled"), uses[k::n]) for k in range(n)]
        self.emptied = [Signal(sem(f"{name}{k}_emptied"), uses[k::n], credit=1) for k in range(n)]
        self.index = {u: i // n for i, u in enumerate(uses)}

    def ap(self, use):
        return self.aps[self.slot[use]]

    def fill(self, use):
        return self.filled[self.slot[use]]

    def empty(self, use):
        return self.emptied[self.slot[use]]

    def free(self, use):
        return self.empty(use).before(self.index[use])


def encoder(nc, d):
    order = layer_order()
    items = attention_items()
    with ExitStack() as ctx:
        def sb(name, *shape):
            return ctx.enter_context(nc.sbuf_tensor(name, [P] + list(shape), F32))

        def sem(name):
            return ctx.enter_context(nc.semaphore(name))

        hT = sb("hT", KT, TOK)
        wring = sb("wring", 2, KT * 512)
        qT = sb("qT", H, TOK)
        kA = sb("kA", 2, TOK)
        kT = sb("kT", 2, TOK)
        vA = sb("vA", 9, HD)
        vX = sb("vX", 9, W)
        gate = sb("gate", 9, W)
        bias = sb("bias", 2, 1024)
        sc = sb("sc", SC_W)
        work = sb("work", 4, 1024)
        stage = sb("stage", 2, 512)
        cache = sb("cache", 3, 2048)
        mK = sb("mK", 2, MEM)
        mV = sb("mV", 2, W)
        con = sb("con", NCONST + 1)
        qs = sb("qs", 2, P)
        qsA = sb("qsA", P)
        selj = sb("selj", P)
        wsel = selj[:, :].rearrange("p (j q) -> p j q", j=PAIRS)
        wi = sb("wi", 9, H)
        lf = sb("lf", 3, 9 * H)
        rstd = sb("rstd", 3, 11)
        stat = sb("stat", 4, 4)
        top8 = sb("top8", 8)
        wmask = sb("wmask", 16)
        wrow = sb("wrow", 8)
        rtmp = sb("rtmp", 2, 6 * ROT)
        bfb = sb("bfb", H)
        credit = sb("credit", 1)

        psS = ctx.enter_context(nc.psum_tensor("psS", [P, 2, 1024], F32))
        psT = ctx.enter_context(nc.psum_tensor("psT", [P, 2, 512], F32))
        psX = ctx.enter_context(nc.psum_tensor("psX", [P, 2, 512], F32))

        ident = con[:, C_ID:C_ID + P]

        s_const = sem("const_loaded")
        s_zero = sem("zeros_set")
        s_x0 = sem("x_copied")
        layer_first = s_x0.num + 1

        s_uses, t_uses, x_uses = [], [], []
        for s in order:
            k = s[0]
            if k == "turn" or k == "OT":
                t_uses += [(s, 0), (s, 1)]
            elif k == "P":
                x_uses.append(s)
            elif k == "TR" and s[1] in ("mm", "A1", "B1", "C1", "M1", "A2"):
                t_uses.append(s)
            elif k in ("ip", "is", "iw", "S"):
                s_uses.append(s)
            elif k == "wrow":
                x_uses.append(s)
            elif k == "T":
                t_uses += [(s, g) for g in range((blocks(s[1]) + 3) // 4)]
            elif k in ("V", "R"):
                x_uses.append(s)
            elif k == "OA":
                t_uses.append(s)
        S = Units(sem, "scores", [psS[:, k, :] for k in range(2)], s_uses)
        T = Units(sem, "turned", [psT[:, k, :] for k in range(2)], t_uses)
        X = Units(sem, "acc", [psX[:, k, :] for k in range(2)], x_uses)

        units = [(c, t) for c in CHUNKS if c[0] != "O" for t in chunk_tiles(c)]
        slot_of = {u: n % 2 for n, u in enumerate(units)}
        stored_dmas = lambda u: {"mm": 1, "A1": 3, "B1": 1}.get(u[0], int(u[0] == "C1" and u[1] >= 4))
        norms = list(range(11))
        x_loaded = [Signal(sem(f"x_loaded{k}"), [n for n in norms if n % 4 == k], lambda e: 16) for k in range(4)]
        gains_loaded = Signal(sem("gains_loaded"), ["g"], lambda e: 48)
        squares = Signal(sem("squares_summed"), norms)
        rooted = Signal(sem("root_taken"), norms)
        normed = Signal(sem("tile_normed"), norms)
        w_loaded = [Signal(sem(f"w_loaded{k}"), CHUNKS[k::2], lambda e: 16) for k in range(2)]
        h_act = Signal(sem("hT_by_act"), norms)
        h_dve = Signal(sem("hT_by_dve"), norms)
        staged = Signal(sem("unit_staged"), units)
        worked = Signal(sem("unit_worked"), [u for u in units if u[0] in ("A1", "A2", "B2", "C2", "M1")])
        stored = [Signal(sem(f"stage{k}_stored"), [u for u in units if slot_of[u] == k and stored_dmas(u)],
                         lambda u: 16 * stored_dmas(u)) for k in range(2)]
        v_units = [(c, t) for c in ("B2", "C2") for t in TILES if c == "B2" or t >= 4]
        v_stored = Signal(sem("v_stored"), [u for u in [("mm", 0), ("mm", 1)] + v_units], lambda e: 16)
        turned = Signal(sem("operand_turned"), [s[1:] for s in t_uses if s[0] == "TR"])
        f_ready = Signal(sem("f_stage"), ["exp", "ln"])
        f_dve = Signal(sem("f_vector"), ["z", "lf", "scan", "spread"])
        f_dma = Signal(sem("f_moved"), ["nat", "rows", "out"],
                       lambda e: {"nat": 48, "rows": 16 * 9, "out": 32}[e])
        wmask_ready = Signal(sem("wmask_ready"), ["w"])
        lines_sem = sem("bias_lines_written")
        index_items = [s for s in order if s[0] in ("ip", "is")]
        relued = Signal(sem("index_relued"), index_items)
        scored = Signal(sem("index_scored"), [s for s in order if s[0] in ("ip", "iw", "wrow")])
        n_work = {}
        for s in order:
            if s[0] in ("ip", "is"):
                n_work[s] = len(n_work)
        qs_uses = [s for s in order if s[0] == "is"] + [("S", x) for x in items if is_sample(x)]
        qs_ready = Signal(sem("qs_ready"), qs_uses)
        cache_loads = [(s, "k") for s in index_items if s[0] == "is"]
        for x in items:
            if is_sample(x):
                cache_loads += [(("S", x), "k"), (("S", x), "v")]
        cslot = {u: n % 3 for n, u in enumerate(cache_loads)}
        cdmas = lambda u: 2 if u[1] == "k" and (u[0][0] == "is" or u[0][1][0] == "A") else 1
        cache_loaded = [Signal(sem(f"cache{k}_loaded"), [u for u in cache_loads if cslot[u] == k],
                               lambda u: 16 * cdmas(u)) for k in range(3)]
        pbias_loads = [(b, h) for b in "BC" for h in range(H)]
        pbias = Signal(sem("prompt_bias_loaded"), pbias_loads, lambda e: 16)
        sbias_loads = [("B", j) for j in range(PAIRS)] + [("C", 0)]
        sbias = Signal(sem("sample_bias_loaded"), sbias_loads, lambda e: 16 * 8)
        strip = Signal(sem("strip_masked"), [("C", h) for h in range(H)])
        sspread = Signal(sem("sample_strip_spread"), [("C", 0)])
        tmask = Signal(sem("token_mask_loaded"), ["m"], lambda e: 16)
        logits = Signal(sem("logits_ready"), items)
        maxes = Signal(sem("max_ready"), items)
        probs = Signal(sem("probs_ready"), items)
        pt_act = Signal(sem("probs_turned_act"), items)
        pt_dve = Signal(sem("probs_turned_dve"), [x for x in items if blocks(x) > 4])
        rsum = Signal(sem("row_sum_inverted"), items)
        om_ready = Signal(sem("own_heads_kept"), [x for x in items if is_sample(x)])
        selj_ready = Signal(sem("selj_ready"), [x for x in items if is_sample(x) and x[0] == "A"])
        gated = Signal(sem("branch_gated"), [s[1] for s in order if s[0] == "R" or (s[0] == "V" and not is_sample(s[1]))])
        selected = Signal(sem("selected"), [ST_] + SEL_TILES)
        o_stored = Signal(sem("branch_stored"), list("BCM"), lambda e: 16)
        o_loaded = [Signal(sem(f"branch_loaded{k}"), [t for t in TILES if t % 4 == k], lambda e: 16) for k in range(4)]
        merged = Signal(sem("merged_turned"), [s for s in order if s[0] in ("OT", "OA")])
        outs = [(c, t) for c in ("O0", "O1") for t in TILES]
        res_loaded = [Signal(sem(f"residual_loaded{k}"), outs[k::2], lambda e: 16) for k in range(2)]
        res_added = Signal(sem("residual_added"), outs)
        res_stored = [Signal(sem(f"residual_stored{k}"), outs[k::2], lambda e: 16) for k in range(2)]
        layer_over = sem("layer_over")
        layer_sems = range(layer_first, layer_over.num + 1)
        go = {n: sem(f"next_layer_{n}") for n in ("sync", "tensor", "scalar", "vector")}
        fin_gain = sem("fin_gain_loaded")
        fin_loaded = [sem(f"fin_loaded{k}") for k in range(4)]
        fin_sq, fin_root, fin_done = sem("fin_squares"), sem("fin_root"), sem("fin_normed")
        fin_stored = [sem(f"y{k}_stored") for k in range(4)]

        last_of = {br: [x for x in items if x[0] == br][-1] for br in BRANCHES}
        before_of = {"B": None, "C": "B", "M": "C", "A": "M"}

        def wait(eng, signal, event):
            eng.wait_ge(signal.sem, signal.at(event))

        def rows(ap, l, per_layer, first, n):
            return ap[bass.ds(l * per_layer + first, n), :]

        def buf(n):
            return work[:, n % 2, :]

        def turned_buf(n):
            return work[:, 2 + n % 2, :]

        n_item = {x: n for n, x in enumerate(items)}

        def next_layer(eng, name):
            eng.drain().then_inc(layer_over, 1)
            eng.wait_ge(go[name], 1)
            eng.sem_clear(go[name])

        block = ctx.enter_context(nc.Block())

        @block.sync
        def _(sp):
            sp.dma_start(con[:, :], d["const"]).then_inc(s_const, 16)
            sp.dma_start(d["xres"], d["x"]).then_inc(s_x0, 16)
            sp.wait_ge(s_x0, 16)

            def load_chunk(l, c):
                n = CHUNKS.index(c)
                if n >= 2:
                    last = ("P", CHUNKS[n - 2], chunk_tiles(CHUNKS[n - 2])[-1])
                    wait(sp, X.fill(last), last)
                sp.dma_start(wring[:, n % 2, :], rows(d["w"], l, len(CHUNKS) * P, n * P, P)
                             ).then_inc(w_loaded[n % 2].sem, 16)

            cache_state = [0]

            def load_cache(l, u):
                n = cache_state[0]
                assert cache_loads[n] == u
                cache_state[0] += 1
                if n >= 3:
                    s, kind = cache_loads[n - 3]
                    use = s if kind == "k" else ("V", s[1])
                    units_ = S if kind == "k" else X
                    wait(sp, units_.fill(use), use)
                s, kind = u
                done = cache_loaded[cslot[u]].sem
                dst = cache[:, cslot[u], :]
                j = s[1] if s[0] == "is" else int(s[1][2][1:])
                br = "I" if s[0] == "is" else s[1][0]
                src = rows(d[kind + br], l, PAIRS * (64 if br in "AI" and kind == "k" else P),
                           j * (64 if br in "AI" and kind == "k" else P), 64 if br in "AI" and kind == "k" else P)
                w = src.shape[1]
                if br in "AI" and kind == "k":
                    sp.dma_start(dst[0:64, 0:w], src).then_inc(done, 16)
                    sp.dma_start(dst[64:128, 0:w], src).then_inc(done, 16)
                else:
                    sp.dma_start(dst[:, 0:w], src).then_inc(done, 16)

            with sp.Fori(0, DEPTH) as l:
                cache_state[0] = 0
                sp.dma_start(bias[:, 0, :], rows(d["gain"], l, 2, 0, 1).to_broadcast([P, D])).then_inc(gains_loaded.sem, 16)
                sp.dma_start(bias[:, 1, :], rows(d["gain"], l, 2, 1, 1).to_broadcast([P, D])).then_inc(gains_loaded.sem, 16)
                sp.dma_start(bfb[:, :], rows(d["bf"], l, 1, 0, 1).to_broadcast([P, H])).then_inc(gains_loaded.sem, 16)
                for n in norms:
                    if n == 1:
                        load_chunk(l, "A1")
                    if n == 4:
                        load_chunk(l, "mm")
                    if n >= 4:
                        wait(sp, T.fill((("turn", n - 4), 1)), (("turn", n - 4), 1))
                    src = d["xres"][n * P:(n + 1) * P, :] if n < 9 else d["mem"][(n - 9) * P:(n - 8) * P, :]
                    sp.dma_start(work[:, n % 4, :], src).then_inc(x_loaded[n % 4].sem, 16)
                wait(sp, squares, 10)
                sp.dma_start(sc[:, SC_OFF[ST_] + PAST:SC_OFF[ST_] + SKEYS], d["tmask"]).then_inc(tmask.sem, 16)
                nxt = [0]

                def cache_upto(l, n):
                    while nxt[0] < n:
                        load_cache(l, cache_loads[nxt[0]])
                        nxt[0] += 1

                cache_upto(l, 3)
                load_chunk(l, "B1")
                cache_upto(l, 4)
                load_chunk(l, "B2")
                for br in BRANCHES:
                    base = 4 + 8 * BRANCHES.index(br)
                    cache_upto(l, base + 3)
                    nexts = {"B": ["C1", "C2"], "C": ["M1", "A2"], "M": [], "A": ["O1"]}[br]
                    if br == "B":
                        load_chunk(l, "C1")
                        load_chunk(l, "C2")
                    if br == "C":
                        load_chunk(l, "M1")
                        load_chunk(l, "A2")
                    if br == "A":
                        load_chunk(l, "O0")
                        load_chunk(l, "O1")
                        wait(sp, o_stored, "M")
                        for t in TILES:
                            if t >= 4:
                                wait(sp, T.fill((("OT", t - 4), 1)), (("OT", t - 4), 1))
                            elif t == 0:
                                last = last_of["M"]
                                wait(sp, X.fill(("V", last)), ("V", last))
                                wait(sp, gated, last)
                            sp.dma_start(work[:, t % 4, 0:3 * W], d["oscr"][t * P:(t + 1) * P, :]
                                         ).then_inc(o_loaded[t % 4].sem, 16)
                    cache_upto(l, base + 8)
                for n, (c, t) in enumerate(outs):
                    if n == 0:
                        wait(sp, gated, last_of["A"])
                        wait(sp, X.fill(("V", last_of["A"])), ("V", last_of["A"]))
                    if n >= 2:
                        wait(sp, res_added, outs[n - 2])
                    h = 512 * int(c[1])
                    sp.dma_start(work[:, n % 2, 0:512], d["xres"][t * P:(t + 1) * P, h:h + 512]
                                 ).then_inc(res_loaded[n % 2].sem, 16)
                next_layer(sp, "sync")
            sp.dma_start(bias[:, 0, :], d["gain"][2 * DEPTH:2 * DEPTH + 1, :].to_broadcast([P, D])).then_inc(fin_gain, 16)
            for t in TILES:
                if t >= 4:
                    sp.wait_ge(fin_stored[t % 4], 16 * (t // 4))
                sp.dma_start(work[:, t % 4, :], d["xres"][t * P:(t + 1) * P, :]).then_inc(fin_loaded[t % 4], 16)

        @block.tensor
        def _(pe):
            pe.wait_ge(s_const, 16)
            pe.wait_ge(s_zero, 1)

            def turn(out, src):
                return pe.transpose(out, src, ident)

            with pe.Fori(0, DEPTH) as l:
                for s in order:
                    k = s[0]
                    if k == "turn":
                        n = s[1]
                        wait(pe, normed, n)
                        for g in range(2):
                            u = (s, g)
                            pe.wait_ge(T.empty(u).sem, T.free(u))
                            for b in range(4):
                                kt = 4 * g + b
                                mm = turn(T.ap(u)[:, b * P:(b + 1) * P], work[:, n % 4, kt * P:(kt + 1) * P])
                            mm.then_inc(T.fill(u).sem, 1)
                    elif k == "P":
                        c, t = s[1:]
                        n = CHUNKS.index(c)
                        if t == 0:
                            wait(pe, w_loaded[n % 2], c)
                        if c in ("A1", "mm"):
                            wait(pe, h_act, t + (9 if c == "mm" else 0))
                            wait(pe, h_dve, t + (9 if c == "mm" else 0))
                        if c[0] == "O":
                            if t == 0 and c == "O0":
                                wait(pe, merged, ("OA", 8))
                        pe.wait_ge(X.empty(s).sem, X.free(s))
                        w = 456 if c == "A1" else 512
                        wv = wring[:, n % 2, :].rearrange("p (k c) -> p k c", k=KT)
                        for kt in range(KT):
                            if c == "mm":
                                lhs = gate[:, :, :].rearrange("p a b -> p (a b)")[:, kt * MEM + t * P:kt * MEM + (t + 1) * P]
                            else:
                                lhs = hT[:, kt, t * P:(t + 1) * P]
                            mm = pe.matmul(X.ap(s)[:, 0:w], lhs, wv[:, kt, 0:w], start=(kt == 0), stop=(kt == KT - 1))
                        mm.then_inc(X.fill(s).sem, 1)
                    elif k == "TR" and s in T.slot:
                        c, t = s[1:]
                        wait(pe, worked if c in ("A1", "A2", "M1") else staged, (c, t))
                        pe.wait_ge(T.empty(s).sem, T.free(s))
                        src = stage[:, slot_of[(c, t)], :]
                        nb = {"A1": 3, "B1": 4, "C1": 4}.get(c, 2)
                        for b in range(nb):
                            mm = turn(T.ap(s)[:, b * P:(b + 1) * P], src[:, b * P:(b + 1) * P])
                        mm.then_inc(T.fill(s).sem, 1)
                    elif k == "ip":
                        _, t, h = s
                        wait(pe, turned, ("A1", 8))
                        pe.wait_ge(S.empty(s).sem, S.free(s))
                        L = (t + 1) * P
                        for c0 in range(0, L, 512):
                            mm = pe.matmul(S.ap(s)[:, c0:min(L, c0 + 512)], qT[:, h, t * P:(t + 1) * P],
                                           kA[:, 0, c0:min(L, c0 + 512)], start=True, stop=True)
                        mm.then_inc(S.fill(s).sem, 1)
                    elif k == "wrow":
                        wait(pe, scored, order[order.index(s) - 1])
                        wait(pe, wmask_ready, "w")
                        pe.wait_ge(X.empty(s).sem, X.free(s))
                        pe.matmul(X.ap(s)[:, 0:16], con[:, C_SELT:C_SELT + P], wmask[:, :], start=True, stop=True
                                  ).then_inc(X.fill(s).sem, 1)
                    elif k == "is":
                        j = s[1]
                        wait(pe, qs_ready, s)
                        wait(pe, cache_loaded[cslot[(s, "k")]], (s, "k"))
                        pe.wait_ge(S.empty(s).sem, S.free(s))
                        kc = cache[:, cslot[(s, "k")], :]
                        for r in range(2):
                            pe.matmul(S.ap(s)[64 * r:64 * r + 64, 0:PAST], qsA[:, 64 * r:64 * r + 64],
                                      kc[:, r * PAST:(r + 1) * PAST], start=True, stop=True)
                        pe.matmul(S.ap(s)[:, PAST:SKEYS], qsA[:, :], kA[:, 0, SEQ:TOK], start=True, stop=True
                                  ).then_inc(S.fill(s).sem, 1)
                    elif k == "iw":
                        j = s[1]
                        wait(pe, relued, ("is", j))
                        wait(pe, scored, ("wrow",))
                        pe.wait_ge(S.empty(s).sem, S.free(s))
                        r = buf(n_work[("is", j)])
                        o = S.ap(s)[32 * j:32 * j + 32, :]
                        pe.matmul(o[:, 0:PAST], wsel[:, j, :], r[:, 0:PAST], start=True, stop=True)
                        pe.matmul(o[:, PAST:SKEYS], wsel[:, j, :], r[:, PAST:SKEYS], start=True, stop=True
                                  ).then_inc(S.fill(s).sem, 1)
                    elif k == "S":
                        br, h, t = s[1]
                        o = S.ap(s)
                        if s[1] == [x for x in items if x[0] == br][0]:
                            wait(pe, turned, ({"A": "A2", "M": "M1"}.get(br, br + "1"), 8))
                        pe.wait_ge(S.empty(s).sem, S.free(s))
                        if is_sample(s[1]):
                            wait(pe, qs_ready, s)
                            wait(pe, cache_loaded[cslot[(s, "k")]], (s, "k"))
                            kc = cache[:, cslot[(s, "k")], :]
                            j = int(t[1:])
                            n = MEM if br == "M" else PAST
                            if br == "A":
                                for r in range(2):
                                    mm = pe.matmul(o[64 * r:64 * r + 64, 0:n], qsA[:, 64 * r:64 * r + 64],
                                                   kc[:, r * n:(r + 1) * n], start=True, stop=False)
                                wait(pe, selj_ready, s[1])
                                sm = sc[:, SC_OFF[ST_]:SC_OFF[ST_] + SKEYS]
                                wait(pe, selected, ST_)
                                pe.matmul(o[:, 0:n], selj[:, :], sm[:, 0:n], start=False, stop=True)
                                pe.matmul(o[:, n:SKEYS], qsA[:, :], kA[:, 1, SEQ:TOK], start=True, stop=False)
                                mm = pe.matmul(o[:, n:SKEYS], selj[:, :], sm[:, n:SKEYS], start=False, stop=True)
                            else:
                                for g in range(2):
                                    for r in range(2):
                                        mm = pe.matmul(o[64 * r:64 * r + 64, 0:n], qs[:, g, 64 * r:64 * r + 64],
                                                       kc[:, (r * 2 + g) * n:(r * 2 + g + 1) * n], start=(g == 0),
                                                       stop=(g == 1))
                                if br != "M":
                                    for g in range(2):
                                        pe.matmul(o[:, n:SKEYS], qs[:, g, :], kT[:, g, SEQ:TOK], start=(g == 0), stop=False)
                                    base = C_CAUS if br == "B" else C_FULL
                                    mm = pe.matmul(o[:, n:SKEYS], ident, con[:, base + 96 - 32 * j:base + 96 - 32 * j + P],
                                                   start=False, stop=True)
                            mm.then_inc(S.fill(s).sem, 1)
                        else:
                            kb = key_tiles(br, t)
                            keys = {"A": kA[:, 1, :], "B": kT[:, h // 2, :], "C": kT[:, h // 2, :], "M": mK[:, h // 2, :]}[br]
                            k0, L = kb[0] * P, len(kb) * P
            
                            q = qT[:, h, t * P:(t + 1) * P]
                            plain = L - P if br == "B" else L
                            for c0 in range(0, plain, 512):
                                c1 = min(plain, c0 + 512)
                                mm = pe.matmul(o[:, c0:c1], q, keys[:, k0 + c0:k0 + c1], start=True, stop=True)
                            if br == "B":
                                pe.matmul(o[:, plain:L], q, keys[:, k0 + plain:k0 + L], start=True, stop=False)
                                mm = pe.matmul(o[:, plain:L], ident, con[:, C_TRI:C_TRI + P], start=False, stop=True)
                            mm.then_inc(S.fill(s).sem, 1)
                    elif k == "T":
                        wait(pe, probs, s[1])
                        p = buf(n_item[s[1]])
                        nb = blocks(s[1])
                        for g in range((nb + 3) // 4):
                            u = (s, g)
                            pe.wait_ge(T.empty(u).sem, T.free(u))
                            for b in range(4 * g, min(nb, 4 * g + 4)):
                                mm = turn(T.ap(u)[:, (b - 4 * g) * P:(b - 4 * g + 1) * P], p[:, b * P:(b + 1) * P])
                            mm.then_inc(T.fill(u).sem, 1)
                    elif k == "V":
                        br, h, t = s[1]
                        nb = blocks(s[1])
                        pT = turned_buf(n_item[s[1]])
                        wait(pe, pt_act, s[1])
                        if nb > 4:
                            wait(pe, pt_dve, s[1])
                        pe.wait_ge(X.empty(s).sem, X.free(s))
                        if s[1] == [x for x in items if x[0] == br][0] and br != "M":
                            c = {"B": "B2", "C": "C2", "A": "A1"}[br]
                            wait(pe, worked, (c, 8))
                        o = X.ap(s)
                        if is_sample(s[1]):
                            cu = (("S", s[1]), "v")
                            wait(pe, cache_loaded[cslot[cu]], cu)
                            w = HD if br == "A" else W
                            nk = 2 if br == "M" else 4
                            vc = cache[:, cslot[cu], :]
                            for b in range(nb):
                                for r in range(2):
                                    if b < nk:
                                        v = vc[:, (r * nk + b) * w:(r * nk + b + 1) * w]
                                    else:
                                        v = (vA if br == "A" else vX)[:, ST_, :]
                                    mm = pe.matmul(o[64 * r:64 * r + 64, 0:w], pT[:, b * P + 64 * r:b * P + 64 * r + 64], v,
                                                   start=(b == 0), stop=(b == nb - 1))
                        else:
                            kb = key_tiles(br, t)
                            for b, kt in enumerate(kb):
                                v = {"A": lambda: vA[:, kt, :], "M": lambda: mV[:, kt, h * HD:(h + 1) * HD]}.get(
                                    br, lambda: vX[:, kt, h * HD:(h + 1) * HD])()
                                mm = pe.matmul(o[:, 0:HD], pT[:, b * P:(b + 1) * P], v, start=(b == 0), stop=(b == nb - 1))
                        mm.then_inc(X.fill(s).sem, 1)
                    elif k == "R":
                        j = int(s[1][2][1:])
                        wait(pe, om_ready, s[1])
                        pe.wait_ge(X.empty(s).sem, X.free(s))
                        pe.matmul(X.ap(s)[32 * j:32 * j + 32, 0:W], con[:, C_SEL:C_SEL + 32],
                                  turned_buf(n_item[s[1]])[:, 0:W], start=True, stop=True).then_inc(X.fill(s).sem, 1)
                    elif k == "OT":
                        t = s[1]
                        wait(pe, o_loaded[t % 4], t)
                        for g in range(2):
                            u = (s, g)
                            pe.wait_ge(T.empty(u).sem, T.free(u))
                            for b in range(3):
                                mm = turn(T.ap(u)[:, b * P:(b + 1) * P], work[:, t % 4, (3 * g + b) * P:(3 * g + b + 1) * P])
                            mm.then_inc(T.fill(u).sem, 1)
                    elif k == "OA":
                        t = s[1]
                        if t == 0:
                            wait(pe, gated, last_of["A"])
                        pe.wait_ge(T.empty(s).sem, T.free(s))
                        for b in range(2):
                            mm = turn(T.ap(s)[:, b * P:(b + 1) * P], gate[:, t, b * P:(b + 1) * P])
                        mm.then_inc(T.fill(s).sem, 1)

                next_layer(pe, "tensor")

        @block.scalar
        def _(act):
            act.wait_ge(s_zero, 1)
            act.wait_ge(s_const, 16)
            with act.Fori(0, DEPTH) as l:
                for s in order:
                    k = s[0]
                    if k == "norm":
                        n = s[1]
                        wait(act, x_loaded[n % 4], n)
                        nc.scalar.activation(sc[:, 0:D], work[:, n % 4, :], ACT.Square, accum_out=rstd[:, 0, n:n + 1]
                                             ).then_inc(squares.sem, 1)
                        act.wait_ge(squares.sem, squares.at(n))
                        nc.scalar.activation(rstd[:, 1, n:n + 1], rstd[:, 0, n:n + 1], ACT.Sqrt,
                                             scale=1.0 / D, bias=con[:, NCONST:NCONST + 1]).then_inc(rooted.sem, 1)
                    elif k == "turn":
                        n = s[1]
                        u = (s, 0)
                        wait(act, T.fill(u), u)
                        src = T.ap(u)[:, :].rearrange("p (b c) -> p b c", b=4)
                        if n < 9:
                            dst = hT[:, 0:4, n * P:(n + 1) * P]
                        else:
                            dst = gate[:, :, :].rearrange("p a b -> p (a b)")[:, 0:4 * MEM].rearrange(
                                "p (k c) -> p k c", k=4)[:, :, (n - 9) * P:(n - 8) * P]
                        nc.scalar.copy(dst, src).then_inc(T.empty(u).sem, 1)
                        act.drain().then_inc(h_act.sem, 1)
                    elif k == "P" and s[1][0] != "O":
                        c, t = s[1:]
                        n = units.index((c, t))
                        sl = slot_of[(c, t)]
                        sg = stage[:, sl, :]
                        if n >= 2:
                            pu = units[n - 2]
                            if ("TR",) + pu in T.slot:
                                wait(act, T.fill(("TR",) + pu), ("TR",) + pu)
                            if pu in worked.upto:
                                wait(act, worked, pu)
                        st = stored[sl]
                        prior = [u for u in units[:n] if slot_of[u] == sl and u in st.upto]
                        if prior:
                            wait(act, st, prior[-1])
                        wait(act, X.fill(s), s)
                        x = X.ap(s)
                        if c == "mm":
                            nc.scalar.copy(mV[:, t, :], x[:, W:2 * W])
                            nc.scalar.copy(sg[:, 0:W], x[:, 0:W]).then_inc(X.empty(s).sem, 1)
                        elif c == "A1":
                            nc.scalar.copy(sg[:, 0:456], x[:, 0:456]).then_inc(X.empty(s).sem, 1)
                        elif c in ("B1", "C1"):
                            nc.scalar.copy(sg, x).then_inc(X.empty(s).sem, 1)
                        else:
                            if t == 0:
                                prev = {"B2": None, "C2": "B", "M1": "C", "A2": "M"}[c]
                                if prev:
                                    wait(act, o_stored, prev)
                                else:
                                    wait(act, X.fill(("P", "mm", 1)), ("P", "mm", 1))
                                if c == "C2":
                                    wait(act, X.fill(("V", last_of["B"])), ("V", last_of["B"]))
                                    wait(act, X.fill(("V", items[n_item[last_of["B"]] - 1])), ("V", items[n_item[last_of["B"]] - 1]))
                                    wait(act, v_stored, ("B2", 8))
                                if c == "B2":
                                    act.wait_ge(v_stored.sem, v_stored.at(("mm", 1)))
                            if c in ("B2", "C2"):
                                nc.scalar.copy(vX[:, t, :], x[:, 0:W])
                            else:
                                nc.scalar.copy(sg[:, 0:W], x[:, 0:W])
                            nc.scalar.activation(sg[:, W:2 * W], x[:, W:2 * W], ACT.Tanh, scale=0.5)
                            nc.scalar.mul(gate[:, t, :], x[:, W:2 * W], 0.5).then_inc(X.empty(s).sem, 1)
                        act.drain().then_inc(staged.sem, 1)
                    elif k == "TR" and s in T.slot:
                        c, t = s[1:]
                        wait(act, T.fill(s), s)
                        if t == 0:
                            prev = {"A1": None, "B1": "idx", "C1": "B", "M1": "C", "A2": "M"}.get(c)
                            if prev == "idx":
                                wait(act, S.fill(("is", PAIRS - 1)), ("is", PAIRS - 1))
                                wait(act, qs_ready, ("is", PAIRS - 1))
                            elif prev:
                                lst = ("S", last_of[prev])
                                wait(act, S.fill(lst), lst)
                                wait(act, qs_ready, lst)
                        tp = T.ap(s)
                        cols = slice(t * P, (t + 1) * P)
                        if c == "mm":
                            nc.scalar.copy(mK[:, :, cols], tp[:, 0:W].rearrange("p (g c) -> p g c", g=2)
                                           ).then_inc(T.empty(s).sem, 1)
                        else:
                            for hp in range(2):
                                half = slice(64 * hp, 64 * hp + 64)
                                last = nc.scalar.mul(qT[half, hp:H:2, cols], tp[half, 0:W].rearrange("p (g c) -> p g c", g=2), 0.125)
                            if c in ("B1", "C1"):
                                last = nc.scalar.copy(kT[:, :, cols], tp[:, W:2 * W].rearrange("p (g c) -> p g c", g=2))
                            if c == "A1":
                                for src in range(2):
                                    for dst in range(2):
                                        last = nc.scalar.copy(kA[64 * dst:64 * dst + 64, src, cols],
                                                              tp[64 * src:64 * src + 64, W:W + P])
                            last.then_inc(T.empty(s).sem, 1)
                        act.drain().then_inc(turned.sem, 1)
                    elif k == "F":
                        wait(act, f_dve, "z")
                        nc.scalar.activation(lf[:, 1, :], lf[:, 1, :], ACT.Exp, scale=-1.0).then_inc(f_ready.sem, 1)
                        act.wait_ge(f_ready.sem, f_ready.at("exp"))
                        nc.scalar.activation(lf[:, 1, :], lf[:, 1, :], ACT.Ln, bias=1.0).then_inc(f_ready.sem, 1)
                    elif k in ("ip", "is"):
                        n = n_work[s]
                        L = (s[1] + 1) * P if k == "ip" else SKEYS
                        wait(act, S.fill(s), s)
                        if n >= 2:
                            pv = [x for x in n_work if n_work[x] == n - 2][0]
                            if pv[0] == "ip":
                                wait(act, scored, pv)
                            else:
                                wait(act, S.fill(("iw", pv[1])), ("iw", pv[1]))
                        else:
                            wait(act, T.fill((("turn", 10), 1)), (("turn", 10), 1))
                        nc.scalar.activation(buf(n)[:, 0:L], S.ap(s)[:, 0:L], ACT.Relu).then_inc(S.empty(s).sem, 1)
                        act.drain().then_inc(relued.sem, 1)
                    elif k == "S":
                        x_ = s[1]
                        L = blocks(x_) * P
                        n = n_item[x_]
                        wait(act, maxes, x_)
                        p = buf(n)[:, 0:L]
                        if n >= 4:
                            wait(act, rsum, items[n - 4])
                        nc.scalar.activation(p, p, ACT.Exp, bias=stat[:, n % 4, 1:2], accum_out=stat[:, n % 4, 2:3]
                                             ).then_inc(probs.sem, 1)
                    elif k == "T":
                        x_ = s[1]
                        n, u = n_item[x_], (s, 0)
                        w = min(4, blocks(x_)) * P
                        wait(act, T.fill(u), u)
                        if n >= 2:
                            pr = items[n - 2]
                            q = ("R", pr) if is_sample(pr) else ("V", pr)
                            wait(act, X.fill(q), q)
                        nc.scalar.copy(turned_buf(n)[:, 0:w], T.ap(u)[:, 0:w]).then_inc(T.empty(u).sem, 1)
                        act.drain().then_inc(pt_act.sem, 1)
                    elif k == "OT" or k == "OA":
                        t = s[1]
                        if k == "OT":
                            for g in range(2):
                                u = (s, g)
                                wait(act, T.fill(u), u)
                                last = nc.scalar.copy(hT[:, 2 + 3 * g:5 + 3 * g, t * P:(t + 1) * P],
                                                      T.ap(u)[:, 0:3 * P].rearrange("p (b c) -> p b c", b=3))
                                last.then_inc(T.empty(u).sem, 1)
                        else:
                            wait(act, T.fill(s), s)
                            nc.scalar.copy(hT[:, 0:2, t * P:(t + 1) * P], T.ap(s)[:, 0:2 * P].rearrange("p (b c) -> p b c", b=2)
                                           ).then_inc(T.empty(s).sem, 1)
                        act.drain().then_inc(merged.sem, 1)
                next_layer(act, "scalar")
            for t in TILES:
                act.wait_ge(fin_loaded[t % 4], 16 * (t // 4 + 1))
                nc.scalar.activation(sc[:, 0:D], work[:, t % 4, :], ACT.Square, accum_out=rstd[:, 0, t:t + 1]).then_inc(fin_sq, 1)
                act.wait_ge(fin_sq, t + 1)
                nc.scalar.activation(rstd[:, 1, t:t + 1], rstd[:, 0, t:t + 1], ACT.Sqrt, scale=1.0 / D,
                                     bias=con[:, NCONST:NCONST + 1]).then_inc(fin_root, 1)

        @block.vector
        def _(dve):
            v = nc.vector
            v.memset(qT[:, :, :], 0.0)
            v.memset(qs[:, :, :], 0.0)
            v.memset(credit[:, :], 0.0).then_inc(s_zero, 1)
            dve.wait_ge(s_zero, 1)
            dve.wait_ge(s_const, 16)

            def rotate(sg, heads, t):
                a = sg[:, 0:heads * HD].rearrange("p (h d) -> p h d", h=heads)
                x1, x2 = a[:, :, 0:ROT], a[:, :, ROT:2 * ROT]
                co = con[:, C_ROPE + 16 * t:C_ROPE + 16 * t + 8].unsqueeze(1).to_broadcast([P, heads, ROT])
                si = con[:, C_ROPE + 16 * t + 8:C_ROPE + 16 * t + 16].unsqueeze(1).to_broadcast([P, heads, ROT])
                u1 = rtmp[:, 0, 0:heads * ROT].rearrange("p (h d) -> p h d", h=heads)
                u2 = rtmp[:, 1, 0:heads * ROT].rearrange("p (h d) -> p h d", h=heads)
                v.tensor_tensor(u1, x1, si, ALU.mult)
                v.tensor_tensor(u2, x2, si, ALU.mult)
                v.tensor_tensor(x1, x1, co, ALU.mult)
                v.tensor_tensor(x2, x2, co, ALU.mult)
                dve.drain()
                v.tensor_tensor(x1, x1, u2, ALU.subtract)
                return v.tensor_tensor(x2, x2, u1, ALU.add)

            with dve.Fori(0, DEPTH) as l:
                for units_ in (S, T, X):
                    for q in units_.emptied:
                        dve.drain().then_inc(q.sem, 1)
                for s in order:
                    k = s[0]
                    if k == "norm":
                        n = s[1]
                        wait(dve, rooted, n)
                        if n == 0:
                            wait(dve, gains_loaded, "g")
                        v.reciprocal(rstd[:, 2, n:n + 1], rstd[:, 1, n:n + 1])
                        dve.drain()
                        v.scalar_tensor_tensor(out=work[:, n % 4, :], in0=work[:, n % 4, :], scalar=rstd[:, 2, n:n + 1],
                                               in1=bias[:, int(n >= 9), :], op0=ALU.mult, op1=ALU.mult).then_inc(normed.sem, 1)
                    elif k == "turn":
                        n = s[1]
                        u = (s, 1)
                        wait(dve, T.fill(u), u)
                        src = T.ap(u)[:, :].rearrange("p (b c) -> p b c", b=4)
                        if n < 9:
                            dst = hT[:, 4:8, n * P:(n + 1) * P]
                        else:
                            dst = gate[:, :, :].rearrange("p a b -> p (a b)")[:, 4 * MEM:8 * MEM].rearrange(
                                "p (k c) -> p k c", k=4)[:, :, (n - 9) * P:(n - 8) * P]
                        v.tensor_copy(dst, src).then_inc(T.empty(u).sem, 1)
                        dve.drain().then_inc(h_dve.sem, 1)
                    elif k == "P" and (s[1], s[2]) in worked.upto:
                        c, t = s[1:]
                        wait(dve, staged, (c, t))
                        sg = stage[:, slot_of[(c, t)], :]
                        if c == "A1":
                            rotate(sg, 6, t)
                            v.tensor_copy(vA[:, t, :], sg[:, 384:448])
                            v.tensor_scalar(wi[:, t, :], sg[:, 448:452], H ** -0.5, None, ALU.mult)
                            v.tensor_tensor(lf[:, 0, t * H:(t + 1) * H], sg[:, 452:456], bfb[:, :], ALU.add)
                        else:
                            if c == "A2":
                                rotate(sg, 4, t)
                            v.scalar_tensor_tensor(out=gate[:, t, :], in0=sg[:, W:2 * W], scalar=1.0, in1=gate[:, t, :],
                                                   op0=ALU.add, op1=ALU.mult)
                        dve.drain().then_inc(worked.sem, 1)
                    elif k == "P" and s[1][0] == "O":
                        c, t = s[1:]
                        n = outs.index((c, t))
                        wait(dve, X.fill(s), s)
                        wait(dve, res_loaded[n % 2], (c, t))
                        if n >= 2:
                            wait(dve, res_stored[n % 2], outs[n - 2])
                        v.tensor_tensor(work[:, 2 + n % 2, 0:512], X.ap(s), work[:, n % 2, 0:512], ALU.add
                                        ).then_inc(X.empty(s).sem, 1)
                        dve.drain().then_inc(res_added.sem, 1)
                    elif k == "F":
                        z, e, m = lf[:, 0, :], lf[:, 1, :], lf[:, 2, :]
                        v.scalar_tensor_tensor(out=e, in0=z, scalar=-1.0, in1=z, op0=ALU.mult, op1=ALU.max)
                        v.tensor_scalar(m, z, 0.0, None, ALU.min)
                        dve.drain().then_inc(f_dve.sem, 1)
                        wait(dve, f_ready, "ln")
                        v.tensor_tensor(z, m, e, ALU.subtract)
                        dve.drain().then_inc(f_dve.sem, 1)
                    elif k == "ip":
                        _, t, h = s
                        L = (t + 1) * P
                        dst = sc[:, SC_OFF[t]:SC_OFF[t] + L]
                        wait(dve, relued, s)
                        r = buf(n_work[s])[:, 0:L]
                        if (t, h) == (SEL_TILES[0], 0):
                            dve.wait_ge(lines_sem, 32)
                        if h == 0:
                            v.tensor_scalar(dst, r, wi[:, t, 0:1], None, ALU.mult)
                        else:
                            v.scalar_tensor_tensor(out=dst, in0=r, scalar=wi[:, t, h:h + 1], in1=dst, op0=ALU.mult, op1=ALU.add)
                        dve.drain().then_inc(scored.sem, 1)
                        if h == H - 1:
                            v.tensor_tensor(dst[:, L - P:L], dst[:, L - P:L], con[:, C_CM + P:C_CM + 2 * P], ALU.add)
                            dve.drain()
                    elif k == "wrow":
                        wait(dve, f_dma, "rows")
                        frow, fsam = work[0:4, 2, :], work[0:32, 3, :]
                        v.tensor_tensor_scan(frow, frow, frow, 0.0, ALU.add, ALU.bypass)
                        v.tensor_tensor_scan(fsam[:, 0:PAST + STEPS], fsam[:, 0:PAST + STEPS], fsam[:, 0:PAST + STEPS], 0.0,
                                             ALU.add, ALU.bypass)
                        dve.drain().then_inc(f_dve.sem, 1)
                        v.tensor_copy(fsam[:, PAST + STEPS:SKEYS].rearrange("p (b i) -> p b i", i=STEPS),
                                      fsam[:, PAST:PAST + STEPS].unsqueeze(1).to_broadcast([32, 7, STEPS]))
                        dve.drain().then_inc(f_dve.sem, 1)
                        wait(dve, X.fill(s), s)
                        for j in range(PAIRS):
                            v.tensor_tensor_reduce(wrow[:, 4:8], X.ap(s)[:, 4 * j:4 * j + 4], con[:, C_HM:C_HM + 4], 1.0, 0.0,
                                                   ALU.mult, ALU.add, wrow[:, j:j + 1])
                            dve.drain()
                        dve.drain().then_inc(X.empty(s).sem, 1)
                        for j in range(PAIRS):
                            v.tensor_scalar(wsel[:, j, :], con[:, C_SEL:C_SEL + 32], wrow[:, j:j + 1], None, ALU.mult)
                        dve.drain().then_inc(scored.sem, 1)
                    elif k == "iw":
                        j = s[1]
                        wait(dve, S.fill(s), s)
                        if j == 0:
                            wait(dve, tmask, "m")
                            v.memset(sc[:, SC_OFF[ST_] + SKEYS:SC_W], 1e30)
                        r0 = slice(32 * j, 32 * j + 32)
                        dst = sc[r0, SC_OFF[ST_]:SC_OFF[ST_] + SKEYS]
                        v.tensor_copy(dst[:, 0:PAST], S.ap(s)[r0, 0:PAST])
                        v.tensor_tensor(dst[:, PAST:SKEYS], S.ap(s)[r0, PAST:SKEYS], dst[:, PAST:SKEYS], ALU.add
                                        ).then_inc(S.empty(s).sem, 1)
                        dve.drain().then_inc(scored.sem, 1)
                    elif k == "K":
                        _, t, i, end = s
                        L = SKEYS + FILL if t == ST_ else (t + 1) * P
                        a = sc[:, SC_OFF[t]:SC_OFF[t] + L]
                        v.max(top8[:, :], a)
                        dve.drain()
                        v.match_replace(a, top8[:, :], a, TAKEN)
                        dve.drain()
                        if end:
                            v.tensor_scalar(a, a, 0.5 * TAKEN, NEG, ALU.is_ge, ALU.mult)
                            dve.drain().then_inc(selected.sem, 1)
                    elif k == "S":
                        x_ = s[1]
                        br, h, t = x_
                        n = n_item[x_]
                        L = blocks(x_) * P
                        wait(dve, S.fill(s), s)
                        src, dst = S.ap(s)[:, 0:L], buf(n)[:, 0:L]
                        mx, nm = stat[:, n % 4, 0:1], stat[:, n % 4, 1:2]
                        if n >= 2:
                            pr = items[n - 2]
                            g = (blocks(pr) + 3) // 4 - 1
                            wait(dve, T.fill((("T", pr), g)), (("T", pr), g))
                            wait(dve, probs, pr)
                        if br == "A" and h == 0 and t in (0, 1):
                            wait(dve, T.fill((("OT", 8), 1)), (("OT", 8), 1))
                        if n < 2:
                            wait(dve, S.fill(("iw", PAIRS - 1)), ("iw", PAIRS - 1))
                            wait(dve, f_dma, "out")
                        if br == "B" or br == "C":
                            if not is_sample(x_):
                                if t == 0:
                                    wait(dve, pbias, (br, h))
                                    if br == "C":
                                        v.tensor_tensor(bias[:, 0, 4 * P:5 * P], bias[:, 0, 4 * P:5 * P], con[:, C_CM + P:C_CM + 2 * P], ALU.add)
                                        v.tensor_scalar(bias[64:128, 0, 0:64], bias[64:128, 0, 0:64], NEG, None, ALU.add)
                                        dve.drain()
                                b_ = bias[:, 0, 0:L] if br == "B" else bias[:, 0, 5 * P - L:5 * P]
                            else:
                                if br == "B" or t == "s0":
                                    wait(dve, sbias, (br, int(t[1:])))
                                if br == "C" and t == "s0":
                                    v.tensor_copy(bias[:, 1, PAST + STEPS:SKEYS].rearrange("p (b i) -> p b i", i=STEPS),
                                                  bias[:, 1, PAST:PAST + STEPS].unsqueeze(1).to_broadcast([P, 7, STEPS]))
                                    dve.drain()
                                b_ = bias[:, 1, 0:L]
                            last = v.tensor_tensor_reduce(dst, src, b_, 1.0, NEG, ALU.subtract if br == "B" else ALU.add,
                                                          ALU.max, mx)
                        elif br == "A" and not is_sample(x_):
                            if t in SEL_TILES:
                                wait(dve, selected, t) if h == 0 else None
                                b_ = sc[:, SC_OFF[t]:SC_OFF[t] + L]
                            else:
                                b_ = con[:, C_CM + 2 * P - L:C_CM + 2 * P]
                            last = v.tensor_tensor_reduce(dst, src, b_, 1.0, NEG, ALU.add, ALU.max, mx)
                        else:
                            last = v.tensor_scalar(dst, src, 0.0, None, ALU.add, ALU.max, accum_out=mx)
                        last.then_inc(S.empty(s).sem, 1)
                        dve.drain().then_inc(logits.sem, 1)
                        v.tensor_scalar(nm, mx, -1.0, None, ALU.mult).then_inc(maxes.sem, 1)
                    elif k == "T":
                        x_ = s[1]
                        if blocks(x_) > 4:
                            n, u = n_item[x_], (s, 1)
                            w = (blocks(x_) - 4) * P
                            wait(dve, T.fill(u), u)
                            if n >= 2:
                                pr = items[n - 2]
                                q = ("R", pr) if is_sample(pr) else ("V", pr)
                                wait(dve, X.fill(q), q)
                            v.tensor_copy(turned_buf(n)[:, 512:512 + w], T.ap(u)[:, 0:w]).then_inc(T.empty(u).sem, 1)
                            dve.drain().then_inc(pt_dve.sem, 1)
                    elif k == "V":
                        x_ = s[1]
                        br, h, t = x_
                        n = n_item[x_]
                        wait(dve, probs, x_)
                        v.reciprocal(stat[:, n % 4, 3:4], stat[:, n % 4, 2:3]).then_inc(rsum.sem, 1)
                        dve.drain()
                        wait(dve, X.fill(s), s)
                        ri = stat[:, n % 4, 3:4]
                        if is_sample(x_):
                            o = X.ap(s)[:, 0:W].rearrange("p (h d) -> p h d", h=H)
                            if br == "A":
                                o = X.ap(s)[:, 0:HD].unsqueeze(1).to_broadcast([P, H, HD])
                            v.scalar_tensor_tensor(out=turned_buf(n)[:, 0:W].rearrange("p (h d) -> p h d", h=H), in0=o, scalar=ri,
                                                   in1=con[:, C_HM:C_HM + 4].unsqueeze(2).to_broadcast([P, H, HD]),
                                                   op0=ALU.mult, op1=ALU.mult).then_inc(X.empty(s).sem, 1)
                            dve.drain().then_inc(om_ready.sem, 1)
                        else:
                            g = gate[:, t, h * HD:(h + 1) * HD]
                            v.scalar_tensor_tensor(out=g, in0=X.ap(s)[:, 0:HD], scalar=ri, in1=g, op0=ALU.mult, op1=ALU.mult
                                                   ).then_inc(X.empty(s).sem, 1)
                            dve.drain().then_inc(gated.sem, 1)
                    elif k == "R":
                        j = int(s[1][2][1:])
                        wait(dve, X.fill(s), s)
                        r0 = slice(32 * j, 32 * j + 32)
                        v.tensor_tensor(gate[r0, ST_, :], X.ap(s)[r0, 0:W], gate[r0, ST_, :], ALU.mult).then_inc(X.empty(s).sem, 1)
                        dve.drain().then_inc(gated.sem, 1)
                next_layer(dve, "vector")
            dve.wait_ge(fin_gain, 16)
            for t in TILES:
                dve.wait_ge(fin_root, t + 1)
                v.reciprocal(rstd[:, 2, t:t + 1], rstd[:, 1, t:t + 1])
                dve.drain()
                v.scalar_tensor_tensor(out=work[:, t % 4, :], in0=work[:, t % 4, :], scalar=rstd[:, 2, t:t + 1],
                                       in1=bias[:, 0, :], op0=ALU.mult, op1=ALU.mult).then_inc(fin_done, 1)

        @block.gpsimd
        def _(pool):
            g = nc.gpsimd
            pool.wait_ge(s_zero, 1)
            pool.wait_ge(s_const, 16)

            def store(dst, src, sem_, **kw):
                pool.dma_start(dst, src, **kw).then_inc(sem_, 16)

            with pool.Fori(0, DEPTH) as l:
                def out_rows(name, t):
                    if t == ST_:
                        return rows(d["s" + name], l, P, 0, P)
                    return rows(d["p" + name], l, SEQ, t * P, P)

                line = sc[0:H, D:D + XL]
                pool.dma_start(line[:, XL - 256:XL], d["cb"][bass.ds(l * H, H), 0:256]).then_inc(lines_sem, 16)
                pool.wait_ge(lines_sem, 16)
                g.tensor_copy(line[:, 0:XL - 256], line[:, XL - 256:XL - 255].to_broadcast([H, XL - 256]))
                pool.drain()
                pool.dma_start(d["xl"], line).then_inc(lines_sem, 16)
                pool.wait_ge(lines_sem, 32)
                for h in range(H):
                    pool.dma_start(d["xr"][h * P:(h + 1) * P, :], d["xl"][h:h + 1, :].to_broadcast([P, XL])
                                   ).then_inc(lines_sem, 16)
                for s in order:
                    k = s[0]
                    if k == "P" and s[1][0] != "O":
                        c, t = s[1:]
                        sg = stage[:, slot_of[(c, t)], :]
                        done = stored[slot_of[(c, t)]].sem
                        if c == "mm":
                            wait(pool, staged, (c, t))
                            store(rows(d["pm_k"], l, MEM, t * P, P), sg[:, 0:W], done)
                            store(rows(d["pm_v"], l, MEM, t * P, P), mV[:, t, :], v_stored.sem)
                        elif c == "A1":
                            wait(pool, worked, (c, t))
                            store(out_rows("a_ki", t), sg[:, 256:320], done)
                            store(out_rows("a_k", t), sg[:, 320:384], done)
                            store(out_rows("a_v", t), sg[:, 384:448], done)
                            if t == ST_:
                                for j in range(PAIRS):
                                    last = g.tensor_scalar(wmask[:, 4 * j:4 * j + 4], wi[:, ST_, :], con[:, C_PM + j:C_PM + j + 1],
                                                           None, ALU.mult)
                                last.then_inc(wmask_ready.sem, 1)
                        elif c in ("B1", "C1"):
                            if c == "B1" or t >= 4:
                                wait(pool, staged, (c, t))
                                if c == "B1":
                                    store(out_rows("b_k", t), sg[:, W:2 * W], done)
                                elif t == ST_:
                                    store(out_rows("c_k", t), sg[:, W:2 * W], done)
                                else:
                                    store(rows(d["pc_k"], l, 512, (t - 4) * P, P), sg[:, W:2 * W], done)
                        elif c in ("B2", "C2"):
                            if c == "B2" or t >= 4:
                                wait(pool, staged, (c, t))
                                if c == "B2":
                                    store(out_rows("b_v", t), vX[:, t, :], v_stored.sem)
                                elif t == ST_:
                                    store(out_rows("c_v", t), vX[:, t, :], v_stored.sem)
                                else:
                                    store(rows(d["pc_v"], l, 512, (t - 4) * P, P), vX[:, t, :], v_stored.sem)
                    elif k == "F":
                        wait(pool, f_dve, "lf")
                        z = lf[:, 0, :].rearrange("p (t h) -> p t h", h=H)
                        store(rows(d["pb_lf"], l, SEQ, 0, SEQ).rearrange("(t p) h -> p t h", p=P), z[:, 0:8, :], f_dma.sem)
                        store(rows(d["sb_lf"], l, P, 0, P), z[:, 8, :], f_dma.sem)
                        store(d["lfnat"].rearrange("(t p) h -> p t h", p=P), z, f_dma.sem)
                        wait(pool, f_dma, "nat")
                        wait(pool, T.fill((("turn", 10), 1)), (("turn", 10), 1))
                        for h in range(H):
                            store(work[h:h + 1, 2, :], d["lfnat"][0:SEQ, h:h + 1].rearrange("s h -> h s"), f_dma.sem,
                                  allow_slow_non_contiguous=True)
                        store(work[0:32, 3, 0:PAST], rows(d["blf"], l, 32, 0, 32), f_dma.sem)
                        for h in range(H):
                            store(work[8 * h:8 * h + 8, 3, PAST:PAST + STEPS],
                                  d["lfnat"][SEQ:TOK, :].rearrange("(r i) h -> h r i", i=STEPS)[h], f_dma.sem,
                                  allow_slow_non_contiguous=True)
                    elif k == "wrow":
                        wait(pool, f_dve, "spread")
                        store(d["fp"], work[0:4, 2, :], f_dma.sem)
                        store(d["fs"], work[0:32, 3, 0:SKEYS], f_dma.sem)
                    elif k == "is":
                        j = s[1]
                        if j == 0:
                            wait(pool, turned, ("A1", 8))
                        else:
                            wait(pool, S.fill(("is", j - 1)), ("is", j - 1))
                        last = g.tensor_copy(qsA[:, :].rearrange("p (r h i) -> p r h i", r=2, h=H),
                                             qT[:, :, SEQ + 32 * j:SEQ + 32 * j + 32].rearrange("p h (r i) -> p r h i", r=2))
                        last.then_inc(qs_ready.sem, 1)
                    elif k == "S":
                        x_ = s[1]
                        br, h, t = x_
                        if not is_sample(x_) and t == 0 and br in "BC":
                            if (br, h) != ("B", 0):
                                pr = items[n_item[x_] - 2] if h else items[n_item[x_] - 2]
                                wait(pool, logits, pr)
                            else:
                                wait(pool, normed, 10)
                                wait(pool, f_dma, "out")
                            if br == "B":
                                pool.dma_start(bias[:, 0, :], d["fp"][h:h + 1, :].to_broadcast([P, SEQ])).then_inc(pbias.sem, 16)
                            else:
                                if h == 0:
                                    pool.wait_ge(lines_sem, 96)
                                src = bass.AP(d["xr"].tensor, h * P * XL + 127, [[XL - 1, P], [1, 5 * P]])
                                pool.dma_start(bias[:, 0, 0:5 * P], src).then_inc(pbias.sem, 16)
                            if br == "C" and h == 0:
                                wait(pool, logits, last_of["B"])
                                for r in range(2):
                                    for hh in range(H):
                                        p0 = 64 * r + 16 * hh
                                        src = bass.AP(d["xr"].tensor, hh * P * XL + 127, [[XL - 1, STEPS], [1, PAST + STEPS]])
                                        pool.dma_start(bias[p0:p0 + STEPS, 1, 0:PAST + STEPS], src).then_inc(sbias.sem, 16)
                        if is_sample(x_):
                            j = int(t[1:])
                            if br == "B":
                                if j:
                                    wait(pool, logits, ("B", j - 1, f"s{j - 1}"))
                                for r in range(2):
                                    for hh in range(H):
                                        p0, q = 64 * r + 16 * hh, 8 * hh + 2 * j + r
                                        pool.dma_start(bias[p0:p0 + STEPS, 1, 0:SKEYS],
                                                       d["fs"][q:q + 1, :].to_broadcast([STEPS, SKEYS])).then_inc(sbias.sem, 16)
                            if j == 0:
                                wait(pool, turned, ({"A": "A2", "M": "M1"}.get(br, br + "1"), 8))
                            prs = [y for y in items[:n_item[x_]] if is_sample(y)]
                            if prs:
                                wait(pool, S.fill(("S", prs[-1])), ("S", prs[-1]))
                            src = qT[:, :, SEQ + 32 * j:SEQ + 32 * j + 32].rearrange("p h (r i) -> p r h i", r=2)
                            if br == "A":
                                if j == 0:
                                    wait(pool, S.fill(("is", PAIRS - 1)), ("is", PAIRS - 1))
                                g.tensor_scalar(selj[:, :], con[:, C_SELT:C_SELT + P], con[:, C_PM + j:C_PM + j + 1], None,
                                                ALU.mult).then_inc(selj_ready.sem, 1)
                                last = g.tensor_copy(qsA[:, :].rearrange("p (r h i) -> p r h i", r=2, h=H), src)
                            else:
                                for gg in range(2):
                                    dst = qs[:, gg, :].rearrange("p (r h i) -> p r h i", r=2, h=H)[:, :, 2 * gg:2 * gg + 2, :]
                                    last = g.tensor_copy(dst, src[:, :, 2 * gg:2 * gg + 2, :])
                            last.then_inc(qs_ready.sem, 1)
                    elif k in ("V", "R") and s[1] == last_of[s[1][0]] and k == "R" and s[1][0] != "A":
                        br = s[1][0]
                        wait(pool, gated, s[1])
                        c0 = GCOL[br] - W
                        store(d["oscr"][:, c0:c0 + W].rearrange("(t p) c -> p t c", p=P), gate[:, :, :], o_stored.sem)
                    elif k == "P" and s[1][0] == "O":
                        c, t = s[1:]
                        n = outs.index((c, t))
                        wait(pool, res_added, (c, t))
                        h = 512 * int(c[1])
                        store(d["xres"][t * P:(t + 1) * P, h:h + 512], work[:, 2 + n % 2, 0:512], res_stored[n % 2].sem)
                for q in stored + [v_stored, f_dma, o_stored, pbias, sbias] + res_stored:
                    pool.wait_ge(q.sem, q.layer)
                pool.wait_ge(lines_sem, 96)
                pool.wait_ge(layer_over, 4)
                pool.dma_reset(layer_sems)
                pool.sem_clear(layer_sems)
                for q in go.values():
                    pool.sem_inc(q, 1)
            for t in TILES:
                pool.wait_ge(fin_done, t + 1)
                pool.dma_start(d["y"][t * P:(t + 1) * P, :], work[:, t % 4, :]).then_inc(fin_stored[t % 4], 16)
            for k in range(4):
                pool.wait_ge(fin_stored[k], 16 * len(TILES[k::4]))


def constants():
    con = np.zeros((P, NCONST + 1), np.float32)
    p = np.arange(P)
    con[:, C_ID:C_ID + P] = np.eye(P)
    con[:, C_TRI:C_TRI + P] = np.where(p[None, :] <= p[:, None], 0, NEG)
    con[:, C_CM + P:C_CM + 2 * P] = np.where(p[None, :] // 64 <= p[:, None] // 64, 0, NEG)
    r, h, i = p // 64, p // STEPS % H, p % STEPS
    for base, causal in ((C_FULL, False), (C_CAUS, True)):
        w = np.full((P, 224), NEG, np.float32)
        for step in range(STEPS):
            ok = (step <= i) | (not causal)
            w[p[ok], 96 + STEPS * r[ok] + step] = 0
        con[:, base:base + 224] = w
    con[:, C_SELT:C_SELT + P] = (p[:, None] % 32 == (STEPS * r + i)[None, :])
    con[:, C_SEL:C_SEL + 32] = ((STEPS * r + i)[:, None] == np.arange(32)[None, :])
    con[:, C_PM:C_PM + 4] = (p[:, None] // 32 == np.arange(4)[None, :])
    con[:, C_HM:C_HM + 4] = (h[:, None] == np.arange(4)[None, :])
    inv = np.float32(500000.0) ** (-np.arange(ROT, dtype=np.float32) / np.float32(ROT))
    for t in TILES:
        pos = (t * P + p if t < NT else PAST + p % STEPS).astype(np.float32)
        ang = (pos[:, None] * inv[None, :].astype(np.float32)).astype(np.float32)
        con[:, C_ROPE + 16 * t:C_ROPE + 16 * t + 8] = np.cos(ang.astype(np.float64))
        con[:, C_ROPE + 16 * t + 8:C_ROPE + 16 * t + 16] = np.sin(ang.astype(np.float64))
    con[:, NCONST] = EPS
    tmask = np.where(p[:, None] // STEPS == p[None, :] // STEPS, 0, NEG).astype(np.float32)
    return con, tmask


def lay_out(x_prompt, x_sample, cache_a_k, cache_a_v, cache_a_kidx, cache_b_k, cache_b_v, cache_b_logf,
            cache_c_k, cache_c_v, cache_mem_k, cache_mem_v, mem_prompt, w_in, w_out, g_norm, b_f, c_bias,
            g_mem, w_mem_kv, g_final):
    a = np.ascontiguousarray
    off, cols = 0, {}
    for name, n in (("a_q", W), ("a_k", HD), ("a_v", HD), ("a_qi", W), ("a_ki", HD), ("a_wi", H), ("a_g", W), ("b_q", W),
                    ("b_k", W), ("b_v", W), ("b_f", H), ("b_g", W), ("c_q", W), ("c_k", W), ("c_v", W), ("c_g", W),
                    ("m_q", W), ("m_g", W)):
        cols[name] = w_in[:, :, off:off + n]
        off += n
    join = lambda *names: np.concatenate([cols[n] for n in names], -1)
    a1 = join("a_qi", "a_ki", "a_k", "a_v", "a_wi", "b_f")
    a1 = np.concatenate([a1, np.zeros(a1.shape[:2] + (512 - a1.shape[2],), a1.dtype)], -1)
    chunks = {"A1": a1, "mm": w_mem_kv, "B1": join("b_q", "b_k"), "B2": join("b_v", "b_g"), "C1": join("c_q", "c_k"),
              "C2": join("c_v", "c_g"), "M1": join("m_q", "m_g"), "A2": join("a_q", "a_g"),
              "O0": w_out[:, :, :512], "O1": w_out[:, :, 512:]}
    w = np.stack([chunks[c] for c in CHUNKS], 1)
    w = w.reshape(DEPTH, len(CHUNKS), KT, P, 512).transpose(0, 1, 3, 2, 4)
    shared_k = lambda c: a(c.reshape(DEPTH, PAIRS, 2, PAST, HD).transpose(0, 1, 4, 2, 3).reshape(-1, 2 * PAST))
    heads_k = lambda c: a(c.reshape(DEPTH, PAIRS, 2, -1, 2, 2, HD).transpose(0, 1, 5, 6, 2, 4, 3).reshape(
        DEPTH * PAIRS * P, -1))
    values = lambda c: a(c.reshape(DEPTH, PAIRS, 2, c.shape[2] // P, P, -1).transpose(0, 1, 4, 2, 3, 5).reshape(
        DEPTH * PAIRS * P, -1))
    con, tmask = constants()
    return {
        "x": a(np.concatenate([x_prompt.reshape(SEQ, D), x_sample.reshape(P, D)])),
        "mem": a(mem_prompt.reshape(MEM, D)),
        "w": a(w.reshape(-1, KT * 512)),
        "gain": a(np.concatenate([np.stack([g_norm, g_mem], 1).reshape(2 * DEPTH, D), g_final[None]])),
        "bf": a(b_f),
        "cb": a(c_bias[:, :, ::-1].reshape(DEPTH * H, -1)),
        "blf": a(cache_b_logf.transpose(0, 3, 1, 2).reshape(DEPTH * H * R, PAST)),
        "kI": shared_k(cache_a_kidx), "kA": shared_k(cache_a_k), "vA": values(cache_a_v),
        "kB": heads_k(cache_b_k), "vB": values(cache_b_v), "kC": heads_k(cache_c_k), "vC": values(cache_c_v),
        "kM": heads_k(cache_mem_k), "vM": values(cache_mem_v),
        "const": con, "tmask": tmask,
    }


_OUTS = {"y": (TOK, D), "pa_k": (DEPTH * SEQ, HD), "pa_v": (DEPTH * SEQ, HD), "pa_ki": (DEPTH * SEQ, HD),
         "pb_k": (DEPTH * SEQ, W), "pb_v": (DEPTH * SEQ, W), "pb_lf": (DEPTH * SEQ, H),
         "pc_k": (DEPTH * 512, W), "pc_v": (DEPTH * 512, W), "pm_k": (DEPTH * MEM, W), "pm_v": (DEPTH * MEM, W),
         "sa_k": (DEPTH * P, HD), "sa_v": (DEPTH * P, HD), "sa_ki": (DEPTH * P, HD),
         "sb_k": (DEPTH * P, W), "sb_v": (DEPTH * P, W), "sb_lf": (DEPTH * P, H),
         "sc_k": (DEPTH * P, W), "sc_v": (DEPTH * P, W)}
_SCRATCH = {"xres": (TOK, D), "oscr": (TOK, 3 * W), "lfnat": (TOK, H), "fp": (H, SEQ), "fs": (H * R, SKEYS), "xl": (H, XL), "xr": (H * P, XL)}


def kernel(**inputs):
    import concourse.bacc as bacc
    from concourse.bass_utils import run_bass_kernel_spmd

    arrays = lay_out(**{k: np.asarray(v) for k, v in inputs.items()})
    nc = bacc.Bacc("TRN2", target_bir_lowering=False, num_devices=1)
    d = {n: nc.dram_tensor(f"in_{n}", a.shape, F32, kind="ExternalInput").ap() for n, a in arrays.items()}
    d |= {n: nc.dram_tensor(f"out_{n}", s, F32, kind="ExternalOutput").ap() for n, s in _OUTS.items()}
    d |= {n: nc.dram_tensor(f"scratch_{n}", s, F32, kind="Internal").ap() for n, s in _SCRATCH.items()}
    encoder(nc, d)
    r = run_bass_kernel_spmd(nc, [{f"in_{n}": a for n, a in arrays.items()}], core_ids=[0]).results[0]
    o = {n: r[f"out_{n}"] for n in _OUTS}
    res = [o["y"][:SEQ].reshape(1, SEQ, D), o["y"][SEQ:].reshape(R, STEPS, D)]
    for n in list(_OUTS)[1:]:
        tail = (H, HD) if n[1] in "bcm" and n[-2:] != "lf" else (_OUTS[n][1],)
        lead = (DEPTH, 1, _OUTS[n][0] // DEPTH) if n[0] == "p" else (DEPTH, R, STEPS)
        res.append(o[n].reshape(lead + tail))
    return tuple(res)
```

```python
from contextlib import ExitStack

import numpy as np

import concourse.bass as bass
from concourse import mybir

F32 = mybir.dt.float32
ALU = mybir.AluOpType
ACT = mybir.ActivationFunctionType

P = 128
D = 1024
KT = D // P
SEQ = 1024
NT = SEQ // P
ST_ = NT
TILES = list(range(NT + 1))
TOK = SEQ + P
DEPTH = 2
NORMS = NT + 1 + 2
R, STEPS = 8, 16
PAIRS = R // 2
PAST = 512
H, HD = 4, 64
W = H * HD
MEM = 256
TOPK_P = min(256, SEQ // 4)
TOPK_S = min(256, (PAST + STEPS) // 4)
ROT = 8
EPS = 1e-6
NEG = -1.0e30
TAKEN = -3.0e38
SKEYS = PAST + P
CHUNKS = ["A1", "mm", "B1", "B2", "C1", "C2", "M1", "A2", "O0", "O1"]
BRANCHES = "BCMA"
UNITS = {"B": ["B1", "B2"], "C": ["C1", "C2"], "M": ["M1"], "A": ["A2"]}
RING = 5
FIRST = {br: c[0] for br, c in UNITS.items()}
SPARE_UNIT = {"B1": 6.8, "C1": 6.8, "A2": 5.6}
LAG = 2
SPARE_ITEM = [0.05, 1.0]
GCOL = {"A": 0, "B": W, "C": 2 * W, "M": 3 * W}
XL = 767

C_ID, C_TRI, C_CM, C_FULL, C_CAUS, C_SELT, C_SEL, C_PM, C_HM, C_ROPE = np.cumsum(
    [0, 128, 128, 256, 224, 224, 128, 32, 4, 4]).tolist()
NCONST = C_ROPE + 9 * 16

SEL_TILES = [t for t in range(NT) if (t + 1) * P > TOPK_P]
SC_OFF, _n = {}, 0
for _t in SEL_TILES:
    SC_OFF[_t] = _n
    _n += (_t + 1) * P
SC_OFF[ST_] = _n
FILL = -TOPK_S % 8
SC_W = _n + SKEYS + FILL


def chunk_tiles(c):
    return [0, 1] if c == "mm" else TILES


def key_tiles(br, t):
    return {"A": range(t + 1), "B": range(t + 1), "C": range(max(0, t - 4), t + 1), "M": range(2)}[br]


def attention_items(br, t):
    j = t - (NT - PAIRS if br == "A" else 0)
    return [(br, h, t) for h in range(H)] + ([(br, j, f"s{j}")] if 0 <= j < PAIRS else [])


def is_sample(item):
    return isinstance(item[2], str)


def blocks(item):
    if is_sample(item):
        return 2 if item[0] == "M" else 5
    return len(key_tiles(item[0], item[2]))


def topk_rounds():
    out = []
    pairs = list(zip(SEL_TILES[0::2], SEL_TILES[1::2]))
    for pair in pairs[:2] + [(ST_,)] + pairs[2:]:
        n = (TOPK_S + FILL if pair == (ST_,) else TOPK_P) // 8
        out += [tuple((t, i, i == n - 1) for t in pair) for i in range(n)]
    return out


def layer_order():
    o = []
    rounds = topk_rounds()
    spare = [0.0]
    cost = lambda t: (2 * ((SKEYS + FILL if t == ST_ else (t + 1) * P) + 60) + 90) / 960
    pushed = []
    unit = [None]

    def select(time):
        spare[0] += time
        while rounds and spare[0] > 0:
            x = rounds.pop(0)
            o.append(("K", x))
            spare[0] -= sum(cost(t) for t, _, _ in x)

    def push(item):
        n = len(pushed)
        pushed.append(item)
        at = lambda i: pushed[i] if i >= 0 else None
        if at(n - 2):
            o.append(("T", at(n - 2)))
        if item and item[0] == "A":
            strip = ST_ if is_sample(item) else item[2]
            while any(t == strip for x in rounds for t, _, _ in x):
                o.append(("K", rounds.pop(0)))
        if item:
            o.append(("S", item))
            if is_sample(item) and item[1] + 1 < PAIRS:
                o.append(("Q", (item[0], item[1] + 1, f"s{item[1] + 1}")))
            spare[0] += SPARE_ITEM[is_sample(item)] * (1 if is_sample(item) else blocks(item))
        if at(n - 3):
            o.append(("V", at(n - 3)))
        if at(n - 4) and is_sample(at(n - 4)):
            o.append(("R", at(n - 4)))

    def turn_last():
        if unit[0]:
            c, t = unit[0]
            o.append(("TR", c, t))
            if t == ST_ and c in FIRST.values():
                br = c[0]
                o.append(("Q", (br, 0, "s0")))
            unit[0] = None

    def project(c, t):
        select(SPARE_UNIT.get(c, 6.2))
        o.append(("P", c, t))
        turn_last()
        unit[0] = (c, t)

    o += [("norm", 0), ("norm", 1), ("turn", 0)]
    for n in TILES:
        o += [("norm", n + 2)] if n + 2 < NORMS else []
        o += [("turn", n + 1), ("P", "A1", n)]
        o += [("TR", "A1", n - 1)] if n else []
    o += [("turn", NORMS - 1), ("P", "mm", 0), ("TR", "A1", ST_), ("P", "mm", 1), ("TR", "mm", 0), ("TR", "mm", 1)]
    o.append(("F",))
    o += [("ip", t, h) for t in SEL_TILES for h in range(H)]
    o.append(("wrow",))
    for j in range(PAIRS):
        o.append(("is", j))
        if j:
            o.append(("iw", j - 1))
    o.append(("iw", PAIRS - 1))
    queue = []

    def attend(keep):
        while len(queue) > keep:
            push(queue.pop(0))

    for br in BRANCHES:
        for t in [ST_] + TILES[:NT]:
            if t == ST_:
                turn_last()
                attend(max(len(queue) // 2, 1))
            for n, c in enumerate(UNITS[br]):
                if t == 0 and br == "C" and n == 1:
                    for _ in range(3):
                        push(None)
                project(c, t)
                if t == ST_:
                    attend(0 if c == UNITS[br][-1] else len(queue) // 2)
                else:
                    attend(LAG if n + 1 == len(UNITS[br]) else (len(queue) + LAG) // 2)
            queue += attention_items(br, t) if t < NT else []
    turn_last()
    others = [("OT", t, g) for t in TILES for g in range(2)]
    while queue or pushed[-4:] != [None] * 4:
        push(queue.pop(0) if queue else None)
        for _ in range(2):
            o += [others.pop(0)] if others else []
    o += others + [("OA", 0)]
    for t in TILES:
        o += [("OA", t + 1)] if t < ST_ else []
        o.append(("P", "O0", t))
    o += [("P", "O1", t) for t in TILES]
    return o


class Signal:

    def __init__(self, sem, events, worth=lambda e: 1, credit=0):
        self.sem, self.credit, self.upto = sem, credit, {}
        n = 0
        for e in events:
            assert e not in self.upto, e
            n += worth(e)
            self.upto[e] = n
        self.layer = n
        self.list = list(events)

    def at(self, event):
        return self.credit + self.upto[event]

    def before(self, n):
        return self.credit + (self.upto[self.list[n - 1]] if n else 0)


class Units:

    def __init__(self, sem, name, aps, uses):
        n = len(aps)
        self.aps, self.slot = aps, {u: i % n for i, u in enumerate(uses)}
        self.filled = [Signal(sem(f"{name}{k}_filled"), uses[k::n]) for k in range(n)]
        self.emptied = [Signal(sem(f"{name}{k}_emptied"), uses[k::n], credit=1) for k in range(n)]
        self.index = {u: i // n for i, u in enumerate(uses)}

    def ap(self, use):
        return self.aps[self.slot[use]]

    def fill(self, use):
        return self.filled[self.slot[use]]

    def empty(self, use):
        return self.emptied[self.slot[use]]

    def free(self, use):
        return self.empty(use).before(self.index[use])


def encoder(nc, d):
    order = layer_order()
    items = [s[1] for s in order if s[0] == "S"]
    with ExitStack() as ctx:
        def sb(name, *shape):
            return ctx.enter_context(nc.sbuf_tensor(name, [P] + list(shape), F32))

        def sem(name):
            return ctx.enter_context(nc.semaphore(name))

        hT = sb("hT", KT, TOK)
        wring = sb("wring", 2, KT * 512)
        qT = sb("qT", H, TOK)
        kA = sb("kA", 2, TOK)
        kT = sb("kT", 2, TOK)
        vA = sb("vA", 9, HD)
        vX = sb("vX", 9, W)
        gate = sb("gate", 9, W)
        bias = sb("bias", H * 5 * P + SKEYS)
        gains = bias[:, 0:2 * D].rearrange("p (n c) -> p n c", n=2)
        halves = bias[:, 0:2 * D].rearrange("p (h c) -> p h c", h=H)
        strips = bias[:, 0:H * 5 * P].rearrange("p (h c) -> p h c", h=H)
        sbias_ = bias[:, H * 5 * P:]
        shared = sb("shared", RING * D + SC_W)
        cache = shared[:, 0:RING * D].rearrange("p (n c) -> p n c", n=RING)
        sc = shared[:, RING * D:RING * D + SC_W]
        xs = shared[:, 0:(NT + 1) * D].rearrange("p (t c) -> p t c", c=D)
        work = sb("work", 4, 1024)
        stage = sb("stage", 2, 512)
        mK = sb("mK", 2, MEM)
        mV = sb("mV", 2, W)
        con = sb("con", NCONST + 1)
        qs = sb("qs", 2, P)
        qsA = qs[:, 0, :]
        selj = sb("selj", P)
        wsel = selj[:, :].rearrange("p (j q) -> p j q", j=PAIRS)
        wi = sb("wi", 9, H)
        lf = sb("lf", 3, 9 * H)
        rstd = sb("rstd", 3, 11)
        stat = sb("stat", 4, 4)
        top8 = sb("top8", 2, 8)
        wmask = sb("wmask", 16)
        wrow = sb("wrow", 8)
        rtmp = sb("rtmp", 2, 6 * ROT)
        bfb = sb("bfb", H)
        credit = sb("credit", 1)

        psS = ctx.enter_context(nc.psum_tensor("psS", [P, 2, 1024], F32))
        psT = ctx.enter_context(nc.psum_tensor("psT", [P, 2, 512], F32))
        psX = ctx.enter_context(nc.psum_tensor("psX", [P, 2, 512], F32))

        ident = con[:, C_ID:C_ID + P]

        s_const = sem("const_loaded")
        s_zero = sem("zeros_set")
        x_in = [sem(f"x{t}_loaded") for t in TILES]
        layer_first = x_in[-1].num + 1

        s_uses, t_uses, x_uses = [], [], []
        for s in order:
            k = s[0]
            if k == "turn":
                t_uses += [(s, 0), (s, 1)]
            elif k == "P":
                x_uses.append(s)
            elif k == "TR" and s[1] in ("mm", "A1", "B1", "C1", "M1", "A2"):
                t_uses.append(s)
            elif k in ("ip", "is", "iw", "S"):
                s_uses.append(s)
            elif k == "wrow":
                x_uses.append(s)
            elif k == "T":
                t_uses += [(s, g) for g in range((blocks(s[1]) + 3) // 4)]
            elif k in ("V", "R"):
                x_uses.append(s)
            elif k in ("OT", "OA"):
                t_uses.append(s)
        S = Units(sem, "scores", [psS[:, k, :] for k in range(2)], s_uses)
        T = Units(sem, "turned", [psT[:, k, :] for k in range(2)], t_uses)
        X = Units(sem, "acc", [psX[:, k, :] for k in range(2)], x_uses)

        units = [s[1:] for s in order if s[0] == "P" and s[1][0] != "O"]
        slot_of = {u: n % 2 for n, u in enumerate(units)}
        stored_dmas = lambda u: {"mm": 1, "A1": 3, "B1": 1}.get(u[0], int(u[0] == "C1" and u[1] >= 4))
        norms = list(range(NORMS))
        mem_loaded = [Signal(sem(f"mem_loaded{k}"), [NT + 1 + k], lambda e: 16) for k in range(2)]
        x_saved = Signal(sem("x_saved"), ["x"], lambda e: 16 * len(TILES))
        gain_loaded = Signal(sem("gain_loaded"), ["g"], lambda e: 16)
        small_loaded = Signal(sem("small_loaded"), ["g"], lambda e: 32)
        squares = Signal(sem("squares_summed"), norms)
        rooted = Signal(sem("root_taken"), norms)
        normed = Signal(sem("tile_normed"), norms)
        w_loaded = [Signal(sem(f"w_loaded{k}"), CHUNKS[k::2], lambda e: 16) for k in range(2)]
        h_act = Signal(sem("hT_by_act"), norms)
        h_dve = Signal(sem("hT_by_dve"), norms)
        staged = Signal(sem("unit_staged"), units)
        worked = Signal(sem("unit_worked"), [u for u in units if u[0] in ("A1", "A2", "B2", "C2", "M1")])
        stored = [Signal(sem(f"stage{k}_stored"), [u for u in units if slot_of[u] == k and stored_dmas(u)],
                         lambda u: 16 * stored_dmas(u)) for k in range(2)]
        v_units = [(c, t) for c, t in units if c == "B2" or (c == "C2" and t >= 4)]
        v_stored = Signal(sem("v_stored"), [u for u in [("mm", 0), ("mm", 1)] + v_units], lambda e: 16)
        turned = Signal(sem("operand_turned"), [s[1:] for s in t_uses if s[0] == "TR"])
        f_ready = Signal(sem("f_stage"), ["exp", "ln"])
        f_dve = Signal(sem("f_vector"), ["z", "lf", "scan", "spread"])
        f_dma = Signal(sem("f_moved"), ["nat", "rows", "out"],
                       lambda e: {"nat": 48, "rows": 16 * 9, "out": 32}[e])
        wmask_ready = Signal(sem("wmask_ready"), ["w"])
        lines_sem = sem("bias_lines_written")
        index_items = [s for s in order if s[0] in ("ip", "is")]
        relued = Signal(sem("index_relued"), index_items)
        scored = Signal(sem("index_scored"), [s for s in order if s[0] in ("ip", "iw", "wrow")])
        n_work = {}
        for s in order:
            if s[0] in ("ip", "is"):
                n_work[s] = len(n_work)
        qs_uses = [s for s in order if s[0] == "is"] + [("S", x) for x in items if is_sample(x)]
        qs_ready = Signal(sem("qs_ready"), qs_uses)
        parts = lambda br: range(2) if br in "BC" else [None]
        cache_loads = []
        for s in order:
            if s[0] == "is":
                cache_loads.append((s, "k", None))
            elif s[0] in ("S", "V") and is_sample(s[1]):
                cache_loads += [(s, "k" if s[0] == "S" else "v", r) for r in parts(s[1][0])]
        cslot = {u: n % RING for n, u in enumerate(cache_loads)}
        cdmas = lambda u: 2 if u[1] == "k" and (u[0][0] == "is" or u[0][1][0] == "A") else 1
        cache_loaded = [Signal(sem(f"cache{k}_loaded"), [u for u in cache_loads if cslot[u] == k],
                               lambda u: 16 * cdmas(u)) for k in range(RING)]
        early = lambda x: x[2] < NT // 2
        b_items = [x for x in items if x[0] == "B" and not is_sample(x) and not early(x)]
        last_early = [x for x in items if x[0] == "B" and not is_sample(x) and early(x)][-1]
        halves_loaded = Signal(sem("bias_halves_loaded"), ["B"], lambda e: 16)
        pbias = [Signal(sem(f"prompt_bias{k}_loaded"), b_items[k::2], lambda e: 16) for k in range(2)]
        strips_loaded = Signal(sem("strips_loaded"), ["C"], lambda e: 16)
        sbias_loads = [("B", j) for j in range(PAIRS)] + [("C", 0)]
        sbias = Signal(sem("sample_bias_loaded"), sbias_loads, lambda e: 32)
        tmask = Signal(sem("token_mask_loaded"), ["m"], lambda e: 16)
        logits = Signal(sem("logits_ready"), items)
        maxes = Signal(sem("max_ready"), items)
        probs = Signal(sem("probs_ready"), items)
        pt_act = Signal(sem("probs_turned_act"), items)
        rsum = Signal(sem("row_sum_inverted"), items)
        om_ready = Signal(sem("own_heads_kept"), [x for x in items if is_sample(x)])
        selj_ready = Signal(sem("selj_ready"), [x for x in items if is_sample(x) and x[0] == "A"])
        gated = Signal(sem("branch_gated"), [s[1] for s in order if s[0] == "R" or (s[0] == "V" and not is_sample(s[1]))])
        selected = Signal(sem("selected"), [t for s in order if s[0] == "K" for t, _, end in s[1] if end])
        o_stored = [Signal(sem(f"branch_tile{t}_stored"), list("BCM"), lambda e: 16) for t in TILES]
        ot_units = [s for s in order if s[0] == "OT"]
        o_loaded = [Signal(sem(f"branch_loaded{k}"), [s for s in ot_units if s[2] == k], lambda e: 16) for k in range(2)]
        merged = Signal(sem("merged_turned"), [s for s in order if s[0] in ("OT", "OA")])
        outs = [(c, t) for c in ("O0", "O1") for t in TILES]
        res_loaded = [Signal(sem(f"residual_loaded{k}"), outs[k::4], lambda e: 16) for k in range(4)]
        res_added = Signal(sem("residual_added"), outs)
        layer_over = sem("layer_over")
        layer_sems = range(layer_first, layer_over.num + 1)
        go = {n: sem(f"next_layer_{n}") for n in ("sync", "tensor", "scalar", "vector")}
        fin_gain = sem("fin_gain_loaded")
        fin_sq, fin_root, fin_done = sem("fin_squares"), sem("fin_root"), sem("fin_normed")
        y_stored = sem("y_stored")

        last_prompt = {br: (br, H - 1, NT - 1) for br in BRANCHES}
        last_sample = {br: (br, PAIRS - 1, f"s{PAIRS - 1}") for br in BRANCHES}
        before = {"B": None, "C": "B", "M": "C", "A": "M"}

        def wait(eng, signal, event):
            eng.wait_ge(signal.sem, signal.at(event))

        def rows(ap, l, per_layer, first, n):
            return ap[bass.ds(l * per_layer + first, n), :]

        def buf(n):
            return work[:, n % 2, :]

        def turned_buf(n):
            return work[:, 2 + n % 2, :]

        n_item = {x: n for n, x in enumerate(items)}

        def next_layer(eng, name):
            eng.drain().then_inc(layer_over, 1)
            eng.wait_ge(go[name], 1)
            eng.sem_clear(go[name])

        block = ctx.enter_context(nc.Block())

        @block.sync
        def _(sp):
            sp.dma_start(con[:, :], d["const"]).then_inc(s_const, 16)

            def load_chunk(l, c):
                n = CHUNKS.index(c)
                if n >= 2:
                    last = [s for s in order if s[0] == "P" and s[1] == CHUNKS[n - 2]][-1]
                    wait(sp, X.fill(last), last)
                sp.dma_start(wring[:, n % 2, :], rows(d["w"], l, len(CHUNKS) * P, n * P, P)
                             ).then_inc(w_loaded[n % 2].sem, 16)

            cache_state = [0]

            def load_cache(l, u):
                n = cache_state[0]
                assert cache_loads[n] == u
                cache_state[0] += 1
                if n >= RING:
                    use = cache_loads[n - RING][0]
                    units_ = X if use[0] == "V" else S
                    wait(sp, units_.fill(use), use)
                use, kind, r = u
                done = cache_loaded[cslot[u]].sem
                dst = cache[:, cslot[u], :]
                j = use[1] if use[0] == "is" else use[1][1]
                br = "I" if use[0] == "is" else use[1][0]
                p = HD if br in "AI" and kind == "k" else P
                src = rows(d[kind + br], l, PAIRS * p, j * p, p)
                if r is not None:
                    src = src[:, r * D:(r + 1) * D]
                w = src.shape[1]
                if br in "AI" and kind == "k":
                    sp.dma_start(dst[0:64, 0:w], src).then_inc(done, 16)
                    sp.dma_start(dst[64:128, 0:w], src).then_inc(done, 16)
                else:
                    sp.dma_start(dst[:, 0:w], src).then_inc(done, 16)

            with sp.Fori(0, DEPTH) as l:
                cache_state[0] = 0
                sp.dma_start(gains[:, 0, :], rows(d["gain"], l, 2, 0, 1).to_broadcast([P, D])).then_inc(gain_loaded.sem, 16)
                load_chunk(l, "A1")
                sp.dma_start(gains[:, 1, :], rows(d["gain"], l, 2, 1, 1).to_broadcast([P, D])).then_inc(small_loaded.sem, 16)
                sp.dma_start(bfb[:, :], rows(d["bf"], l, 1, 0, 1).to_broadcast([P, H])).then_inc(small_loaded.sem, 16)
                load_chunk(l, "mm")
                for t in TILES:
                    sp.wait_ge(x_in[t], 16)
                    sp.dma_start(d["xres"][t * P:(t + 1) * P, :], xs[:, t, :]).then_inc(x_saved.sem, 16)
                for k in range(2):
                    n = NT + 1 + k
                    wait(sp, T.fill((("turn", n - 4), 1)), (("turn", n - 4), 1))
                    sp.dma_start(work[:, n % 4, :], d["mem"][k * P:(k + 1) * P, :]).then_inc(mem_loaded[k].sem, 16)
                wait(sp, normed, ST_)
                wait(sp, x_saved, "x")
                sp.wait_ge(lines_sem, 32)
                sp.dma_start(sc[:, SC_OFF[ST_] + PAST:SC_OFF[ST_] + SKEYS], d["tmask"]).then_inc(tmask.sem, 16)
                nxt = [0]

                def cache_upto(l, n):
                    while nxt[0] < n:
                        load_cache(l, cache_loads[nxt[0]])
                        nxt[0] += 1

                count = lambda br: sum(1 for u in cache_loads if u[0][0] != "is" and u[0][1][0] == br)
                cache_upto(l, PAIRS)
                upto = PAIRS
                load_chunk(l, "B1")
                load_chunk(l, "B2")
                for br in BRANCHES:
                    upto += count(br)
                    cache_upto(l, upto)
                    for c in {"B": ["C1", "C2"], "C": ["M1", "A2"], "M": [], "A": ["O0", "O1"]}[br]:
                        load_chunk(l, c)
                wait(sp, turned, ("A2", NT - 1))
                for n, u in enumerate(ot_units):
                    _, t, g = u
                    if g == 0:
                        wait(sp, o_stored[t], "M")
                    if n >= 2:
                        wait(sp, T.fill(ot_units[n - 2]), ot_units[n - 2])
                    sp.dma_start(stage[:, g, 0:3 * P], d["oscr"][t * P:(t + 1) * P, 3 * P * g:3 * P * (g + 1)]
                                 ).then_inc(o_loaded[g].sem, 16)
                for n, (c, t) in enumerate(outs):
                    if n == 0:
                        wait(sp, gated, items[-1])
                    if n >= 4:
                        wait(sp, res_added, outs[n - 4])
                    h = 512 * int(c[1])
                    sp.dma_start(work[:, n % 4, 0:512], d["xres"][t * P:(t + 1) * P, h:h + 512]
                                 ).then_inc(res_loaded[n % 4].sem, 16)
                next_layer(sp, "sync")
            sp.dma_start(gains[:, 0, :], d["gain"][2 * DEPTH:2 * DEPTH + 1, :].to_broadcast([P, D])).then_inc(fin_gain, 16)
            for t in TILES:
                sp.wait_ge(fin_done, t + 1)
                sp.dma_start(d["y"][t * P:(t + 1) * P, :], xs[:, t, :]).then_inc(y_stored, 16)
            sp.wait_ge(y_stored, 16 * len(TILES))

        @block.tensor
        def _(pe):
            pe.wait_ge(s_const, 16)
            pe.wait_ge(s_zero, 1)

            def turn(out, src):
                return pe.transpose(out, src, ident)

            with pe.Fori(0, DEPTH) as l:
                for s in order:
                    k = s[0]
                    if k == "turn":
                        n = s[1]
                        wait(pe, normed, n)
                        for g in range(2):
                            u = (s, g)
                            pe.wait_ge(T.empty(u).sem, T.free(u))
                            for b in range(4):
                                kt = 4 * g + b
                                mm = turn(T.ap(u)[:, b * P:(b + 1) * P], work[:, n % 4, kt * P:(kt + 1) * P])
                            mm.then_inc(T.fill(u).sem, 1)
                    elif k == "P":
                        c, t = s[1:]
                        n = CHUNKS.index(c)
                        wait(pe, w_loaded[n % 2], c)
                        if c in ("A1", "mm"):
                            wait(pe, h_act, t + (9 if c == "mm" else 0))
                            wait(pe, h_dve, t + (9 if c == "mm" else 0))
                        if c == "O0":
                            wait(pe, merged, ("OA", t))
                        pe.wait_ge(X.empty(s).sem, X.free(s))
                        w = 456 if c == "A1" else 512
                        wv = wring[:, n % 2, :].rearrange("p (k c) -> p k c", k=KT)
                        for kt in range(KT):
                            if c == "mm":
                                lhs = gate[:, :, :].rearrange("p a b -> p (a b)")[:, kt * MEM + t * P:kt * MEM + (t + 1) * P]
                            else:
                                lhs = hT[:, kt, t * P:(t + 1) * P]
                            mm = pe.matmul(X.ap(s)[:, 0:w], lhs, wv[:, kt, 0:w], start=(kt == 0), stop=(kt == KT - 1))
                        mm.then_inc(X.fill(s).sem, 1)
                    elif k == "TR" and s in T.slot:
                        c, t = s[1:]
                        wait(pe, worked if c in ("A1", "A2") else staged, (c, t))
                        pe.wait_ge(T.empty(s).sem, T.free(s))
                        src = stage[:, slot_of[(c, t)], :]
                        nb = {"A1": 3, "B1": 4, "C1": 4}.get(c, 2)
                        for b in range(nb):
                            mm = turn(T.ap(s)[:, b * P:(b + 1) * P], src[:, b * P:(b + 1) * P])
                        mm.then_inc(T.fill(s).sem, 1)
                    elif k == "ip":
                        _, t, h = s
                        wait(pe, turned, ("A1", 8))
                        pe.wait_ge(S.empty(s).sem, S.free(s))
                        L = (t + 1) * P
                        for c0 in range(0, L, 512):
                            mm = pe.matmul(S.ap(s)[:, c0:min(L, c0 + 512)], qT[:, h, t * P:(t + 1) * P],
                                           kA[:, 0, c0:min(L, c0 + 512)], start=True, stop=True)
                        mm.then_inc(S.fill(s).sem, 1)
                    elif k == "wrow":
                        wait(pe, scored, order[order.index(s) - 1])
                        wait(pe, wmask_ready, "w")
                        pe.wait_ge(X.empty(s).sem, X.free(s))
                        pe.matmul(X.ap(s)[:, 0:16], con[:, C_SELT:C_SELT + P], wmask[:, :], start=True, stop=True
                                  ).then_inc(X.fill(s).sem, 1)
                    elif k == "is":
                        j = s[1]
                        wait(pe, qs_ready, s)
                        wait(pe, cache_loaded[cslot[(s, "k", None)]], (s, "k", None))
                        pe.wait_ge(S.empty(s).sem, S.free(s))
                        kc = cache[:, cslot[(s, "k", None)], :]
                        for r in range(2):
                            pe.matmul(S.ap(s)[64 * r:64 * r + 64, 0:PAST], qsA[:, 64 * r:64 * r + 64],
                                      kc[:, r * PAST:(r + 1) * PAST], start=True, stop=True)
                        pe.matmul(S.ap(s)[:, PAST:SKEYS], qsA[:, :], kA[:, 0, SEQ:TOK], start=True, stop=True
                                  ).then_inc(S.fill(s).sem, 1)
                    elif k == "iw":
                        j = s[1]
                        wait(pe, relued, ("is", j))
                        wait(pe, scored, ("wrow",))
                        pe.wait_ge(S.empty(s).sem, S.free(s))
                        r = buf(n_work[("is", j)])
                        o = S.ap(s)[32 * j:32 * j + 32, :]
                        pe.matmul(o[:, 0:PAST], wsel[:, j, :], r[:, 0:PAST], start=True, stop=True)
                        pe.matmul(o[:, PAST:SKEYS], wsel[:, j, :], r[:, PAST:SKEYS], start=True, stop=True
                                  ).then_inc(S.fill(s).sem, 1)
                    elif k == "S":
                        br, h, t = s[1]
                        o = S.ap(s)
                        wait(pe, turned, ({"A": "A2", "M": "M1"}.get(br, br + "1"), ST_ if is_sample(s[1]) else t))
                        pe.wait_ge(S.empty(s).sem, S.free(s))
                        if is_sample(s[1]):
                            wait(pe, qs_ready, s)
                            kc = []
                            for r in parts(br):
                                wait(pe, cache_loaded[cslot[(s, "k", r)]], (s, "k", r))
                                kc.append(cache[:, cslot[(s, "k", r)], :])
                            j = h
                            n = MEM if br == "M" else PAST
                            if br == "A":
                                for r in range(2):
                                    mm = pe.matmul(o[64 * r:64 * r + 64, 0:n], qsA[:, 64 * r:64 * r + 64],
                                                   kc[0][:, r * n:(r + 1) * n], start=True, stop=False)
                                wait(pe, selj_ready, s[1])
                                sm = sc[:, SC_OFF[ST_]:SC_OFF[ST_] + SKEYS]
                                wait(pe, selected, ST_)
                                pe.matmul(o[:, 0:n], selj[:, :], sm[:, 0:n], start=False, stop=True)
                                pe.matmul(o[:, n:SKEYS], qsA[:, :], kA[:, 1, SEQ:TOK], start=True, stop=False)
                                mm = pe.matmul(o[:, n:SKEYS], selj[:, :], sm[:, n:SKEYS], start=False, stop=True)
                            else:
                                for g in range(2):
                                    for r in range(2):
                                        mm = pe.matmul(o[64 * r:64 * r + 64, 0:n], qs[:, g, 64 * r:64 * r + 64],
                                                       kc[r][:, g * n:(g + 1) * n] if br != "M" else
                                                       kc[0][:, (r * 2 + g) * n:(r * 2 + g + 1) * n], start=(g == 0),
                                                       stop=(g == 1))
                                if br != "M":
                                    for g in range(2):
                                        pe.matmul(o[:, n:SKEYS], qs[:, g, :], kT[:, g, SEQ:TOK], start=(g == 0), stop=False)
                                    base = C_CAUS if br == "B" else C_FULL
                                    mm = pe.matmul(o[:, n:SKEYS], ident, con[:, base + 96 - 32 * j:base + 96 - 32 * j + P],
                                                   start=False, stop=True)
                            mm.then_inc(S.fill(s).sem, 1)
                        else:
                            kb = key_tiles(br, t)
                            keys = {"A": kA[:, 1, :], "B": kT[:, h // 2, :], "C": kT[:, h // 2, :], "M": mK[:, h // 2, :]}[br]
                            k0, L = kb[0] * P, len(kb) * P
            
                            q = qT[:, h, t * P:(t + 1) * P]
                            plain = L - P if br == "B" else L
                            for c0 in range(0, plain, 512):
                                c1 = min(plain, c0 + 512)
                                mm = pe.matmul(o[:, c0:c1], q, keys[:, k0 + c0:k0 + c1], start=True, stop=True)
                            if br == "B":
                                pe.matmul(o[:, plain:L], q, keys[:, k0 + plain:k0 + L], start=True, stop=False)
                                mm = pe.matmul(o[:, plain:L], ident, con[:, C_TRI:C_TRI + P], start=False, stop=True)
                            mm.then_inc(S.fill(s).sem, 1)
                    elif k == "T":
                        wait(pe, probs, s[1])
                        p = buf(n_item[s[1]])
                        nb = blocks(s[1])
                        for g in range((nb + 3) // 4):
                            u = (s, g)
                            pe.wait_ge(T.empty(u).sem, T.free(u))
                            for b in range(4 * g, min(nb, 4 * g + 4)):
                                mm = turn(T.ap(u)[:, (b - 4 * g) * P:(b - 4 * g + 1) * P], p[:, b * P:(b + 1) * P])
                            mm.then_inc(T.fill(u).sem, 1)
                    elif k == "V":
                        br, h, t = s[1]
                        nb = blocks(s[1])
                        pT = turned_buf(n_item[s[1]])
                        wait(pe, pt_act, s[1])
                        pe.wait_ge(X.empty(s).sem, X.free(s))
                        if br in "BC":
                            wait(pe, staged, (br + "2", ST_ if is_sample(s[1]) else t))
                        o = X.ap(s)
                        if is_sample(s[1]):
                            vc = []
                            for r in parts(br):
                                wait(pe, cache_loaded[cslot[(s, "v", r)]], (s, "v", r))
                                vc.append(cache[:, cslot[(s, "v", r)], :])
                            w = HD if br == "A" else W
                            nk = 2 if br == "M" else 4
                            for b in range(nb):
                                for r in range(2):
                                    if b < nk:
                                        k0 = b if br in "BC" else r * nk + b
                                        v = vc[r if br in "BC" else 0][:, k0 * w:(k0 + 1) * w]
                                    else:
                                        v = (vA if br == "A" else vX)[:, ST_, :]
                                    mm = pe.matmul(o[64 * r:64 * r + 64, 0:w], pT[:, b * P + 64 * r:b * P + 64 * r + 64], v,
                                                   start=(b == 0), stop=(b == nb - 1))
                        else:
                            kb = key_tiles(br, t)
                            for b, kt in enumerate(kb):
                                v = {"A": lambda: vA[:, kt, :], "M": lambda: mV[:, kt, h * HD:(h + 1) * HD]}.get(
                                    br, lambda: vX[:, kt, h * HD:(h + 1) * HD])()
                                mm = pe.matmul(o[:, 0:HD], pT[:, b * P:(b + 1) * P], v, start=(b == 0), stop=(b == nb - 1))
                        mm.then_inc(X.fill(s).sem, 1)
                    elif k == "R":
                        j = s[1][1]
                        wait(pe, om_ready, s[1])
                        pe.wait_ge(X.empty(s).sem, X.free(s))
                        pe.matmul(X.ap(s)[32 * j:32 * j + 32, 0:W], con[:, C_SEL:C_SEL + 32],
                                  turned_buf(n_item[s[1]])[:, 0:W], start=True, stop=True).then_inc(X.fill(s).sem, 1)
                    elif k == "OT":
                        g = s[2]
                        wait(pe, o_loaded[g], s)
                        pe.wait_ge(T.empty(s).sem, T.free(s))
                        for b in range(3):
                            mm = turn(T.ap(s)[:, b * P:(b + 1) * P], stage[:, g, b * P:(b + 1) * P])
                        mm.then_inc(T.fill(s).sem, 1)
                    elif k == "OA":
                        t = s[1]
                        wait(pe, gated, last_sample["A"] if t == ST_ else ("A", H - 1, t))
                        pe.wait_ge(T.empty(s).sem, T.free(s))
                        for b in range(2):
                            mm = turn(T.ap(s)[:, b * P:(b + 1) * P], gate[:, t, b * P:(b + 1) * P])
                        mm.then_inc(T.fill(s).sem, 1)
                next_layer(pe, "tensor")

        @block.scalar
        def _(act):
            for t in TILES:
                act.dma_start(xs[:, t, :], d["x"][t * P:(t + 1) * P, :]).then_inc(x_in[t], 16)
            act.wait_ge(s_zero, 1)
            act.wait_ge(s_const, 16)
            with act.Fori(0, DEPTH) as l:
                for s in order:
                    k = s[0]
                    if k == "norm":
                        n = s[1]
                        if n <= ST_:
                            act.wait_ge(x_in[n], 16)
                        else:
                            wait(act, mem_loaded[n - NT - 1], n)
                        src = xs[:, n, :] if n <= ST_ else work[:, n % 4, :]
                        nc.scalar.activation(psS[:, 0, :], src, ACT.Square, accum_out=rstd[:, 0, n:n + 1]
                                             ).then_inc(squares.sem, 1)
                        act.wait_ge(squares.sem, squares.at(n))
                        nc.scalar.activation(rstd[:, 1, n:n + 1], rstd[:, 0, n:n + 1], ACT.Sqrt,
                                             scale=1.0 / D, bias=con[:, NCONST:NCONST + 1]).then_inc(rooted.sem, 1)
                    elif k == "turn":
                        n = s[1]
                        u = (s, 0)
                        wait(act, T.fill(u), u)
                        src = T.ap(u)[:, :].rearrange("p (b c) -> p b c", b=4)
                        if n < 9:
                            dst = hT[:, 0:4, n * P:(n + 1) * P]
                        else:
                            dst = gate[:, :, :].rearrange("p a b -> p (a b)")[:, 0:4 * MEM].rearrange(
                                "p (k c) -> p k c", k=4)[:, :, (n - 9) * P:(n - 8) * P]
                        nc.scalar.copy(dst, src).then_inc(T.empty(u).sem, 1)
                        act.drain().then_inc(h_act.sem, 1)
                    elif k == "P" and s[1][0] != "O":
                        c, t = s[1:]
                        n = units.index((c, t))
                        sl = slot_of[(c, t)]
                        sg = stage[:, sl, :]
                        if n >= 2:
                            pu = units[n - 2]
                            if ("TR",) + pu in T.slot:
                                wait(act, T.fill(("TR",) + pu), ("TR",) + pu)
                            if pu in worked.upto:
                                wait(act, worked, pu)
                        st = stored[sl]
                        prior = [u for u in units[:n] if slot_of[u] == sl and u in st.upto]
                        if prior:
                            wait(act, st, prior[-1])
                        wait(act, X.fill(s), s)
                        x = X.ap(s)
                        if c == "mm":
                            nc.scalar.copy(mV[:, t, :], x[:, W:2 * W])
                            nc.scalar.copy(sg[:, 0:W], x[:, 0:W]).then_inc(X.empty(s).sem, 1)
                        elif c == "A1":
                            nc.scalar.copy(sg[:, 0:456], x[:, 0:456]).then_inc(X.empty(s).sem, 1)
                        elif c in ("B1", "C1"):
                            nc.scalar.copy(sg, x).then_inc(X.empty(s).sem, 1)
                        else:
                            prev = {"B2": None, "C2": "B", "M1": "C", "A2": "M"}[c]
                            if prev:
                                wait(act, o_stored[t], prev)
                            elif t == ST_:
                                wait(act, X.fill(("P", "mm", 1)), ("P", "mm", 1))
                                act.wait_ge(v_stored.sem, v_stored.at(("mm", 1)))
                            if c == "C2" and t in (ST_, 0):
                                use = ("V", (last_sample if t == ST_ else last_prompt)["B"])
                                wait(act, X.fill(use), use)
                                wait(act, v_stored, ("B2", NT - 1))
                            if c in ("B2", "C2"):
                                nc.scalar.copy(vX[:, t, :], x[:, 0:W])
                            else:
                                nc.scalar.copy(sg[:, 0:W], x[:, 0:W])
                            nc.scalar.activation(sg[:, W:2 * W], x[:, W:2 * W], ACT.Tanh, scale=0.5)
                            nc.scalar.mul(gate[:, t, :], x[:, W:2 * W], 0.5).then_inc(X.empty(s).sem, 1)
                        act.drain().then_inc(staged.sem, 1)
                    elif k == "TR" and s in T.slot:
                        c, t = s[1:]
                        wait(act, T.fill(s), s)
                        if c[0] in BRANCHES and t in (ST_, 0) and c != "A1":
                            prev = before[c[0]]
                            use = ("is", PAIRS - 1) if not prev else ("S", (last_sample if t == ST_ else last_prompt)[prev])
                            wait(act, S.fill(use), use)
                            if t == ST_:
                                wait(act, qs_ready, use)
                        tp = T.ap(s)
                        cols = slice(t * P, (t + 1) * P)
                        if c == "mm":
                            nc.scalar.copy(mK[:, :, cols], tp[:, 0:W].rearrange("p (g c) -> p g c", g=2)
                                           ).then_inc(T.empty(s).sem, 1)
                        else:
                            for hp in range(2):
                                half = slice(64 * hp, 64 * hp + 64)
                                last = nc.scalar.mul(qT[half, hp:H:2, cols], tp[half, 0:W].rearrange("p (g c) -> p g c", g=2), 0.125)
                            if c in ("B1", "C1"):
                                last = nc.scalar.copy(kT[:, :, cols], tp[:, W:2 * W].rearrange("p (g c) -> p g c", g=2))
                            if c == "A1":
                                for src in range(2):
                                    for dst in range(2):
                                        last = nc.scalar.copy(kA[64 * dst:64 * dst + 64, src, cols],
                                                              tp[64 * src:64 * src + 64, W:W + P])
                            last.then_inc(T.empty(s).sem, 1)
                        act.drain().then_inc(turned.sem, 1)
                    elif k == "F":
                        wait(act, f_dve, "z")
                        nc.scalar.activation(lf[:, 1, :], lf[:, 1, :], ACT.Exp, scale=-1.0).then_inc(f_ready.sem, 1)
                        act.wait_ge(f_ready.sem, f_ready.at("exp"))
                        nc.scalar.activation(lf[:, 1, :], lf[:, 1, :], ACT.Ln, bias=1.0).then_inc(f_ready.sem, 1)
                    elif k in ("ip", "is"):
                        n = n_work[s]
                        L = (s[1] + 1) * P if k == "ip" else SKEYS
                        wait(act, S.fill(s), s)
                        if n >= 2:
                            pv = [x for x in n_work if n_work[x] == n - 2][0]
                            if pv[0] == "ip":
                                wait(act, scored, pv)
                            else:
                                wait(act, S.fill(("iw", pv[1])), ("iw", pv[1]))
                        else:
                            wait(act, T.fill((("turn", 10), 1)), (("turn", 10), 1))
                        nc.scalar.activation(buf(n)[:, 0:L], S.ap(s)[:, 0:L], ACT.Relu).then_inc(S.empty(s).sem, 1)
                        act.drain().then_inc(relued.sem, 1)
                    elif k == "S":
                        x_ = s[1]
                        L = blocks(x_) * P
                        n = n_item[x_]
                        wait(act, maxes, x_)
                        p = buf(n)[:, 0:L]
                        if n >= 4:
                            wait(act, rsum, items[n - 4])
                        nc.scalar.activation(p, p, ACT.Exp, bias=stat[:, n % 4, 1:2], accum_out=stat[:, n % 4, 2:3]
                                             ).then_inc(probs.sem, 1)
                    elif k == "T":
                        x_ = s[1]
                        n, u = n_item[x_], (s, 0)
                        w = min(4, blocks(x_)) * P
                        wait(act, T.fill(u), u)
                        if n >= 2:
                            pr = items[n - 2]
                            q = ("R", pr) if is_sample(pr) else ("V", pr)
                            wait(act, X.fill(q), q)
                        nc.scalar.copy(turned_buf(n)[:, 0:w], T.ap(u)[:, 0:w]).then_inc(T.empty(u).sem, 1)
                        if blocks(x_) > 4:
                            u, w = (s, 1), (blocks(x_) - 4) * P
                            wait(act, T.fill(u), u)
                            nc.scalar.copy(turned_buf(n)[:, 4 * P:4 * P + w], T.ap(u)[:, 0:w]).then_inc(T.empty(u).sem, 1)
                        act.drain().then_inc(pt_act.sem, 1)
                    elif k == "OT" or k == "OA":
                        t = s[1]
                        if k == "OT":
                            g = s[2]
                            wait(act, T.fill(s), s)
                            nc.scalar.copy(hT[:, 2 + 3 * g:5 + 3 * g, t * P:(t + 1) * P],
                                           T.ap(s)[:, 0:3 * P].rearrange("p (b c) -> p b c", b=3)).then_inc(T.empty(s).sem, 1)
                        else:
                            wait(act, T.fill(s), s)
                            nc.scalar.copy(hT[:, 0:2, t * P:(t + 1) * P], T.ap(s)[:, 0:2 * P].rearrange("p (b c) -> p b c", b=2)
                                           ).then_inc(T.empty(s).sem, 1)
                        act.drain().then_inc(merged.sem, 1)
                next_layer(act, "scalar")
            for t in TILES:
                nc.scalar.activation(psS[:, 0, :], xs[:, t, :], ACT.Square, accum_out=rstd[:, 0, t:t + 1]).then_inc(fin_sq, 1)
                act.wait_ge(fin_sq, t + 1)
                nc.scalar.activation(rstd[:, 1, t:t + 1], rstd[:, 0, t:t + 1], ACT.Sqrt, scale=1.0 / D,
                                     bias=con[:, NCONST:NCONST + 1]).then_inc(fin_root, 1)

        @block.vector
        def _(dve):
            v = nc.vector
            v.memset(qT[:, :, :], 0.0)
            v.memset(qs[:, :, :], 0.0)
            v.memset(credit[:, :], 0.0).then_inc(s_zero, 1)
            dve.wait_ge(s_zero, 1)
            dve.wait_ge(s_const, 16)

            def rotate(sg, heads, t):
                a = sg[:, 0:heads * HD].rearrange("p (h d) -> p h d", h=heads)
                x1, x2 = a[:, :, 0:ROT], a[:, :, ROT:2 * ROT]
                co = con[:, C_ROPE + 16 * t:C_ROPE + 16 * t + 8].unsqueeze(1).to_broadcast([P, heads, ROT])
                si = con[:, C_ROPE + 16 * t + 8:C_ROPE + 16 * t + 16].unsqueeze(1).to_broadcast([P, heads, ROT])
                u1 = rtmp[:, 0, 0:heads * ROT].rearrange("p (h d) -> p h d", h=heads)
                u2 = rtmp[:, 1, 0:heads * ROT].rearrange("p (h d) -> p h d", h=heads)
                v.tensor_tensor(u1, x1, si, ALU.mult)
                v.tensor_tensor(u2, x2, si, ALU.mult)
                v.tensor_tensor(x1, x1, co, ALU.mult)
                v.tensor_tensor(x2, x2, co, ALU.mult)
                dve.drain()
                v.tensor_tensor(x1, x1, u2, ALU.subtract)
                return v.tensor_tensor(x2, x2, u1, ALU.add)

            with dve.Fori(0, DEPTH) as l:
                for units_ in (S, T, X):
                    for q in units_.emptied:
                        dve.drain().then_inc(q.sem, 1)
                for s in order:
                    k = s[0]
                    if k == "norm":
                        n = s[1]
                        wait(dve, rooted, n)
                        if n == 0:
                            wait(dve, gain_loaded, "g")
                        if n == ST_ + 1:
                            wait(dve, small_loaded, "g")
                        if n >= 4:
                            wait(dve, T.fill((("turn", n - 4), 1)), (("turn", n - 4), 1))
                        v.reciprocal(rstd[:, 2, n:n + 1], rstd[:, 1, n:n + 1])
                        dve.drain()
                        src = xs[:, n, :] if n <= ST_ else work[:, n % 4, :]
                        v.scalar_tensor_tensor(out=work[:, n % 4, :], in0=src, scalar=rstd[:, 2, n:n + 1],
                                               in1=gains[:, int(n >= 9), :], op0=ALU.mult, op1=ALU.mult).then_inc(normed.sem, 1)
                    elif k == "turn":
                        n = s[1]
                        u = (s, 1)
                        wait(dve, T.fill(u), u)
                        src = T.ap(u)[:, :].rearrange("p (b c) -> p b c", b=4)
                        if n < 9:
                            dst = hT[:, 4:8, n * P:(n + 1) * P]
                        else:
                            dst = gate[:, :, :].rearrange("p a b -> p (a b)")[:, 4 * MEM:8 * MEM].rearrange(
                                "p (k c) -> p k c", k=4)[:, :, (n - 9) * P:(n - 8) * P]
                        v.tensor_copy(dst, src).then_inc(T.empty(u).sem, 1)
                        dve.drain().then_inc(h_dve.sem, 1)
                    elif k == "P" and (s[1], s[2]) in worked.upto:
                        c, t = s[1:]
                        wait(dve, staged, (c, t))
                        sg = stage[:, slot_of[(c, t)], :]
                        if c == "A1":
                            if t == 0:
                                wait(dve, small_loaded, "g")
                            rotate(sg, 6, t)
                            v.tensor_copy(vA[:, t, :], sg[:, 384:448])
                            v.tensor_scalar(wi[:, t, :], sg[:, 448:452], H ** -0.5, None, ALU.mult)
                            v.tensor_tensor(lf[:, 0, t * H:(t + 1) * H], sg[:, 452:456], bfb[:, :], ALU.add)
                        else:
                            if c == "A2":
                                rotate(sg, 4, t)
                            v.scalar_tensor_tensor(out=gate[:, t, :], in0=sg[:, W:2 * W], scalar=1.0, in1=gate[:, t, :],
                                                   op0=ALU.add, op1=ALU.mult)
                        dve.drain().then_inc(worked.sem, 1)
                    elif k == "P" and s[1][0] == "O":
                        c, t = s[1:]
                        n = outs.index((c, t))
                        wait(dve, X.fill(s), s)
                        wait(dve, res_loaded[n % 4], (c, t))
                        h = 512 * int(c[1])
                        v.tensor_tensor(xs[:, t, h:h + 512], X.ap(s), work[:, n % 4, 0:512], ALU.add
                                        ).then_inc(X.empty(s).sem, 1)
                        dve.drain().then_inc(res_added.sem, 1)
                    elif k == "F":
                        z, e, m = lf[:, 0, :], lf[:, 1, :], lf[:, 2, :]
                        v.scalar_tensor_tensor(out=e, in0=z, scalar=-1.0, in1=z, op0=ALU.mult, op1=ALU.max)
                        v.tensor_scalar(m, z, 0.0, None, ALU.min)
                        dve.drain().then_inc(f_dve.sem, 1)
                        wait(dve, f_ready, "ln")
                        v.tensor_tensor(z, m, e, ALU.subtract)
                        dve.drain().then_inc(f_dve.sem, 1)
                    elif k == "ip":
                        _, t, h = s
                        L = (t + 1) * P
                        dst = sc[:, SC_OFF[t]:SC_OFF[t] + L]
                        wait(dve, relued, s)
                        r = buf(n_work[s])[:, 0:L]
                        if (t, h) == (SEL_TILES[0], 0):
                            dve.wait_ge(lines_sem, 32)
                            wait(dve, x_saved, "x")
                        if h == 0:
                            v.tensor_scalar(dst, r, wi[:, t, 0:1], None, ALU.mult)
                        else:
                            v.scalar_tensor_tensor(out=dst, in0=r, scalar=wi[:, t, h:h + 1], in1=dst, op0=ALU.mult, op1=ALU.add)
                        dve.drain().then_inc(scored.sem, 1)
                        if h == H - 1:
                            v.tensor_tensor(dst[:, L - P:L], dst[:, L - P:L], con[:, C_CM + P:C_CM + 2 * P], ALU.add)
                            dve.drain()
                    elif k == "wrow":
                        wait(dve, f_dma, "rows")
                        frow, fsam = work[0:4, 2, :], work[0:32, 3, :]
                        v.tensor_tensor_scan(frow, frow, frow, 0.0, ALU.add, ALU.bypass)
                        v.tensor_tensor_scan(fsam[:, 0:PAST + STEPS], fsam[:, 0:PAST + STEPS], fsam[:, 0:PAST + STEPS], 0.0,
                                             ALU.add, ALU.bypass)
                        dve.drain().then_inc(f_dve.sem, 1)
                        v.tensor_copy(fsam[:, PAST + STEPS:SKEYS].rearrange("p (b i) -> p b i", i=STEPS),
                                      fsam[:, PAST:PAST + STEPS].unsqueeze(1).to_broadcast([32, 7, STEPS]))
                        dve.drain().then_inc(f_dve.sem, 1)
                        wait(dve, X.fill(s), s)
                        for j in range(PAIRS):
                            v.tensor_tensor_reduce(wrow[:, 4:8], X.ap(s)[:, 4 * j:4 * j + 4], con[:, C_HM:C_HM + 4], 1.0, 0.0,
                                                   ALU.mult, ALU.add, wrow[:, j:j + 1])
                            dve.drain()
                        dve.drain().then_inc(X.empty(s).sem, 1)
                        for j in range(PAIRS):
                            v.tensor_scalar(wsel[:, j, :], con[:, C_SEL:C_SEL + 32], wrow[:, j:j + 1], None, ALU.mult)
                        dve.drain().then_inc(scored.sem, 1)
                    elif k == "iw":
                        j = s[1]
                        wait(dve, S.fill(s), s)
                        if j == 0:
                            wait(dve, tmask, "m")
                            v.memset(sc[:, SC_OFF[ST_] + SKEYS:SC_W], 1e30)
                        r0 = slice(32 * j, 32 * j + 32)
                        dst = sc[r0, SC_OFF[ST_]:SC_OFF[ST_] + SKEYS]
                        v.tensor_copy(dst[:, 0:PAST], S.ap(s)[r0, 0:PAST])
                        v.tensor_tensor(dst[:, PAST:SKEYS], S.ap(s)[r0, PAST:SKEYS], dst[:, PAST:SKEYS], ALU.add
                                        ).then_inc(S.empty(s).sem, 1)
                        dve.drain().then_inc(scored.sem, 1)
                    elif k == "K":
                        rows_ = []
                        for t, i, end in s[1]:
                            L = SKEYS + FILL if t == ST_ else (t + 1) * P
                            rows_.append((sc[:, SC_OFF[t]:SC_OFF[t] + L], end, t))
                        for n, (a, end, t) in enumerate(rows_):
                            v.max(top8[:, n, :], a)
                        dve.drain()
                        for n, (a, end, t) in enumerate(rows_):
                            v.match_replace(a, top8[:, n, :], a, TAKEN)
                        dve.drain()
                        for n, (a, end, t) in enumerate(rows_):
                            if end:
                                v.tensor_scalar(a, a, 0.5 * TAKEN, NEG, ALU.is_ge, ALU.mult)
                                dve.drain().then_inc(selected.sem, 1)
                    elif k == "S":
                        x_ = s[1]
                        br, h, t = x_
                        n = n_item[x_]
                        L = blocks(x_) * P
                        wait(dve, S.fill(s), s)
                        src, dst = S.ap(s)[:, 0:L], buf(n)[:, 0:L]
                        mx, nm = stat[:, n % 4, 0:1], stat[:, n % 4, 1:2]
                        if n >= 2:
                            pr = items[n - 2]
                            g = (blocks(pr) + 3) // 4 - 1
                            wait(dve, T.fill((("T", pr), g)), (("T", pr), g))
                            wait(dve, probs, pr)
                        if n < 2:
                            wait(dve, S.fill(("iw", PAIRS - 1)), ("iw", PAIRS - 1))
                            wait(dve, f_dma, "out")
                        if br == "B" or br == "C":
                            if not is_sample(x_):
                                if br == "B":
                                    if early(x_):
                                        wait(dve, halves_loaded, "B")
                                        b_ = halves[:, h, 0:L]
                                    else:
                                        m = b_items.index(x_)
                                        wait(dve, pbias[m % 2], x_)
                                        b_ = gains[:, m % 2, 0:L]
                                else:
                                    if (h, t) == (0, 0):
                                        wait(dve, strips_loaded, "C")
                                        cm = con[:, C_CM + P:C_CM + 2 * P].unsqueeze(1).to_broadcast([P, H, P])
                                        v.tensor_tensor(strips[:, :, 4 * P:5 * P], strips[:, :, 4 * P:5 * P], cm, ALU.add)
                                        v.tensor_scalar(strips[64:128, :, 0:64], strips[64:128, :, 0:64], NEG, None, ALU.add)
                                        dve.drain()
                                    b_ = strips[:, h, 5 * P - L:5 * P]
                            else:
                                if br == "B" or h == 0:
                                    wait(dve, sbias, (br, h))
                                if br == "C" and h == 0:
                                    v.tensor_copy(sbias_[:, PAST + STEPS:SKEYS].rearrange("p (b i) -> p b i", i=STEPS),
                                                  sbias_[:, PAST:PAST + STEPS].unsqueeze(1).to_broadcast([P, 7, STEPS]))
                                    dve.drain()
                                b_ = sbias_[:, 0:L]
                            last = v.tensor_tensor_reduce(dst, src, b_, 1.0, NEG, ALU.subtract if br == "B" else ALU.add,
                                                          ALU.max, mx)
                        elif br == "A" and not is_sample(x_):
                            if t in SEL_TILES:
                                b_ = sc[:, SC_OFF[t]:SC_OFF[t] + L]
                            else:
                                b_ = con[:, C_CM + 2 * P - L:C_CM + 2 * P]
                            last = v.tensor_tensor_reduce(dst, src, b_, 1.0, NEG, ALU.add, ALU.max, mx)
                        else:
                            last = v.tensor_scalar(dst, src, 0.0, None, ALU.add, ALU.max, accum_out=mx)
                        last.then_inc(S.empty(s).sem, 1)
                        dve.drain().then_inc(logits.sem, 1)
                        v.tensor_scalar(nm, mx, -1.0, None, ALU.mult).then_inc(maxes.sem, 1)
                    elif k == "V":
                        x_ = s[1]
                        br, h, t = x_
                        n = n_item[x_]
                        wait(dve, probs, x_)
                        v.reciprocal(stat[:, n % 4, 3:4], stat[:, n % 4, 2:3]).then_inc(rsum.sem, 1)
                        dve.drain()
                        wait(dve, X.fill(s), s)
                        ri = stat[:, n % 4, 3:4]
                        if is_sample(x_):
                            o = X.ap(s)[:, 0:W].rearrange("p (h d) -> p h d", h=H)
                            if br == "A":
                                o = X.ap(s)[:, 0:HD].unsqueeze(1).to_broadcast([P, H, HD])
                            v.scalar_tensor_tensor(out=turned_buf(n)[:, 0:W].rearrange("p (h d) -> p h d", h=H), in0=o, scalar=ri,
                                                   in1=con[:, C_HM:C_HM + 4].unsqueeze(2).to_broadcast([P, H, HD]),
                                                   op0=ALU.mult, op1=ALU.mult).then_inc(X.empty(s).sem, 1)
                            dve.drain().then_inc(om_ready.sem, 1)
                        else:
                            g = gate[:, t, h * HD:(h + 1) * HD]
                            v.scalar_tensor_tensor(out=g, in0=X.ap(s)[:, 0:HD], scalar=ri, in1=g, op0=ALU.mult, op1=ALU.mult
                                                   ).then_inc(X.empty(s).sem, 1)
                            dve.drain().then_inc(gated.sem, 1)
                    elif k == "R":
                        j = s[1][1]
                        wait(dve, X.fill(s), s)
                        r0 = slice(32 * j, 32 * j + 32)
                        v.tensor_tensor(gate[r0, ST_, :], X.ap(s)[r0, 0:W], gate[r0, ST_, :], ALU.mult).then_inc(X.empty(s).sem, 1)
                        dve.drain().then_inc(gated.sem, 1)
                next_layer(dve, "vector")
            dve.wait_ge(fin_gain, 16)
            for t in TILES:
                dve.wait_ge(fin_root, t + 1)
                v.reciprocal(rstd[:, 2, t:t + 1], rstd[:, 1, t:t + 1])
                dve.drain()
                v.scalar_tensor_tensor(out=xs[:, t, :], in0=xs[:, t, :], scalar=rstd[:, 2, t:t + 1],
                                       in1=gains[:, 0, :], op0=ALU.mult, op1=ALU.mult).then_inc(fin_done, 1)

        @block.gpsimd
        def _(pool):
            g = nc.gpsimd
            pool.wait_ge(s_zero, 1)
            pool.wait_ge(s_const, 16)

            def store(dst, src, sem_, **kw):
                pool.dma_start(dst, src, **kw).then_inc(sem_, 16)

            with pool.Fori(0, DEPTH) as l:
                def out_rows(name, t):
                    if t == ST_:
                        return rows(d["s" + name], l, P, 0, P)
                    return rows(d["p" + name], l, SEQ, t * P, P)

                line = sc[0:H, 4 * D:4 * D + XL]
                pool.dma_start(line[:, XL - 256:XL], d["cb"][bass.ds(l * H, H), 0:256]).then_inc(lines_sem, 16)
                pool.wait_ge(lines_sem, 16)
                g.tensor_copy(line[:, 0:XL - 256], line[:, XL - 256:XL - 255].to_broadcast([H, XL - 256]))
                pool.drain()
                pool.dma_start(d["xl"], line).then_inc(lines_sem, 16)
                pool.wait_ge(lines_sem, 32)
                for h in range(H):
                    pool.dma_start(d["xr"][h * P:(h + 1) * P, :], d["xl"][h:h + 1, :].to_broadcast([P, XL])
                                   ).then_inc(lines_sem, 16)
                def prompt_bias(m):
                    _, h, t = b_items[m]
                    L = (t + 1) * P
                    pool.dma_start(gains[:, m % 2, 0:L], d["fp"][h:h + 1, 0:L].to_broadcast([P, L])).then_inc(pbias[m % 2].sem, 16)

                def sample_bias(br, j):
                    for r in range(2):
                        if br == "B":
                            src = bass.AP(d["fs"].tensor, (2 * j + r) * SKEYS, [[R * SKEYS, H], [0, STEPS], [1, SKEYS]])
                        else:
                            src = bass.AP(d["xr"].tensor, P - 1, [[P * XL, H], [XL - 1, STEPS], [1, PAST + STEPS]])
                        pool.dma_start(sbias_[64 * r:64 * r + 64, 0:src.shape[-1]], src).then_inc(sbias.sem, 16)

                for s in order:
                    k = s[0]
                    if k == "P" and s[1][0] != "O":
                        c, t = s[1:]
                        sg = stage[:, slot_of[(c, t)], :]
                        done = stored[slot_of[(c, t)]].sem
                        if (c, t) == ("B1", ST_):
                            wait(pool, normed, NORMS - 1)
                            wait(pool, f_dma, "out")
                            src = bass.AP(d["fp"].tensor, 0, [[0, P], [SEQ, H], [1, SEQ // 2]])
                            pool.dma_start(halves, src).then_inc(halves_loaded.sem, 16)
                            sample_bias("B", 0)
                        if c == "mm":
                            wait(pool, staged, (c, t))
                            store(rows(d["pm_k"], l, MEM, t * P, P), sg[:, 0:W], done)
                            store(rows(d["pm_v"], l, MEM, t * P, P), mV[:, t, :], v_stored.sem)
                        elif c == "A1":
                            wait(pool, worked, (c, t))
                            store(out_rows("a_ki", t), sg[:, 256:320], done)
                            store(out_rows("a_k", t), sg[:, 320:384], done)
                            store(out_rows("a_v", t), sg[:, 384:448], done)
                            if t == ST_:
                                for j in range(PAIRS):
                                    last = g.tensor_scalar(wmask[:, 4 * j:4 * j + 4], wi[:, ST_, :], con[:, C_PM + j:C_PM + j + 1],
                                                           None, ALU.mult)
                                last.then_inc(wmask_ready.sem, 1)
                        elif c in ("B1", "C1"):
                            if c == "B1" or t >= 4:
                                wait(pool, staged, (c, t))
                                if c == "B1":
                                    store(out_rows("b_k", t), sg[:, W:2 * W], done)
                                elif t == ST_:
                                    store(out_rows("c_k", t), sg[:, W:2 * W], done)
                                else:
                                    store(rows(d["pc_k"], l, 512, (t - 4) * P, P), sg[:, W:2 * W], done)
                        elif c in ("B2", "C2"):
                            if c == "B2" or t >= 4:
                                wait(pool, staged, (c, t))
                                if c == "B2":
                                    store(out_rows("b_v", t), vX[:, t, :], v_stored.sem)
                                elif t == ST_:
                                    store(out_rows("c_v", t), vX[:, t, :], v_stored.sem)
                                else:
                                    store(rows(d["pc_v"], l, 512, (t - 4) * P, P), vX[:, t, :], v_stored.sem)
                    elif k == "F":
                        wait(pool, f_dve, "lf")
                        z = lf[:, 0, :].rearrange("p (t h) -> p t h", h=H)
                        store(rows(d["pb_lf"], l, SEQ, 0, SEQ).rearrange("(t p) h -> p t h", p=P), z[:, 0:8, :], f_dma.sem)
                        store(rows(d["sb_lf"], l, P, 0, P), z[:, 8, :], f_dma.sem)
                        store(d["lfnat"].rearrange("(t p) h -> p t h", p=P), z, f_dma.sem)
                        wait(pool, f_dma, "nat")
                        wait(pool, T.fill((("turn", 10), 1)), (("turn", 10), 1))
                        for h in range(H):
                            store(work[h:h + 1, 2, :], d["lfnat"][0:SEQ, h:h + 1].rearrange("s h -> h s"), f_dma.sem,
                                  allow_slow_non_contiguous=True)
                        store(work[0:32, 3, 0:PAST], rows(d["blf"], l, 32, 0, 32), f_dma.sem)
                        for h in range(H):
                            store(work[8 * h:8 * h + 8, 3, PAST:PAST + STEPS],
                                  d["lfnat"][SEQ:TOK, :].rearrange("(r i) h -> h r i", i=STEPS)[h], f_dma.sem,
                                  allow_slow_non_contiguous=True)
                    elif k == "wrow":
                        wait(pool, f_dve, "spread")
                        store(d["fp"], work[0:4, 2, :], f_dma.sem)
                        store(d["fs"], work[0:32, 3, 0:SKEYS], f_dma.sem)
                    elif k == "is":
                        j = s[1]
                        if j == 0:
                            wait(pool, turned, ("A1", 8))
                        else:
                            wait(pool, S.fill(("is", j - 1)), ("is", j - 1))
                        last = g.tensor_copy(qsA[:, :].rearrange("p (r h i) -> p r h i", r=2, h=H),
                                             qT[:, :, SEQ + 32 * j:SEQ + 32 * j + 32].rearrange("p h (r i) -> p r h i", r=2))
                        last.then_inc(qs_ready.sem, 1)
                    elif k == "Q":
                        x_ = s[1]
                        br, j, t = x_
                        if j == 0:
                            wait(pool, turned, ({"A": "A2", "M": "M1"}.get(br, br + "1"), ST_))
                        prs = [y for y in items[:n_item[x_]] if is_sample(y)]
                        if prs:
                            wait(pool, S.fill(("S", prs[-1])), ("S", prs[-1]))
                        src = qT[:, :, SEQ + 32 * j:SEQ + 32 * j + 32].rearrange("p h (r i) -> p r h i", r=2)
                        if br == "A":
                            if j == 0:
                                wait(pool, S.fill(("is", PAIRS - 1)), ("is", PAIRS - 1))
                            g.tensor_scalar(selj[:, :], con[:, C_SELT:C_SELT + P], con[:, C_PM + j:C_PM + j + 1], None,
                                            ALU.mult).then_inc(selj_ready.sem, 1)
                            last = g.tensor_copy(qsA[:, :].rearrange("p (r h i) -> p r h i", r=2, h=H), src)
                        else:
                            if br == "B" and j == 0:
                                wait(pool, S.fill(("is", PAIRS - 1)), ("is", PAIRS - 1))
                                g.memset(qs[:, :, :], 0.0)
                                pool.drain()
                            for gg in range(2):
                                dst = qs[:, gg, :].rearrange("p (r h i) -> p r h i", r=2, h=H)[:, :, 2 * gg:2 * gg + 2, :]
                                last = g.tensor_copy(dst, src[:, :, 2 * gg:2 * gg + 2, :])
                        last.then_inc(qs_ready.sem, 1)
                    elif k == "S":
                        x_ = s[1]
                        br, h, t = x_
                        if br == "B" and (is_sample(x_) or x_ == last_early or not early(x_)):
                            wait(pool, logits, x_)
                            if is_sample(x_):
                                if h == PAIRS - 1:
                                    pool.wait_ge(lines_sem, 96)
                                sample_bias(*sbias_loads[h + 1])
                            elif x_ == last_early:
                                prompt_bias(0)
                                prompt_bias(1)
                            elif b_items.index(x_) + 2 < len(b_items):
                                prompt_bias(b_items.index(x_) + 2)
                            elif x_ == b_items[-1]:
                                src = bass.AP(d["xr"].tensor, P - 1, [[XL - 1, P], [P * XL, H], [1, 5 * P]])
                                pool.dma_start(strips, src).then_inc(strips_loaded.sem, 16)
                    elif s[0] in "VR" and s[1][0] != "A" and s[1][1] == H - 1 and is_sample(s[1]) == (k == "R"):
                        br, _, t = s[1]
                        wait(pool, gated, s[1])
                        t = ST_ if k == "R" else t
                        store(d["oscr"][t * P:(t + 1) * P, GCOL[br] - W:GCOL[br]], gate[:, t, :], o_stored[t].sem)
                for q in stored + [v_stored, f_dma, halves_loaded, strips_loaded, sbias] + pbias + o_stored:
                    pool.wait_ge(q.sem, q.layer)
                pool.wait_ge(lines_sem, 96)
                pool.wait_ge(layer_over, 4)
                pool.dma_reset(layer_sems)
                pool.sem_clear(layer_sems)
                for q in go.values():
                    pool.sem_inc(q, 1)


def constants():
    con = np.zeros((P, NCONST + 1), np.float32)
    p = np.arange(P)
    con[:, C_ID:C_ID + P] = np.eye(P)
    con[:, C_TRI:C_TRI + P] = np.where(p[None, :] <= p[:, None], 0, NEG)
    con[:, C_CM + P:C_CM + 2 * P] = np.where(p[None, :] // 64 <= p[:, None] // 64, 0, NEG)
    r, h, i = p // 64, p // STEPS % H, p % STEPS
    for base, causal in ((C_FULL, False), (C_CAUS, True)):
        w = np.full((P, 224), NEG, np.float32)
        for step in range(STEPS):
            ok = (step <= i) | (not causal)
            w[p[ok], 96 + STEPS * r[ok] + step] = 0
        con[:, base:base + 224] = w
    con[:, C_SELT:C_SELT + P] = (p[:, None] % 32 == (STEPS * r + i)[None, :])
    con[:, C_SEL:C_SEL + 32] = ((STEPS * r + i)[:, None] == np.arange(32)[None, :])
    con[:, C_PM:C_PM + 4] = (p[:, None] // 32 == np.arange(4)[None, :])
    con[:, C_HM:C_HM + 4] = (h[:, None] == np.arange(4)[None, :])
    inv = np.float32(500000.0) ** (-np.arange(ROT, dtype=np.float32) / np.float32(ROT))
    for t in TILES:
        pos = (t * P + p if t < NT else PAST + p % STEPS).astype(np.float32)
        ang = (pos[:, None] * inv[None, :].astype(np.float32)).astype(np.float32)
        con[:, C_ROPE + 16 * t:C_ROPE + 16 * t + 8] = np.cos(ang.astype(np.float64))
        con[:, C_ROPE + 16 * t + 8:C_ROPE + 16 * t + 16] = np.sin(ang.astype(np.float64))
    con[:, NCONST] = EPS
    tmask = np.where(p[:, None] // STEPS == p[None, :] // STEPS, 0, NEG).astype(np.float32)
    return con, tmask


def lay_out(x_prompt, x_sample, cache_a_k, cache_a_v, cache_a_kidx, cache_b_k, cache_b_v, cache_b_logf,
            cache_c_k, cache_c_v, cache_mem_k, cache_mem_v, mem_prompt, w_in, w_out, g_norm, b_f, c_bias,
            g_mem, w_mem_kv, g_final):
    a = np.ascontiguousarray
    off, cols = 0, {}
    for name, n in (("a_q", W), ("a_k", HD), ("a_v", HD), ("a_qi", W), ("a_ki", HD), ("a_wi", H), ("a_g", W), ("b_q", W),
                    ("b_k", W), ("b_v", W), ("b_f", H), ("b_g", W), ("c_q", W), ("c_k", W), ("c_v", W), ("c_g", W),
                    ("m_q", W), ("m_g", W)):
        cols[name] = w_in[:, :, off:off + n]
        off += n
    join = lambda *names: np.concatenate([cols[n] for n in names], -1)
    a1 = join("a_qi", "a_ki", "a_k", "a_v", "a_wi", "b_f")
    a1 = np.concatenate([a1, np.zeros(a1.shape[:2] + (512 - a1.shape[2],), a1.dtype)], -1)
    chunks = {"A1": a1, "mm": w_mem_kv, "B1": join("b_q", "b_k"), "B2": join("b_v", "b_g"), "C1": join("c_q", "c_k"),
              "C2": join("c_v", "c_g"), "M1": join("m_q", "m_g"), "A2": join("a_q", "a_g"),
              "O0": w_out[:, :, :512], "O1": w_out[:, :, 512:]}
    w = np.stack([chunks[c] for c in CHUNKS], 1)
    w = w.reshape(DEPTH, len(CHUNKS), KT, P, 512).transpose(0, 1, 3, 2, 4)
    shared_k = lambda c: a(c.reshape(DEPTH, PAIRS, 2, PAST, HD).transpose(0, 1, 4, 2, 3).reshape(-1, 2 * PAST))
    heads_k = lambda c: a(c.reshape(DEPTH, PAIRS, 2, -1, 2, 2, HD).transpose(0, 1, 5, 6, 2, 4, 3).reshape(
        DEPTH * PAIRS * P, -1))
    values = lambda c: a(c.reshape(DEPTH, PAIRS, 2, c.shape[2] // P, P, -1).transpose(0, 1, 4, 2, 3, 5).reshape(
        DEPTH * PAIRS * P, -1))
    con, tmask = constants()
    return {
        "x": a(np.concatenate([x_prompt.reshape(SEQ, D), x_sample.reshape(P, D)])),
        "mem": a(mem_prompt.reshape(MEM, D)),
        "w": a(w.reshape(-1, KT * 512)),
        "gain": a(np.concatenate([np.stack([g_norm, g_mem], 1).reshape(2 * DEPTH, D), g_final[None]])),
        "bf": a(b_f),
        "cb": a(c_bias[:, :, ::-1].reshape(DEPTH * H, -1)),
        "blf": a(cache_b_logf.transpose(0, 3, 1, 2).reshape(DEPTH * H * R, PAST)),
        "kI": shared_k(cache_a_kidx), "kA": shared_k(cache_a_k), "vA": values(cache_a_v),
        "kB": heads_k(cache_b_k), "vB": values(cache_b_v), "kC": heads_k(cache_c_k), "vC": values(cache_c_v),
        "kM": heads_k(cache_mem_k), "vM": values(cache_mem_v),
        "const": con, "tmask": tmask,
    }


_OUTS = {"y": (TOK, D), "pa_k": (DEPTH * SEQ, HD), "pa_v": (DEPTH * SEQ, HD), "pa_ki": (DEPTH * SEQ, HD),
         "pb_k": (DEPTH * SEQ, W), "pb_v": (DEPTH * SEQ, W), "pb_lf": (DEPTH * SEQ, H),
         "pc_k": (DEPTH * 512, W), "pc_v": (DEPTH * 512, W), "pm_k": (DEPTH * MEM, W), "pm_v": (DEPTH * MEM, W),
         "sa_k": (DEPTH * P, HD), "sa_v": (DEPTH * P, HD), "sa_ki": (DEPTH * P, HD),
         "sb_k": (DEPTH * P, W), "sb_v": (DEPTH * P, W), "sb_lf": (DEPTH * P, H),
         "sc_k": (DEPTH * P, W), "sc_v": (DEPTH * P, W)}
_SCRATCH = {"xres": (TOK, D), "oscr": (TOK, 3 * W), "lfnat": (TOK, H), "fp": (H, SEQ), "fs": (H * R, SKEYS), "xl": (H, XL), "xr": (H * P, XL)}


def kernel(**inputs):
    import concourse.bacc as bacc
    from concourse.bass_utils import run_bass_kernel_spmd

    arrays = lay_out(**{k: np.asarray(v) for k, v in inputs.items()})
    nc = bacc.Bacc("TRN2", target_bir_lowering=False, num_devices=1)
    d = {n: nc.dram_tensor(f"in_{n}", a.shape, F32, kind="ExternalInput").ap() for n, a in arrays.items()}
    d |= {n: nc.dram_tensor(f"out_{n}", s, F32, kind="ExternalOutput").ap() for n, s in _OUTS.items()}
    d |= {n: nc.dram_tensor(f"scratch_{n}", s, F32, kind="Internal").ap() for n, s in _SCRATCH.items()}
    encoder(nc, d)
    r = run_bass_kernel_spmd(nc, [{f"in_{n}": a for n, a in arrays.items()}], core_ids=[0]).results[0]
    o = {n: r[f"out_{n}"] for n in _OUTS}
    res = [o["y"][:SEQ].reshape(1, SEQ, D), o["y"][SEQ:].reshape(R, STEPS, D)]
    for n in list(_OUTS)[1:]:
        tail = (H, HD) if n[1] in "bcm" and n[-2:] != "lf" else (_OUTS[n][1],)
        lead = (DEPTH, 1, _OUTS[n][0] // DEPTH) if n[0] == "p" else (DEPTH, R, STEPS)
        res.append(o[n].reshape(lead + tail))
    return tuple(res)
```

```python
from contextlib import ExitStack

import numpy as np

import concourse.bass as bass
from concourse import mybir

F32 = mybir.dt.float32
ALU = mybir.AluOpType
ACT = mybir.ActivationFunctionType

P = 128
D = 1024
KT = D // P
SEQ = 1024
NT = SEQ // P
ST_ = NT
TILES = list(range(NT + 1))
TOK = SEQ + P
DEPTH = 2
NORMS = NT + 1 + 2
R, STEPS = 8, 16
PAIRS = R // 2
PAST = 512
H, HD = 4, 64
W = H * HD
MEM = 256
TOPK_P = min(256, SEQ // 4)
TOPK_S = min(256, (PAST + STEPS) // 4)
ROT = 8
EPS = 1e-6
NEG = -1.0e30
TAKEN = -3.0e38
SKEYS = PAST + P
CHUNKS = ["A1", "mm", "B1", "B2", "C1", "C2", "M1", "A2", "O0", "O1"]
BRANCHES = "BCMA"
UNITS = {"B": ["B1", "B2"], "C": ["C1", "C2"], "M": ["M1"], "A": ["A2"]}
RING = 5
AHEAD = 2
PHASES = ["B", "C", "MA"]
LAG = 2
SPARE_UNIT = {"B1": 7.0, "C1": 7.0, "A2": 5.6}
SPARE_OTHER = 5.8
SPARE_ITEM = [0.05, 1.0]
GCOL = {"A": 0, "B": W, "C": 2 * W, "M": 3 * W}
XL = 767

C_ID, C_TRI, C_CM, C_FULL, C_CAUS, C_SELT, C_SEL, C_PM, C_HM, C_ROPE = np.cumsum(
    [0, 128, 128, 256, 224, 224, 128, 32, 4, 4]).tolist()
NCONST = C_ROPE + 9 * 16

SEL_TILES = [t for t in range(NT) if (t + 1) * P > TOPK_P]
SC_OFF = {t: sum(u + 1 for u in SEL_TILES if u < t) * P for t in SEL_TILES + [ST_]}
FILL = -TOPK_S % 8
SC_W = SC_OFF[ST_] + SKEYS + FILL


def chunk_tiles(c):
    return [0, 1] if c == "mm" else TILES


def key_tiles(br, t):
    return {"A": range(t + 1), "B": range(t + 1), "C": range(max(0, t - 4), t + 1), "M": range(2)}[br]


def attention_items(br, t):
    j = t - (NT - PAIRS if br == "A" else 0)
    return [(br, h, t) for h in range(H)] + ([(br, j, f"s{j}")] if 0 <= j < PAIRS else [])


def is_sample(item):
    return isinstance(item[2], str)


def blocks(item):
    if is_sample(item):
        return 2 if item[0] == "M" else 5
    return len(key_tiles(item[0], item[2]))


def topk_rounds():
    out = []
    pairs = list(zip(SEL_TILES[0::2], SEL_TILES[1::2]))
    for pair in pairs[:2] + [(ST_,)] + pairs[2:]:
        n = (TOPK_S + FILL if pair == (ST_,) else TOPK_P) // 8
        out += [tuple((t, i, i == n - 1) for t in pair) for i in range(n)]
    return out


def layer_order():
    o = []
    rounds = topk_rounds()
    spare = [0.0]
    cost = lambda t: (2 * ((SKEYS + FILL if t == ST_ else (t + 1) * P) + 60) + 90) / 960
    pushed = []
    unit = [None]
    since = [0]

    def select(time):
        spare[0] += time
        while rounds and spare[0] > 0:
            x = rounds.pop(0)
            o.append(("K", x))
            spare[0] -= sum(cost(t) for t, _, _ in x)

    def push(item):
        n = len(pushed)
        pushed.append(item)
        at = lambda i: pushed[i] if i >= 0 else None
        if at(n - 2):
            o.append(("T", at(n - 2)))
        if item and item[0] == "A":
            strip = ST_ if is_sample(item) else item[2]
            while any(t == strip for x in rounds for t, _, _ in x):
                o.append(("K", rounds.pop(0)))
        if item:
            o.append(("S", item))
            if is_sample(item) and item[1] + 1 < PAIRS:
                o.append(("Q", (item[0], item[1] + 1, f"s{item[1] + 1}")))
            elif is_sample(item) and item[0] == "M":
                o.append(("Q", ("A", 0, "s0")))
            spare[0] += SPARE_ITEM[is_sample(item)] * (1 if is_sample(item) else blocks(item))
        if at(n - 3):
            o.append(("V", at(n - 3)))
        if at(n - 4) and is_sample(at(n - 4)):
            o.append(("R", at(n - 4)))

    def turn_last():
        if unit[0]:
            c, t = unit[0]
            o.append(("TR", c, t))
            if t == ST_ and c in ("C1", "M1"):
                o.append(("Q", (c[0], 0, "s0")))
            unit[0] = None

    def project(c, t):
        if o[-1][0] != "P" and since[0] < len(pushed):
            turn_last()
        since[0] = len(pushed)
        select(SPARE_UNIT.get(c, SPARE_OTHER))
        o.append(("P", c, t))
        turn_last()
        unit[0] = (c, t)

    o += [("norm", 0), ("norm", 1), ("turn", 0)]
    for n in TILES:
        o += [("norm", n + 2)] if n + 2 < NORMS else []
        o += [("turn", n + 1), ("P", "A1", n)]
        o += [("TR", "A1", n - 1)] if n else []
    o += [("turn", NORMS - 1), ("P", "mm", 0), ("TR", "A1", ST_), ("P", "mm", 1), ("TR", "mm", 0), ("TR", "mm", 1)]
    o.append(("F",))
    index = [("ip", t, h) for t in SEL_TILES for h in range(H)]
    o += index[:-H] + [("Q", 0), ("wrow",)] + index[-H:]
    for j in range(PAIRS):
        o.append(("is", j))
        if j + 1 < PAIRS:
            o.append(("Q", j + 1))
        if j:
            o.append(("iw", j - 1))
        if j < 2:
            o.append(("P", UNITS["B"][j], ST_))
    o += [("iw", PAIRS - 1), ("TR", "B1", ST_), ("Q", ("B", 0, "s0"))]
    queue = []

    def attend(keep):
        while len(queue) > keep:
            push(queue.pop(0))

    for phase in PHASES:
        chunks = [c for br in phase for c in UNITS[br]]
        for t in [ST_] + TILES[:NT]:
            if (phase, t) == ("B", ST_):
                continue
            if t == ST_:
                turn_last()
                attend(max(len(queue) // 2, 1))
            for n, c in enumerate(chunks):
                if n == 1 and (phase, t) in (("C", 0), ("MA", ST_)):
                    attend(0)
                    for _ in range(3):
                        push(None)
                project(c, t)
                if t == ST_:
                    attend(len(queue) // 2 if n == 0 else 0)
                else:
                    attend(LAG if n else (len(queue) + LAG) // 2)
            new = [attention_items(br, t) for br in phase] if t < NT else []
            while any(new):
                queue += [x.pop(0) for x in new if x]
    turn_last()
    others = [("OT", t, g) for t in TILES for g in range(2)]
    while queue or pushed[-4:] != [None] * 4:
        push(queue.pop(0) if queue else None)
        if others[0][1] < NT - 1:
            o.append(others.pop(0))
    o += others + [("OA", 0)]
    for t in TILES:
        o += [("OA", t + 1)] if t < ST_ else []
        o.append(("P", "O0", t))
    o += [("P", "O1", t) for t in TILES]
    return o


class Signal:

    def __init__(self, sem, events, worth=lambda e: 1, credit=0):
        self.sem, self.credit, self.upto = sem, credit, {}
        n = 0
        for e in events:
            assert e not in self.upto, e
            n += worth(e)
            self.upto[e] = n
        self.layer = n
        self.list = list(events)

    def at(self, event):
        return self.credit + self.upto[event]

    def before(self, n):
        return self.credit + (self.upto[self.list[n - 1]] if n else 0)


class Units:

    def __init__(self, sem, name, aps, uses):
        n = len(aps)
        self.aps, self.slot = aps, {u: i % n for i, u in enumerate(uses)}
        self.filled = [Signal(sem(f"{name}{k}_filled"), uses[k::n]) for k in range(n)]
        self.emptied = [Signal(sem(f"{name}{k}_emptied"), uses[k::n], credit=1) for k in range(n)]
        self.index = {u: i // n for i, u in enumerate(uses)}

    def ap(self, use):
        return self.aps[self.slot[use]]

    def fill(self, use):
        return self.filled[self.slot[use]]

    def empty(self, use):
        return self.emptied[self.slot[use]]

    def free(self, use):
        return self.empty(use).before(self.index[use])


def encoder(nc, d):
    order = layer_order()
    items = [s[1] for s in order if s[0] == "S"]
    with ExitStack() as ctx:
        def sb(name, *shape):
            return ctx.enter_context(nc.sbuf_tensor(name, [P] + list(shape), F32))

        def sem(name):
            return ctx.enter_context(nc.semaphore(name))

        hT = sb("hT", KT, TOK)
        wring = sb("wring", 2, KT * 512)
        qT = sb("qT", H, TOK)
        kA = sb("kA", 2, TOK)
        kv = sb("kv", H * TOK)
        kT = kv[:, 0:2 * TOK].rearrange("p (g c) -> p g c", g=2)
        vX = kv[:, 2 * TOK:].rearrange("p (t c) -> p t c", c=W)
        gain = kv[:, 0:D]
        qTA = kv[:, :].rearrange("p (h c) -> p h c", h=H)
        vA = sb("vA", 9, HD)
        gate = sb("gate", 9, W)
        bias = sb("bias", H * 5 * P + SKEYS)
        gateA = bias[:, 0:(NT + 1) * W].rearrange("p (t c) -> p t c", c=W)
        gains = bias[:, 0:2 * D].rearrange("p (n c) -> p n c", n=2)
        halves = bias[:, 0:2 * D].rearrange("p (h c) -> p h c", h=H)
        strips = bias[:, 0:H * 5 * P].rearrange("p (h c) -> p h c", h=H)
        sbias_ = bias[:, H * 5 * P:]
        shared = sb("shared", RING * D + SC_W)
        cache = shared[:, 0:RING * D].rearrange("p (n c) -> p n c", n=RING)
        sc = shared[:, RING * D:RING * D + SC_W]
        xs = shared[:, 0:(NT + 1) * D].rearrange("p (t c) -> p t c", c=D)
        work = sb("work", 4, 1024)
        stage = sb("stage", 2, 512)
        mK = sb("mK", 2, MEM)
        mV = sb("mV", 2, W)
        con = sb("con", NCONST + 1)
        qs = sb("qs", 2, P)
        qsA = qs[:, 0, :]
        selj = sb("selj", P)
        wsel = selj[:, :].rearrange("p (j q) -> p j q", j=PAIRS)
        wi = sb("wi", 9, H)
        lf = sb("lf", 3, 9 * H)
        rstd = sb("rstd", 3, NORMS)
        final = sb("final", 2, NT + 1)
        stat = sb("stat", 4, 4)
        top8 = sb("top8", 2, 8)
        wmask = sb("wmask", 16)
        wrow = sb("wrow", 8)
        rtmp = sb("rtmp", 2, 6 * ROT)
        bfb = sb("bfb", H)
        credit = sb("credit", 1)

        psS = ctx.enter_context(nc.psum_tensor("psS", [P, 2, 1024], F32))
        psT = ctx.enter_context(nc.psum_tensor("psT", [P, 2, 512], F32))
        psX = ctx.enter_context(nc.psum_tensor("psX", [P, 2, 512], F32))

        ident = con[:, C_ID:C_ID + P]

        s_const = sem("const_loaded")
        s_gain = sem("first_gain_loaded")
        s_summed, s_ahead, s_last = sem("first_squares_summed"), sem("first_roots_taken"), sem("last_root_taken")
        s_zero = sem("zeros_set")
        x_in = [sem(f"x{t}_loaded") for t in TILES]
        layer_first = x_in[-1].num + 1

        s_uses, t_uses, x_uses = [], [], []
        for s in order:
            k = s[0]
            if k == "P":
                x_uses.append(s)
            elif k == "TR" and s[1] in ("mm", "A1", "B1", "C1", "M1", "A2"):
                t_uses.append(s)
            elif k in ("turn", "ip", "is", "iw", "S"):
                s_uses.append(s)
            elif k == "wrow":
                x_uses.append(s)
            elif k == "T":
                t_uses += [(s, g) for g in range((blocks(s[1]) + 3) // 4)]
            elif k in ("V", "R"):
                x_uses.append(s)
            elif k in ("OT", "OA"):
                t_uses.append(s)
        S = Units(sem, "scores", [psS[:, k, :] for k in range(2)], s_uses)
        T = Units(sem, "turned", [psT[:, k, :] for k in range(2)], t_uses)
        X = Units(sem, "acc", [psX[:, k, :] for k in range(2)], x_uses)

        units = [s[1:] for s in order if s[0] == "P" and s[1][0] != "O"]
        slot_of = {u: n % 2 for n, u in enumerate(units)}
        stored_dmas = lambda u: {"mm": 1, "A1": 3, "B1": 1}.get(u[0], int(u[0] == "C1" and u[1] >= 4))
        norms = list(range(NORMS))
        mem_loaded = [Signal(sem(f"mem_loaded{k}"), [NT + 1 + k], lambda e: 16) for k in range(2)]
        x_saved = Signal(sem("x_saved"), ["x"], lambda e: 16 * len(TILES))
        gain_loaded = Signal(sem("gain_loaded"), ["g"], lambda e: 16)
        small_loaded = Signal(sem("small_loaded"), ["g"], lambda e: 32)
        squares = Signal(sem("squares_summed"), norms[AHEAD:])
        rooted = Signal(sem("root_taken"), norms[AHEAD:])
        normed = Signal(sem("tile_normed"), norms)
        w_loaded = [Signal(sem(f"w_loaded{k}"), CHUNKS[k::2], lambda e: 16) for k in range(2)]
        h_act = Signal(sem("hT_by_act"), norms)
        h_dve = Signal(sem("hT_by_dve"), norms)
        staged = Signal(sem("unit_staged"), units)
        worked = Signal(sem("unit_worked"), [u for u in units if u[0] in ("A1", "A2", "B2", "C2", "M1")])
        stored = [Signal(sem(f"stage{k}_stored"), [u for u in units if slot_of[u] == k and stored_dmas(u)],
                         lambda u: 16 * stored_dmas(u)) for k in range(2)]
        v_units = [(c, t) for c, t in units if c == "B2" or (c == "C2" and t >= 4)]
        v_stored = Signal(sem("v_stored"), [u for u in [("mm", 0), ("mm", 1)] + v_units], lambda e: 16)
        turned = Signal(sem("operand_turned"), [s[1:] for s in t_uses if s[0] == "TR"])
        f_ready = Signal(sem("f_stage"), ["exp", "ln"])
        f_dve = Signal(sem("f_vector"), ["z", "lf", "scan", "spread"])
        f_dma = Signal(sem("f_moved"), ["nat", "rows", "out"],
                       lambda e: {"nat": 48, "rows": 16 * 9, "out": 32}[e])
        wmask_ready = Signal(sem("wmask_ready"), ["w"])
        lines_sem = sem("bias_lines_written")
        index_items = [s for s in order if s[0] in ("ip", "is")]
        relued = Signal(sem("index_relued"), index_items)
        scored = Signal(sem("index_scored"), [s for s in order if s[0] in ("ip", "iw", "wrow")])
        n_work = {}
        for s in order:
            if s[0] in ("ip", "is"):
                n_work[s] = len(n_work)
        qs_uses = [s for s in order if s[0] == "is"] + [("S", x) for x in items if is_sample(x)]
        qs_ready = Signal(sem("qs_ready"), qs_uses)
        parts = lambda br: range(2) if br in "BC" else [None]
        cache_loads = []
        for s in order:
            if s[0] == "is":
                cache_loads.append((s, "k", None))
            elif s[0] in ("S", "V") and is_sample(s[1]):
                cache_loads += [(s, "k" if s[0] == "S" else "v", r) for r in parts(s[1][0])]
        cslot = {u: n % RING for n, u in enumerate(cache_loads)}
        cdmas = lambda u: 2 if u[1] == "k" and (u[0][0] == "is" or u[0][1][0] == "A") else 1
        cache_loaded = [Signal(sem(f"cache{k}_loaded"), [u for u in cache_loads if cslot[u] == k],
                               lambda u: 16 * cdmas(u)) for k in range(RING)]
        early = lambda x: x[2] < NT // 2
        b_items = [x for x in items if x[0] == "B" and not is_sample(x) and not early(x)]
        last_early = [x for x in items if x[0] == "B" and not is_sample(x) and early(x)][-1]
        zeroed = Signal(sem("queries_zeroed"), ["A"])
        halves_loaded = Signal(sem("bias_halves_loaded"), ["B"], lambda e: 16)
        pbias = [Signal(sem(f"prompt_bias{k}_loaded"), b_items[k::2], lambda e: 16) for k in range(2)]
        strips_loaded = Signal(sem("strips_loaded"), ["C"], lambda e: 16)
        sbias_loads = [("B", j) for j in range(PAIRS)] + [("C", 0)]
        sbias = Signal(sem("sample_bias_loaded"), sbias_loads, lambda e: 32)
        tmask = Signal(sem("token_mask_loaded"), ["m"], lambda e: 16)
        logits = Signal(sem("logits_ready"), items)
        probs = Signal(sem("probs_ready"), items)
        pt_act = Signal(sem("probs_turned_act"), items)
        rsum = Signal(sem("row_sum_inverted"), items)
        om_ready = Signal(sem("own_heads_kept"), [x for x in items if is_sample(x)])
        selj_ready = Signal(sem("selj_ready"), [x for x in items if is_sample(x) and x[0] == "A"])
        gated = Signal(sem("branch_gated"), [s[1] for s in order if s[0] == "R" or (s[0] == "V" and not is_sample(s[1]))])
        selected = Signal(sem("selected"), [t for s in order if s[0] == "K" for t, _, end in s[1] if end])
        o_stored = [Signal(sem(f"branch_tile{t}_stored"), list("BCM"), lambda e: 16) for t in TILES]
        ot_units = [s for s in order if s[0] == "OT"]
        o_loaded = [Signal(sem(f"branch_loaded{k}"), [s for s in ot_units if s[2] == k], lambda e: 16) for k in range(2)]
        merged = Signal(sem("merged_turned"), [s for s in order if s[0] in ("OT", "OA")])
        outs = [(c, t) for c in ("O0", "O1") for t in TILES]
        res_loaded = [Signal(sem(f"residual_loaded{k}"), outs[k::4], lambda e: 16) for k in range(4)]
        summed = Signal(sem("final_squares_summed"), TILES[:NT])
        res_added = Signal(sem("residual_added"), outs)
        layer_over = sem("layer_over")
        layer_sems = range(layer_first, layer_over.num + 1)
        go = {n: sem(f"next_layer_{n}") for n in ("sync", "tensor", "scalar", "vector")}
        fin_done = sem("final_normed")
        y_stored = sem("y_stored")

        last_prompt = {br: (br, H - 1, NT - 1) for br in BRANCHES}
        last_sample = {br: (br, PAIRS - 1, f"s{PAIRS - 1}") for br in BRANCHES}
        before = {"B": None, "C": "B", "M": "C"}

        def wait(eng, signal, event):
            eng.wait_ge(signal.sem, signal.at(event))

        def rows(ap, l, per_layer, first, n):
            return ap[bass.ds(l * per_layer + first, n), :]

        scratch = gate[:, 0:4, :].rearrange("p a b -> p (a b)")

        def queries(br):
            return qTA if br == "A" else qT

        def gates(br):
            return gateA if br == "A" else gate

        def buf(n):
            return work[:, n % 2, :]

        def turned_buf(n):
            return work[:, 2 + n % 2, :]

        n_item = {x: n for n, x in enumerate(items)}

        def next_layer(eng, name):
            eng.drain().then_inc(layer_over, 1)
            eng.wait_ge(go[name], 1)
            eng.sem_clear(go[name])

        block = ctx.enter_context(nc.Block())

        @block.sync
        def _(sp):
            sp.dma_start(xs[:, 0, :], d["x"][0:P, :]).then_inc(x_in[0], 16)
            sp.dma_start(con[:, :], d["const"]).then_inc(s_const, 16)
            sp.dma_start(gain, d["gain"][0:1, :].to_broadcast([P, D])).then_inc(s_gain, 16)
            sp.dma_start(xs[:, 1, :], d["x"][P:2 * P, :]).then_inc(x_in[1], 16)

            def load_chunk(l, c):
                n = CHUNKS.index(c)
                if n >= 2:
                    last = [s for s in order if s[0] == "P" and s[1] == CHUNKS[n - 2]][-1]
                    wait(sp, X.fill(last), last)
                sp.dma_start(wring[:, n % 2, :], rows(d["w"], l, len(CHUNKS) * P, n * P, P)
                             ).then_inc(w_loaded[n % 2].sem, 16)

            cache_state = [0]

            def load_cache(l, u):
                n = cache_state[0]
                assert cache_loads[n] == u
                cache_state[0] += 1
                if n >= RING:
                    use = cache_loads[n - RING][0]
                    units_ = X if use[0] == "V" else S
                    wait(sp, units_.fill(use), use)
                use, kind, r = u
                done = cache_loaded[cslot[u]].sem
                dst = cache[:, cslot[u], :]
                j = use[1] if use[0] == "is" else use[1][1]
                br = "I" if use[0] == "is" else use[1][0]
                p = HD if br in "AI" and kind == "k" else P
                src = rows(d[kind + br], l, PAIRS * p, j * p, p)
                if r is not None:
                    src = src[:, r * D:(r + 1) * D]
                w = src.shape[1]
                if br in "AI" and kind == "k":
                    sp.dma_start(dst[0:64, 0:w], src).then_inc(done, 16)
                    sp.dma_start(dst[64:128, 0:w], src).then_inc(done, 16)
                else:
                    sp.dma_start(dst[:, 0:w], src).then_inc(done, 16)

            with sp.Fori(0, DEPTH) as l:
                cache_state[0] = 0
                load_chunk(l, "A1")
                sp.dma_start(gains[:, 1, :], rows(d["gain"], l, 2, 1, 1).to_broadcast([P, D])).then_inc(small_loaded.sem, 16)
                sp.dma_start(bfb[:, :], rows(d["bf"], l, 1, 0, 1).to_broadcast([P, H])).then_inc(small_loaded.sem, 16)
                load_chunk(l, "mm")
                for t in TILES:
                    sp.wait_ge(x_in[t], 16)
                    sp.dma_start(d["xres"][t * P:(t + 1) * P, :], xs[:, t, :]).then_inc(x_saved.sem, 16)
                for k in range(2):
                    n = NT + 1 + k
                    wait(sp, S.fill(("turn", n - 4)), ("turn", n - 4))
                    sp.dma_start(work[:, n % 4, :], d["mem"][k * P:(k + 1) * P, :]).then_inc(mem_loaded[k].sem, 16)
                wait(sp, normed, ST_)
                wait(sp, x_saved, "x")
                sp.wait_ge(lines_sem, 32)
                sp.dma_start(sc[:, SC_OFF[ST_] + PAST:SC_OFF[ST_] + SKEYS], d["tmask"]).then_inc(tmask.sem, 16)
                nxt = [0]

                def cache_upto(l, n):
                    while nxt[0] < n:
                        load_cache(l, cache_loads[nxt[0]])
                        nxt[0] += 1

                count = lambda br: sum(1 for u in cache_loads if u[0][0] != "is" and u[0][1][0] == br)
                cache_upto(l, PAIRS)
                upto = PAIRS
                load_chunk(l, "B1")
                load_chunk(l, "B2")
                for br in BRANCHES:
                    upto += count(br)
                    if br == "A":
                        cache_upto(l, upto - 2)
                        load_chunk(l, "O0")
                    cache_upto(l, upto)
                    for c in {"B": ["C1", "C2"], "C": ["M1", "A2"], "M": [], "A": ["O1"]}[br]:
                        load_chunk(l, c)
                wait(sp, turned, ("A2", NT - 1))
                for n, u in enumerate(ot_units):
                    _, t, g = u
                    if g == 0:
                        wait(sp, o_stored[t], "M")
                    if n >= 2:
                        wait(sp, T.fill(ot_units[n - 2]), ot_units[n - 2])
                    sp.dma_start(stage[:, g, 0:3 * P], d["oscr"][t * P:(t + 1) * P, 3 * P * g:3 * P * (g + 1)]
                                 ).then_inc(o_loaded[g].sem, 16)
                for n, (c, t) in enumerate(outs):
                    if n == 0:
                        wait(sp, gated, items[-1])
                    if n >= 4:
                        wait(sp, res_added, outs[n - 4])
                    h = 512 * int(c[1])
                    sp.dma_start(work[:, n % 4, 0:512], d["xres"][t * P:(t + 1) * P, h:h + 512]
                                 ).then_inc(res_loaded[n % 4].sem, 16)
                    if n == 3:
                        sp.dma_start(gain, d["gain"][bass.ds(2 * l + 2, 1), :].to_broadcast([P, D])).then_inc(gain_loaded.sem, 16)
                wait(sp, gain_loaded, "g")
                next_layer(sp, "sync")
            for t in TILES:
                sp.wait_ge(fin_done, t + 1)
                sp.dma_start(d["y"][t * P:(t + 1) * P, :], xs[:, t, :]).then_inc(y_stored, 16)
            sp.wait_ge(y_stored, 16 * len(TILES))

        @block.tensor
        def _(pe):
            pe.wait_ge(s_const, 16)
            pe.wait_ge(s_zero, 1)

            def turn(out, src):
                return pe.transpose(out, src, ident)

            with pe.Fori(0, DEPTH) as l:
                for s in order:
                    k = s[0]
                    if k == "turn":
                        n = s[1]
                        wait(pe, normed, n)
                        pe.wait_ge(S.empty(s).sem, S.free(s))
                        if n >= 2:
                            wait(pe, h_act, n - 2)
                        for kt in range(KT):
                            mm = turn(S.ap(s)[:, kt * P:(kt + 1) * P], work[:, n % 4, kt * P:(kt + 1) * P])
                        mm.then_inc(S.fill(s).sem, 1)
                    elif k == "P":
                        c, t = s[1:]
                        n = CHUNKS.index(c)
                        wait(pe, w_loaded[n % 2], c)
                        if c in ("A1", "mm"):
                            wait(pe, h_act, t + (9 if c == "mm" else 0))
                            wait(pe, h_dve, t + (9 if c == "mm" else 0))
                        if c == "O0":
                            wait(pe, merged, ("OA", t))
                        pe.wait_ge(X.empty(s).sem, X.free(s))
                        w = 456 if c == "A1" else 512
                        wv = wring[:, n % 2, :].rearrange("p (k c) -> p k c", k=KT)
                        for kt in range(KT):
                            if c == "mm":
                                lhs = gate[:, :, :].rearrange("p a b -> p (a b)")[:, kt * MEM + t * P:kt * MEM + (t + 1) * P]
                            else:
                                lhs = hT[:, kt, t * P:(t + 1) * P]
                            mm = pe.matmul(X.ap(s)[:, 0:w], lhs, wv[:, kt, 0:w], start=(kt == 0), stop=(kt == KT - 1))
                        mm.then_inc(X.fill(s).sem, 1)
                    elif k == "TR" and s in T.slot:
                        c, t = s[1:]
                        wait(pe, worked if c in ("A1", "A2") else staged, (c, t))
                        pe.wait_ge(T.empty(s).sem, T.free(s))
                        src = stage[:, slot_of[(c, t)], :]
                        nb = {"A1": 3, "B1": 4, "C1": 4}.get(c, 2)
                        for b in range(nb):
                            mm = turn(T.ap(s)[:, b * P:(b + 1) * P], src[:, b * P:(b + 1) * P])
                        mm.then_inc(T.fill(s).sem, 1)
                    elif k == "ip":
                        _, t, h = s
                        wait(pe, turned, ("A1", 8))
                        pe.wait_ge(S.empty(s).sem, S.free(s))
                        L = (t + 1) * P
                        for c0 in range(0, L, 512):
                            mm = pe.matmul(S.ap(s)[:, c0:min(L, c0 + 512)], qT[:, h, t * P:(t + 1) * P],
                                           kA[:, 0, c0:min(L, c0 + 512)], start=True, stop=True)
                        mm.then_inc(S.fill(s).sem, 1)
                    elif k == "wrow":
                        wait(pe, wmask_ready, "w")
                        pe.wait_ge(X.empty(s).sem, X.free(s))
                        pe.matmul(X.ap(s)[:, 0:16], con[:, C_SELT:C_SELT + P], wmask[:, :], start=True, stop=True
                                  ).then_inc(X.fill(s).sem, 1)
                    elif k == "is":
                        j = s[1]
                        wait(pe, qs_ready, s)
                        wait(pe, cache_loaded[cslot[(s, "k", None)]], (s, "k", None))
                        pe.wait_ge(S.empty(s).sem, S.free(s))
                        kc = cache[:, cslot[(s, "k", None)], :]
                        for r in range(2):
                            pe.matmul(S.ap(s)[64 * r:64 * r + 64, 0:PAST], qsA[:, 64 * r:64 * r + 64],
                                      kc[:, r * PAST:(r + 1) * PAST], start=True, stop=True)
                        pe.matmul(S.ap(s)[:, PAST:SKEYS], qsA[:, :], kA[:, 0, SEQ:TOK], start=True, stop=True
                                  ).then_inc(S.fill(s).sem, 1)
                    elif k == "iw":
                        j = s[1]
                        wait(pe, relued, ("is", j))
                        wait(pe, scored, ("wrow",))
                        pe.wait_ge(S.empty(s).sem, S.free(s))
                        r = buf(n_work[("is", j)])
                        o = S.ap(s)[32 * j:32 * j + 32, :]
                        pe.matmul(o[:, 0:PAST], wsel[:, j, :], r[:, 0:PAST], start=True, stop=True)
                        pe.matmul(o[:, PAST:SKEYS], wsel[:, j, :], r[:, PAST:SKEYS], start=True, stop=True
                                  ).then_inc(S.fill(s).sem, 1)
                    elif k == "S":
                        br, h, t = s[1]
                        o = S.ap(s)
                        wait(pe, turned, ({"A": "A2", "M": "M1"}.get(br, br + "1"), ST_ if is_sample(s[1]) else t))
                        pe.wait_ge(S.empty(s).sem, S.free(s))
                        if is_sample(s[1]):
                            wait(pe, qs_ready, s)
                            kc = []
                            for r in parts(br):
                                wait(pe, cache_loaded[cslot[(s, "k", r)]], (s, "k", r))
                                kc.append(cache[:, cslot[(s, "k", r)], :])
                            j = h
                            n = MEM if br == "M" else PAST
                            if br == "A":
                                for r in range(2):
                                    mm = pe.matmul(o[64 * r:64 * r + 64, 0:n], qsA[:, 64 * r:64 * r + 64],
                                                   kc[0][:, r * n:(r + 1) * n], start=True, stop=False)
                                wait(pe, selj_ready, s[1])
                                sm = sc[:, SC_OFF[ST_]:SC_OFF[ST_] + SKEYS]
                                wait(pe, selected, ST_)
                                pe.matmul(o[:, 0:n], selj[:, :], sm[:, 0:n], start=False, stop=True)
                                pe.matmul(o[:, n:SKEYS], qsA[:, :], kA[:, 1, SEQ:TOK], start=True, stop=False)
                                mm = pe.matmul(o[:, n:SKEYS], selj[:, :], sm[:, n:SKEYS], start=False, stop=True)
                            else:
                                for g in range(2):
                                    for r in range(2):
                                        mm = pe.matmul(o[64 * r:64 * r + 64, 0:n], qs[:, g, 64 * r:64 * r + 64],
                                                       kc[r][:, g * n:(g + 1) * n] if br != "M" else
                                                       kc[0][:, (r * 2 + g) * n:(r * 2 + g + 1) * n], start=(g == 0),
                                                       stop=(g == 1))
                                if br != "M":
                                    for g in range(2):
                                        pe.matmul(o[:, n:SKEYS], qs[:, g, :], kT[:, g, SEQ:TOK], start=(g == 0), stop=False)
                                    base = C_CAUS if br == "B" else C_FULL
                                    mm = pe.matmul(o[:, n:SKEYS], ident, con[:, base + 96 - 32 * j:base + 96 - 32 * j + P],
                                                   start=False, stop=True)
                            mm.then_inc(S.fill(s).sem, 1)
                        else:
                            kb = key_tiles(br, t)
                            keys = {"A": kA[:, 1, :], "B": kT[:, h // 2, :], "C": kT[:, h // 2, :], "M": mK[:, h // 2, :]}[br]
                            k0, L = kb[0] * P, len(kb) * P

                            q = queries(br)[:, h, t * P:(t + 1) * P]
                            plain = L - P if br == "B" else L
                            for c0 in range(0, plain, 512):
                                c1 = min(plain, c0 + 512)
                                mm = pe.matmul(o[:, c0:c1], q, keys[:, k0 + c0:k0 + c1], start=True, stop=True)
                            if br == "B":
                                pe.matmul(o[:, plain:L], q, keys[:, k0 + plain:k0 + L], start=True, stop=False)
                                mm = pe.matmul(o[:, plain:L], ident, con[:, C_TRI:C_TRI + P], start=False, stop=True)
                            mm.then_inc(S.fill(s).sem, 1)
                    elif k == "T":
                        wait(pe, probs, s[1])
                        p = buf(n_item[s[1]])
                        nb = blocks(s[1])
                        for g in range((nb + 3) // 4):
                            u = (s, g)
                            pe.wait_ge(T.empty(u).sem, T.free(u))
                            for b in range(4 * g, min(nb, 4 * g + 4)):
                                mm = turn(T.ap(u)[:, (b - 4 * g) * P:(b - 4 * g + 1) * P], p[:, b * P:(b + 1) * P])
                            mm.then_inc(T.fill(u).sem, 1)
                    elif k == "V":
                        br, h, t = s[1]
                        nb = blocks(s[1])
                        pT = turned_buf(n_item[s[1]])
                        wait(pe, pt_act, s[1])
                        pe.wait_ge(X.empty(s).sem, X.free(s))
                        if br in "BC":
                            wait(pe, staged, (br + "2", ST_ if is_sample(s[1]) else t))
                        o = X.ap(s)
                        if is_sample(s[1]):
                            vc = []
                            for r in parts(br):
                                wait(pe, cache_loaded[cslot[(s, "v", r)]], (s, "v", r))
                                vc.append(cache[:, cslot[(s, "v", r)], :])
                            w = HD if br == "A" else W
                            nk = 2 if br == "M" else 4
                            for b in range(nb):
                                for r in range(2):
                                    if b < nk:
                                        k0 = b if br in "BC" else r * nk + b
                                        v = vc[r if br in "BC" else 0][:, k0 * w:(k0 + 1) * w]
                                    else:
                                        v = (vA if br == "A" else vX)[:, ST_, :]
                                    mm = pe.matmul(o[64 * r:64 * r + 64, 0:w], pT[:, b * P + 64 * r:b * P + 64 * r + 64], v,
                                                   start=(b == 0), stop=(b == nb - 1))
                        else:
                            kb = key_tiles(br, t)
                            for b, kt in enumerate(kb):
                                v = {"A": lambda: vA[:, kt, :], "M": lambda: mV[:, kt, h * HD:(h + 1) * HD]}.get(
                                    br, lambda: vX[:, kt, h * HD:(h + 1) * HD])()
                                mm = pe.matmul(o[:, 0:HD], pT[:, b * P:(b + 1) * P], v, start=(b == 0), stop=(b == nb - 1))
                        mm.then_inc(X.fill(s).sem, 1)
                    elif k == "R":
                        j = s[1][1]
                        wait(pe, om_ready, s[1])
                        pe.wait_ge(X.empty(s).sem, X.free(s))
                        pe.matmul(X.ap(s)[32 * j:32 * j + 32, 0:W], con[:, C_SEL:C_SEL + 32],
                                  turned_buf(n_item[s[1]])[:, 0:W], start=True, stop=True).then_inc(X.fill(s).sem, 1)
                    elif k == "OT":
                        g = s[2]
                        wait(pe, o_loaded[g], s)
                        pe.wait_ge(T.empty(s).sem, T.free(s))
                        for b in range(3):
                            mm = turn(T.ap(s)[:, b * P:(b + 1) * P], stage[:, g, b * P:(b + 1) * P])
                        mm.then_inc(T.fill(s).sem, 1)
                    elif k == "OA":
                        t = s[1]
                        wait(pe, gated, last_sample["A"] if t == ST_ else ("A", H - 1, t))
                        pe.wait_ge(T.empty(s).sem, T.free(s))
                        for b in range(2):
                            mm = turn(T.ap(s)[:, b * P:(b + 1) * P], gateA[:, t, b * P:(b + 1) * P])
                        mm.then_inc(T.fill(s).sem, 1)
                next_layer(pe, "tensor")

        @block.scalar
        def _(act):
            def root(t, sem_, count):
                nc.scalar.activation(scratch, xs[:, t, :], ACT.Square, accum_out=final[:, 0, t:t + 1]).then_inc(sem_, 1)
                act.wait_ge(sem_, count)
                return nc.scalar.activation(final[:, 1, t:t + 1], final[:, 0, t:t + 1], ACT.Sqrt,
                                            scale=1.0 / D, bias=con[:, NCONST:NCONST + 1])

            act.wait_ge(s_zero, 1)
            act.wait_ge(s_const, 16)
            for t in range(AHEAD):
                act.wait_ge(x_in[t], 16)
                root(t, s_summed, t + 1).then_inc(s_ahead, 1)
            with act.Fori(0, DEPTH) as l:
                for s in order:
                    k = s[0]
                    if k == "norm" and s[1] >= AHEAD:
                        n = s[1]
                        if n <= ST_:
                            act.wait_ge(x_in[n], 16)
                        else:
                            wait(act, mem_loaded[n - NT - 1], n)
                        src = xs[:, n, :] if n <= ST_ else work[:, n % 4, :]
                        nc.scalar.activation(scratch, src, ACT.Square, accum_out=rstd[:, 0, n:n + 1]
                                             ).then_inc(squares.sem, 1)
                        act.wait_ge(squares.sem, squares.at(n))
                        nc.scalar.activation(rstd[:, 1, n:n + 1], rstd[:, 0, n:n + 1], ACT.Sqrt,
                                             scale=1.0 / D, bias=con[:, NCONST:NCONST + 1]).then_inc(rooted.sem, 1)
                    elif k == "turn":
                        n = s[1]
                        wait(act, S.fill(s), s)
                        src = S.ap(s)[:, 0:4 * P].rearrange("p (b c) -> p b c", b=4)
                        if n < 9:
                            dst = hT[:, 0:4, n * P:(n + 1) * P]
                        else:
                            dst = gate[:, :, :].rearrange("p a b -> p (a b)")[:, 0:4 * MEM].rearrange(
                                "p (k c) -> p k c", k=4)[:, :, (n - 9) * P:(n - 8) * P]
                        nc.scalar.copy(dst, src)
                        act.drain().then_inc(h_act.sem, 1)
                    elif k == "P" and s[1] == "O1":
                        t = s[2]
                        if t < ST_:
                            wait(act, res_added, s[1:])
                            root(t, summed.sem, summed.at(t))
                    elif k == "P" and s[1][0] != "O":
                        c, t = s[1:]
                        n = units.index((c, t))
                        sl = slot_of[(c, t)]
                        sg = stage[:, sl, :]
                        if n >= 2:
                            pu = units[n - 2]
                            if ("TR",) + pu in T.slot:
                                wait(act, T.fill(("TR",) + pu), ("TR",) + pu)
                            if pu in worked.upto:
                                wait(act, worked, pu)
                        st = stored[sl]
                        prior = [u for u in units[:n] if slot_of[u] == sl and u in st.upto]
                        if prior:
                            wait(act, st, prior[-1])
                        wait(act, X.fill(s), s)
                        x = X.ap(s)
                        if c == "mm":
                            nc.scalar.copy(mV[:, t, :], x[:, W:2 * W])
                            nc.scalar.copy(sg[:, 0:W], x[:, 0:W]).then_inc(X.empty(s).sem, 1)
                        elif c == "A1":
                            nc.scalar.copy(sg[:, 0:456], x[:, 0:456]).then_inc(X.empty(s).sem, 1)
                        elif c in ("B1", "C1"):
                            nc.scalar.copy(sg, x).then_inc(X.empty(s).sem, 1)
                        else:
                            prev = {"B2": None, "C2": "B", "M1": "C", "A2": None}[c]
                            if prev:
                                wait(act, o_stored[t], prev)
                            elif c == "A2":
                                wait(act, logits, last_prompt["C"])
                            elif t == ST_:
                                wait(act, X.fill(("P", "mm", 1)), ("P", "mm", 1))
                                act.wait_ge(v_stored.sem, v_stored.at(("mm", 1)))
                            if c == "C2" and t in (ST_, 0):
                                use = ("V", (last_sample if t == ST_ else last_prompt)["B"])
                                wait(act, X.fill(use), use)
                                wait(act, v_stored, ("B2", NT - 1))
                            if c in ("B2", "C2"):
                                nc.scalar.copy(vX[:, t, :], x[:, 0:W])
                            else:
                                nc.scalar.copy(sg[:, 0:W], x[:, 0:W])
                            nc.scalar.activation(sg[:, W:2 * W], x[:, W:2 * W], ACT.Tanh, scale=0.5)
                            nc.scalar.mul(gates(c[0])[:, t, :], x[:, W:2 * W], 0.5).then_inc(X.empty(s).sem, 1)
                        act.drain().then_inc(staged.sem, 1)
                    elif k == "TR" and s in T.slot:
                        c, t = s[1:]
                        wait(act, T.fill(s), s)
                        if c == "A2" and t == ST_:
                            wait(act, zeroed, "A")
                        if c in ("B1", "C1", "M1") and t in (ST_, 0):
                            prev = before[c[0]]
                            use = ("is", PAIRS - 1) if not prev else ("S", (last_sample if t == ST_ else last_prompt)[prev])
                            wait(act, S.fill(use), use)
                            if t == ST_:
                                wait(act, qs_ready, use)
                        tp = T.ap(s)
                        cols = slice(t * P, (t + 1) * P)
                        if c == "mm":
                            nc.scalar.copy(mK[:, :, cols], tp[:, 0:W].rearrange("p (g c) -> p g c", g=2)
                                           ).then_inc(T.empty(s).sem, 1)
                        else:
                            for hp in range(2):
                                half = slice(64 * hp, 64 * hp + 64)
                                last = nc.scalar.mul(queries("A" if c == "A2" else "B")[half, hp:H:2, cols],
                                                     tp[half, 0:W].rearrange("p (g c) -> p g c", g=2), HD ** -0.5)
                            if c in ("B1", "C1"):
                                last = nc.scalar.copy(kT[:, :, cols], tp[:, W:2 * W].rearrange("p (g c) -> p g c", g=2))
                            if c == "A1":
                                for src in range(2):
                                    for dst in range(2):
                                        last = nc.scalar.copy(kA[64 * dst:64 * dst + 64, src, cols],
                                                              tp[64 * src:64 * src + 64, W:W + P])
                            last.then_inc(T.empty(s).sem, 1)
                        act.drain().then_inc(turned.sem, 1)
                    elif k == "F":
                        wait(act, f_dve, "z")
                        nc.scalar.activation(lf[:, 1, :], lf[:, 1, :], ACT.Exp, scale=-1.0).then_inc(f_ready.sem, 1)
                        act.wait_ge(f_ready.sem, f_ready.at("exp"))
                        nc.scalar.activation(lf[:, 1, :], lf[:, 1, :], ACT.Ln, bias=1.0).then_inc(f_ready.sem, 1)
                    elif k in ("ip", "is"):
                        n = n_work[s]
                        L = (s[1] + 1) * P if k == "ip" else SKEYS
                        wait(act, S.fill(s), s)
                        if n >= 2:
                            pv = [x for x in n_work if n_work[x] == n - 2][0]
                            if pv[0] == "ip":
                                wait(act, scored, pv)
                            else:
                                wait(act, S.fill(("iw", pv[1])), ("iw", pv[1]))
                        else:
                            wait(act, S.fill(("turn", 10)), ("turn", 10))
                        nc.scalar.activation(buf(n)[:, 0:L], S.ap(s)[:, 0:L], ACT.Relu).then_inc(S.empty(s).sem, 1)
                        act.drain().then_inc(relued.sem, 1)
                    elif k == "S":
                        x_ = s[1]
                        L = blocks(x_) * P
                        n = n_item[x_]
                        wait(act, logits, x_)
                        p = buf(n)[:, 0:L]
                        if n >= 4:
                            wait(act, rsum, items[n - 4])
                        nc.scalar.activation(p, p, ACT.Exp, scale=-1.0, bias=stat[:, n % 4, 1:2], accum_out=stat[:, n % 4, 2:3]
                                             ).then_inc(probs.sem, 1)
                    elif k == "T":
                        x_ = s[1]
                        n, u = n_item[x_], (s, 0)
                        w = min(4, blocks(x_)) * P
                        wait(act, T.fill(u), u)
                        if n >= 2:
                            pr = items[n - 2]
                            q = ("R", pr) if is_sample(pr) else ("V", pr)
                            wait(act, X.fill(q), q)
                        nc.scalar.copy(turned_buf(n)[:, 0:w], T.ap(u)[:, 0:w]).then_inc(T.empty(u).sem, 1)
                        if blocks(x_) > 4:
                            u, w = (s, 1), (blocks(x_) - 4) * P
                            wait(act, T.fill(u), u)
                            nc.scalar.copy(turned_buf(n)[:, 4 * P:4 * P + w], T.ap(u)[:, 0:w]).then_inc(T.empty(u).sem, 1)
                        act.drain().then_inc(pt_act.sem, 1)
                    elif k == "OT" or k == "OA":
                        t = s[1]
                        if k == "OT":
                            g = s[2]
                            wait(act, T.fill(s), s)
                            nc.scalar.copy(hT[:, 2 + 3 * g:5 + 3 * g, t * P:(t + 1) * P],
                                           T.ap(s)[:, 0:3 * P].rearrange("p (b c) -> p b c", b=3)).then_inc(T.empty(s).sem, 1)
                        else:
                            wait(act, T.fill(s), s)
                            nc.scalar.copy(hT[:, 0:2, t * P:(t + 1) * P], T.ap(s)[:, 0:2 * P].rearrange("p (b c) -> p b c", b=2)
                                           ).then_inc(T.empty(s).sem, 1)
                        act.drain().then_inc(merged.sem, 1)
                next_layer(act, "scalar")
            root(ST_, s_summed, AHEAD + 1).then_inc(s_last, 1)

        @block.vector
        def _(dve):
            v = nc.vector
            v.memset(qT[:, :, :], 0.0)
            v.memset(qs[:, :, :], 0.0)
            v.memset(credit[:, :], 0.0).then_inc(s_zero, 1)
            dve.wait_ge(s_zero, 1)
            dve.wait_ge(s_const, 16)

            def rotate(sg, heads, t):
                a = sg[:, 0:heads * HD].rearrange("p (h d) -> p h d", h=heads)
                x1, x2 = a[:, :, 0:ROT], a[:, :, ROT:2 * ROT]
                co = con[:, C_ROPE + 16 * t:C_ROPE + 16 * t + 8].unsqueeze(1).to_broadcast([P, heads, ROT])
                si = con[:, C_ROPE + 16 * t + 8:C_ROPE + 16 * t + 16].unsqueeze(1).to_broadcast([P, heads, ROT])
                u1 = rtmp[:, 0, 0:heads * ROT].rearrange("p (h d) -> p h d", h=heads)
                u2 = rtmp[:, 1, 0:heads * ROT].rearrange("p (h d) -> p h d", h=heads)
                v.tensor_tensor(u1, x1, si, ALU.mult)
                v.tensor_tensor(u2, x2, si, ALU.mult)
                v.tensor_tensor(x1, x1, co, ALU.mult)
                v.tensor_tensor(x2, x2, co, ALU.mult)
                dve.drain()
                v.tensor_tensor(x1, x1, u2, ALU.subtract)
                return v.tensor_tensor(x2, x2, u1, ALU.add)

            inverting = []

            with dve.Fori(0, DEPTH) as l:
                for units_ in (S, T, X):
                    for q in units_.emptied:
                        dve.drain().then_inc(q.sem, 1)
                for s in order:
                    k = s[0]
                    if k == "norm":
                        n = s[1]
                        if n < AHEAD:
                            dve.wait_ge(s_ahead, n + 1)
                        else:
                            wait(dve, rooted, n)
                        if n == 0:
                            dve.wait_ge(s_gain, 16)
                        if n == ST_ + 1:
                            wait(dve, small_loaded, "g")
                        if n >= 4:
                            wait(dve, S.fill(("turn", n - 4)), ("turn", n - 4))
                        v.reciprocal(rstd[:, 2, n:n + 1], (final if n < AHEAD else rstd)[:, 1, n:n + 1])
                        dve.drain()
                        src = xs[:, n, :] if n <= ST_ else work[:, n % 4, :]
                        v.scalar_tensor_tensor(out=work[:, n % 4, :], in0=src, scalar=rstd[:, 2, n:n + 1],
                                               in1=gain if n <= ST_ else gains[:, 1, :], op0=ALU.mult, op1=ALU.mult).then_inc(normed.sem, 1)
                    elif k == "turn":
                        n = s[1]
                        wait(dve, S.fill(s), s)
                        src = S.ap(s)[:, 4 * P:8 * P].rearrange("p (b c) -> p b c", b=4)
                        if n < 9:
                            dst = hT[:, 4:8, n * P:(n + 1) * P]
                        else:
                            dst = gate[:, :, :].rearrange("p a b -> p (a b)")[:, 4 * MEM:8 * MEM].rearrange(
                                "p (k c) -> p k c", k=4)[:, :, (n - 9) * P:(n - 8) * P]
                        v.tensor_copy(dst, src).then_inc(S.empty(s).sem, 1)
                        dve.drain().then_inc(h_dve.sem, 1)
                    elif k == "P" and (s[1], s[2]) in worked.upto:
                        c, t = s[1:]
                        wait(dve, staged, (c, t))
                        sg = stage[:, slot_of[(c, t)], :]
                        if c == "A1":
                            if t == 0:
                                wait(dve, small_loaded, "g")
                            rotate(sg, 6, t)
                            v.tensor_copy(vA[:, t, :], sg[:, 384:448])
                            v.tensor_scalar(wi[:, t, :], sg[:, 448:452], H ** -0.5, None, ALU.mult)
                            v.tensor_tensor(lf[:, 0, t * H:(t + 1) * H], sg[:, 452:456], bfb[:, :], ALU.add)
                        else:
                            if c == "A2":
                                rotate(sg, 4, t)
                            ga = gates(c[0])[:, t, :]
                            v.scalar_tensor_tensor(out=ga, in0=sg[:, W:2 * W], scalar=1.0, in1=ga,
                                                   op0=ALU.add, op1=ALU.mult)
                        dve.drain().then_inc(worked.sem, 1)
                    elif k == "P" and s[1][0] == "O":
                        c, t = s[1:]
                        n = outs.index((c, t))
                        wait(dve, X.fill(s), s)
                        wait(dve, res_loaded[n % 4], (c, t))
                        h = 512 * int(c[1])
                        v.tensor_tensor(xs[:, t, h:h + 512], X.ap(s), work[:, n % 4, 0:512], ALU.add
                                        ).then_inc(X.empty(s).sem, 1)
                        dve.drain().then_inc(res_added.sem, 1)
                    elif k == "F":
                        z, e, m = lf[:, 0, :], lf[:, 1, :], lf[:, 2, :]
                        v.scalar_tensor_tensor(out=e, in0=z, scalar=-1.0, in1=z, op0=ALU.mult, op1=ALU.max)
                        v.tensor_scalar(m, z, 0.0, None, ALU.min)
                        dve.drain().then_inc(f_dve.sem, 1)
                        wait(dve, f_ready, "ln")
                        v.tensor_tensor(z, m, e, ALU.subtract)
                        dve.drain().then_inc(f_dve.sem, 1)
                    elif k == "ip":
                        _, t, h = s
                        L = (t + 1) * P
                        dst = sc[:, SC_OFF[t]:SC_OFF[t] + L]
                        wait(dve, relued, s)
                        r = buf(n_work[s])[:, 0:L]
                        if (t, h) == (SEL_TILES[0], 0):
                            dve.wait_ge(lines_sem, 32)
                            wait(dve, x_saved, "x")
                        if h == 0:
                            v.tensor_scalar(dst, r, wi[:, t, 0:1], None, ALU.mult)
                        else:
                            v.scalar_tensor_tensor(out=dst, in0=r, scalar=wi[:, t, h:h + 1], in1=dst, op0=ALU.mult, op1=ALU.add)
                        dve.drain().then_inc(scored.sem, 1)
                        if h == H - 1:
                            v.tensor_tensor(dst[:, L - P:L], dst[:, L - P:L], con[:, C_CM + P:C_CM + 2 * P], ALU.add)
                            dve.drain()
                    elif k == "wrow":
                        wait(dve, f_dma, "rows")
                        frow, fsam = work[0:4, 2, :], work[0:32, 3, :]
                        v.tensor_tensor_scan(frow, frow, frow, 0.0, ALU.add, ALU.bypass)
                        v.tensor_tensor_scan(fsam[:, 0:PAST + STEPS], fsam[:, 0:PAST + STEPS], fsam[:, 0:PAST + STEPS], 0.0,
                                             ALU.add, ALU.bypass)
                        dve.drain().then_inc(f_dve.sem, 1)
                        v.tensor_scalar(frow, frow, -1.0, None, ALU.mult)
                        v.tensor_scalar(fsam[:, 0:PAST + STEPS], fsam[:, 0:PAST + STEPS], -1.0, None, ALU.mult)
                        dve.drain()
                        v.tensor_copy(fsam[:, PAST + STEPS:SKEYS].rearrange("p (b i) -> p b i", i=STEPS),
                                      fsam[:, PAST:PAST + STEPS].unsqueeze(1).to_broadcast([32, 7, STEPS]))
                        dve.drain().then_inc(f_dve.sem, 1)
                        wait(dve, X.fill(s), s)
                        for j in range(PAIRS):
                            v.tensor_tensor_reduce(wrow[:, 4:8], X.ap(s)[:, 4 * j:4 * j + 4], con[:, C_HM:C_HM + 4], 1.0, 0.0,
                                                   ALU.mult, ALU.add, wrow[:, j:j + 1])
                            dve.drain()
                        dve.drain().then_inc(X.empty(s).sem, 1)
                        for j in range(PAIRS):
                            v.tensor_scalar(wsel[:, j, :], con[:, C_SEL:C_SEL + 32], wrow[:, j:j + 1], None, ALU.mult)
                        dve.drain().then_inc(scored.sem, 1)
                    elif k == "iw":
                        j = s[1]
                        wait(dve, S.fill(s), s)
                        if j == 0:
                            wait(dve, tmask, "m")
                            v.memset(sc[:, SC_OFF[ST_] + SKEYS:SC_W], 1e30)
                        r0 = slice(32 * j, 32 * j + 32)
                        dst = sc[r0, SC_OFF[ST_]:SC_OFF[ST_] + SKEYS]
                        v.tensor_copy(dst[:, 0:PAST], S.ap(s)[r0, 0:PAST])
                        v.tensor_tensor(dst[:, PAST:SKEYS], S.ap(s)[r0, PAST:SKEYS], dst[:, PAST:SKEYS], ALU.add
                                        ).then_inc(S.empty(s).sem, 1)
                        dve.drain().then_inc(scored.sem, 1)
                    elif k == "K":
                        rows_ = []
                        for t, i, end in s[1]:
                            L = SKEYS + FILL if t == ST_ else (t + 1) * P
                            rows_.append((sc[:, SC_OFF[t]:SC_OFF[t] + L], end, t))
                        for n, (a, end, t) in enumerate(rows_):
                            v.max(top8[:, n, :], a)
                        dve.drain()
                        for n, (a, end, t) in enumerate(rows_):
                            v.match_replace(a, top8[:, n, :], a, TAKEN)
                        dve.drain()
                        for n, (a, end, t) in enumerate(rows_):
                            if end:
                                v.tensor_scalar(a, a, 0.5 * TAKEN, NEG, ALU.is_ge, ALU.mult)
                                dve.drain().then_inc(selected.sem, 1)
                    elif k == "S":
                        x_ = s[1]
                        br, h, t = x_
                        n = n_item[x_]
                        L = blocks(x_) * P
                        wait(dve, S.fill(s), s)
                        src, dst = S.ap(s)[:, 0:L], buf(n)[:, 0:L]
                        nm = stat[:, n % 4, 1:2]
                        if n >= 2:
                            pr = items[n - 2]
                            g = (blocks(pr) + 3) // 4 - 1
                            wait(dve, T.fill((("T", pr), g)), (("T", pr), g))
                            wait(dve, probs, pr)
                        if n < 2:
                            wait(dve, S.fill(("iw", PAIRS - 1)), ("iw", PAIRS - 1))
                            wait(dve, f_dma, "out")
                        if br == "B" or br == "C":
                            if not is_sample(x_):
                                if br == "B":
                                    if early(x_):
                                        wait(dve, halves_loaded, "B")
                                        b_ = halves[:, h, 0:L]
                                    else:
                                        m = b_items.index(x_)
                                        wait(dve, pbias[m % 2], x_)
                                        b_ = gains[:, m % 2, 0:L]
                                else:
                                    if (h, t) == (0, 0):
                                        wait(dve, strips_loaded, "C")
                                        cm = con[:, C_CM + P:C_CM + 2 * P].unsqueeze(1).to_broadcast([P, H, P])
                                        v.tensor_tensor(strips[:, :, 4 * P:5 * P], strips[:, :, 4 * P:5 * P], cm, ALU.add)
                                        v.tensor_scalar(strips[64:128, :, 0:64], strips[64:128, :, 0:64], NEG, None, ALU.add)
                                        dve.drain()
                                    b_ = strips[:, h, 5 * P - L:5 * P]
                            else:
                                if br == "B" or h == 0:
                                    wait(dve, sbias, (br, h))
                                if br == "C" and h == 0:
                                    v.tensor_copy(sbias_[:, PAST + STEPS:SKEYS].rearrange("p (b i) -> p b i", i=STEPS),
                                                  sbias_[:, PAST:PAST + STEPS].unsqueeze(1).to_broadcast([P, 7, STEPS]))
                                    dve.drain()
                                b_ = sbias_[:, 0:L]
                            last = v.tensor_tensor_reduce(dst, src, b_, -1.0, -NEG, ALU.add, ALU.min, nm)
                        elif br == "A" and not is_sample(x_):
                            if t in SEL_TILES:
                                b_ = sc[:, SC_OFF[t]:SC_OFF[t] + L]
                            else:
                                b_ = con[:, C_CM + 2 * P - L:C_CM + 2 * P]
                            last = v.tensor_tensor_reduce(dst, src, b_, -1.0, -NEG, ALU.add, ALU.min, nm)
                        else:
                            last = v.tensor_scalar(dst, src, -1.0, None, ALU.mult, ALU.min, accum_out=nm)
                        last.then_inc(S.empty(s).sem, 1)
                        dve.drain().then_inc(logits.sem, 1)
                        inverting.clear()
                    elif k == "T":
                        n = n_item[s[1]]
                        wait(dve, probs, s[1])
                        v.reciprocal(stat[:, n % 4, 3:4], stat[:, n % 4, 2:3]).then_inc(rsum.sem, 1)
                        inverting.append(s[1])
                    elif k == "V":
                        x_ = s[1]
                        br, h, t = x_
                        n = n_item[x_]
                        if x_ in inverting:
                            dve.drain()
                        inverting.clear()
                        wait(dve, X.fill(s), s)
                        ri = stat[:, n % 4, 3:4]
                        if is_sample(x_):
                            o = X.ap(s)[:, 0:W].rearrange("p (h d) -> p h d", h=H)
                            if br == "A":
                                o = X.ap(s)[:, 0:HD].unsqueeze(1).to_broadcast([P, H, HD])
                            v.scalar_tensor_tensor(out=turned_buf(n)[:, 0:W].rearrange("p (h d) -> p h d", h=H), in0=o, scalar=ri,
                                                   in1=con[:, C_HM:C_HM + 4].unsqueeze(2).to_broadcast([P, H, HD]),
                                                   op0=ALU.mult, op1=ALU.mult).then_inc(X.empty(s).sem, 1)
                            dve.drain().then_inc(om_ready.sem, 1)
                        else:
                            g = gates(br)[:, t, h * HD:(h + 1) * HD]
                            v.scalar_tensor_tensor(out=g, in0=X.ap(s)[:, 0:HD], scalar=ri, in1=g, op0=ALU.mult, op1=ALU.mult
                                                   ).then_inc(X.empty(s).sem, 1)
                            dve.drain().then_inc(gated.sem, 1)
                    elif k == "R":
                        j = s[1][1]
                        wait(dve, X.fill(s), s)
                        r0 = slice(32 * j, 32 * j + 32)
                        ga = gates(s[1][0])[r0, ST_, :]
                        v.tensor_tensor(ga, X.ap(s)[r0, 0:W], ga, ALU.mult).then_inc(X.empty(s).sem, 1)
                        dve.drain().then_inc(gated.sem, 1)
                next_layer(dve, "vector")
            v.reciprocal(final[:, 0, 0:NT], final[:, 1, 0:NT])
            dve.drain()
            for t in TILES:
                if t == ST_:
                    dve.wait_ge(s_last, 1)
                    v.reciprocal(final[:, 0, t:t + 1], final[:, 1, t:t + 1])
                    dve.drain()
                v.scalar_tensor_tensor(out=xs[:, t, :], in0=xs[:, t, :], scalar=final[:, 0, t:t + 1],
                                       in1=gain, op0=ALU.mult, op1=ALU.mult).then_inc(fin_done, 1)

        @block.gpsimd
        def _(pool):
            g = nc.gpsimd
            for t in TILES[2:]:
                pool.dma_start(xs[:, t, :], d["x"][t * P:(t + 1) * P, :]).then_inc(x_in[t], 16)
            pool.wait_ge(s_zero, 1)
            pool.wait_ge(s_const, 16)

            def store(dst, src, sem_, **kw):
                pool.dma_start(dst, src, **kw).then_inc(sem_, 16)

            with pool.Fori(0, DEPTH) as l:
                def out_rows(name, t):
                    if t == ST_:
                        return rows(d["s" + name], l, P, 0, P)
                    return rows(d["p" + name], l, SEQ, t * P, P)

                line = sc[0:H, 4 * D:4 * D + XL]

                def bias_lines(part):
                    if part == 0:
                        pool.dma_start(line[:, XL - 256:XL], d["cb"][bass.ds(l * H, H), 0:256]).then_inc(lines_sem, 16)
                    elif part == 1:
                        pool.wait_ge(lines_sem, 16)
                        g.tensor_copy(line[:, 0:XL - 256], line[:, XL - 256:XL - 255].to_broadcast([H, XL - 256]))
                        pool.drain()
                        pool.dma_start(d["xl"], line).then_inc(lines_sem, 16)
                    else:
                        pool.wait_ge(lines_sem, 32)
                        for h in range(H):
                            pool.dma_start(d["xr"][h * P:(h + 1) * P, :], d["xl"][h:h + 1, :].to_broadcast([P, XL])
                                           ).then_inc(lines_sem, 16)

                def prompt_bias(m):
                    _, h, t = b_items[m]
                    L = (t + 1) * P
                    pool.dma_start(gains[:, m % 2, 0:L], d["fp"][h:h + 1, 0:L].to_broadcast([P, L])).then_inc(pbias[m % 2].sem, 16)

                def sample_bias(br, j):
                    for r in range(2):
                        if br == "B":
                            src = bass.AP(d["fs"].tensor, (2 * j + r) * SKEYS, [[R * SKEYS, H], [0, STEPS], [1, SKEYS]])
                        else:
                            src = bass.AP(d["xr"].tensor, P - 1, [[P * XL, H], [XL - 1, STEPS], [1, PAST + STEPS]])
                        pool.dma_start(sbias_[64 * r:64 * r + 64, 0:src.shape[-1]], src).then_inc(sbias.sem, 16)

                for s in order:
                    k = s[0]
                    if k == "P" and s[1][0] != "O":
                        c, t = s[1:]
                        sg = stage[:, slot_of[(c, t)], :]
                        done = stored[slot_of[(c, t)]].sem
                        if (c, t) == ("A2", ST_):
                            use = ("V", last_prompt["C"])
                            wait(pool, X.fill(use), use)
                            wait(pool, v_stored, ("C2", NT - 1))
                            pool.drain()
                            g.memset(qTA[64:128, 0:H:2, :], 0.0)
                            pool.drain()
                            g.memset(qTA[0:64, 1:H:2, :], 0.0)
                            pool.drain().then_inc(zeroed.sem, 1)
                        if (c, t) == ("B2", ST_):
                            wait(pool, normed, NORMS - 1)
                            wait(pool, f_dma, "out")
                            src = bass.AP(d["fp"].tensor, 0, [[0, P], [SEQ, H], [1, SEQ // 2]])
                            pool.dma_start(halves, src).then_inc(halves_loaded.sem, 16)
                            sample_bias("B", 0)
                        if c == "mm":
                            wait(pool, staged, (c, t))
                            store(rows(d["pm_k"], l, MEM, t * P, P), sg[:, 0:W], done)
                            store(rows(d["pm_v"], l, MEM, t * P, P), mV[:, t, :], v_stored.sem)
                        elif c == "A1":
                            wait(pool, worked, (c, t))
                            store(out_rows("a_ki", t), sg[:, 256:320], done)
                            store(out_rows("a_k", t), sg[:, 320:384], done)
                            store(out_rows("a_v", t), sg[:, 384:448], done)
                            if 1 <= t <= 3:
                                bias_lines(t - 1)
                            if t == ST_:
                                for j in range(PAIRS):
                                    last = g.tensor_scalar(wmask[:, 4 * j:4 * j + 4], wi[:, ST_, :], con[:, C_PM + j:C_PM + j + 1],
                                                           None, ALU.mult)
                                last.then_inc(wmask_ready.sem, 1)
                        elif c in ("B1", "C1"):
                            if c == "B1" or t >= 4:
                                wait(pool, staged, (c, t))
                                if c == "B1":
                                    store(out_rows("b_k", t), sg[:, W:2 * W], done)
                                elif t == ST_:
                                    store(out_rows("c_k", t), sg[:, W:2 * W], done)
                                else:
                                    store(rows(d["pc_k"], l, 512, (t - 4) * P, P), sg[:, W:2 * W], done)
                        elif c in ("B2", "C2"):
                            if c == "B2" or t >= 4:
                                wait(pool, staged, (c, t))
                                if c == "B2":
                                    store(out_rows("b_v", t), vX[:, t, :], v_stored.sem)
                                elif t == ST_:
                                    store(out_rows("c_v", t), vX[:, t, :], v_stored.sem)
                                else:
                                    store(rows(d["pc_v"], l, 512, (t - 4) * P, P), vX[:, t, :], v_stored.sem)
                    elif k == "F":
                        wait(pool, f_dve, "lf")
                        z = lf[:, 0, :].rearrange("p (t h) -> p t h", h=H)
                        store(rows(d["pb_lf"], l, SEQ, 0, SEQ).rearrange("(t p) h -> p t h", p=P), z[:, 0:8, :], f_dma.sem)
                        store(rows(d["sb_lf"], l, P, 0, P), z[:, 8, :], f_dma.sem)
                        store(d["lfnat"].rearrange("(t p) h -> p t h", p=P), z, f_dma.sem)
                        wait(pool, f_dma, "nat")
                        wait(pool, S.fill(("turn", 10)), ("turn", 10))
                        for h in range(H):
                            store(work[h:h + 1, 2, :], d["lfnat"][0:SEQ, h:h + 1].rearrange("s h -> h s"), f_dma.sem,
                                  allow_slow_non_contiguous=True)
                        store(work[0:32, 3, 0:PAST], rows(d["blf"], l, 32, 0, 32), f_dma.sem)
                        for h in range(H):
                            store(work[8 * h:8 * h + 8, 3, PAST:PAST + STEPS],
                                  d["lfnat"][SEQ:TOK, :].rearrange("(r i) h -> h r i", i=STEPS)[h], f_dma.sem,
                                  allow_slow_non_contiguous=True)
                    elif k == "wrow":
                        wait(pool, f_dve, "spread")
                        store(d["fp"], work[0:4, 2, :], f_dma.sem)
                        store(d["fs"], work[0:32, 3, 0:SKEYS], f_dma.sem)
                    elif k == "Q" and s[1] in range(PAIRS):
                        j = s[1]
                        if j == 0:
                            wait(pool, turned, ("A1", 8))
                        else:
                            wait(pool, S.fill(("is", j - 1)), ("is", j - 1))
                        last = g.tensor_copy(qsA[:, :].rearrange("p (r h i) -> p r h i", r=2, h=H),
                                             qT[:, :, SEQ + 32 * j:SEQ + 32 * j + 32].rearrange("p h (r i) -> p r h i", r=2))
                        last.then_inc(qs_ready.sem, 1)
                    elif k == "Q":
                        x_ = s[1]
                        br, j, t = x_
                        if j == 0:
                            wait(pool, turned, ({"A": "A2", "M": "M1"}.get(br, br + "1"), ST_))
                        prs = [y for y in items[:n_item[x_]] if is_sample(y)]
                        if prs:
                            wait(pool, S.fill(("S", prs[-1])), ("S", prs[-1]))
                        src = queries(br)[:, :, SEQ + 32 * j:SEQ + 32 * j + 32].rearrange("p h (r i) -> p r h i", r=2)
                        if br == "A":
                            if j == 0:
                                wait(pool, S.fill(("is", PAIRS - 1)), ("is", PAIRS - 1))
                            g.tensor_scalar(selj[:, :], con[:, C_SELT:C_SELT + P], con[:, C_PM + j:C_PM + j + 1], None,
                                            ALU.mult).then_inc(selj_ready.sem, 1)
                            last = g.tensor_copy(qsA[:, :].rearrange("p (r h i) -> p r h i", r=2, h=H), src)
                        else:
                            if br == "B" and j == 0:
                                wait(pool, S.fill(("is", PAIRS - 1)), ("is", PAIRS - 1))
                                g.memset(qs[:, :, :], 0.0)
                                pool.drain()
                            for gg in range(2):
                                dst = qs[:, gg, :].rearrange("p (r h i) -> p r h i", r=2, h=H)[:, :, 2 * gg:2 * gg + 2, :]
                                last = g.tensor_copy(dst, src[:, :, 2 * gg:2 * gg + 2, :])
                        last.then_inc(qs_ready.sem, 1)
                    elif k == "S":
                        x_ = s[1]
                        br, h, t = x_
                        if br == "B" and (is_sample(x_) or x_ == last_early or not early(x_)):
                            wait(pool, logits, x_)
                            if is_sample(x_):
                                if h == PAIRS - 1:
                                    pool.wait_ge(lines_sem, 96)
                                sample_bias(*sbias_loads[h + 1])
                            elif x_ == last_early:
                                prompt_bias(0)
                                prompt_bias(1)
                            elif b_items.index(x_) + 2 < len(b_items):
                                prompt_bias(b_items.index(x_) + 2)
                            elif x_ == b_items[-1]:
                                src = bass.AP(d["xr"].tensor, P - 1, [[XL - 1, P], [P * XL, H], [1, 5 * P]])
                                pool.dma_start(strips, src).then_inc(strips_loaded.sem, 16)
                    elif s[0] in "VR" and s[1][0] != "A" and s[1][1] == H - 1 and is_sample(s[1]) == (k == "R"):
                        br, _, t = s[1]
                        wait(pool, gated, s[1])
                        t = ST_ if k == "R" else t
                        store(d["oscr"][t * P:(t + 1) * P, GCOL[br] - W:GCOL[br]], gate[:, t, :], o_stored[t].sem)
                for q in stored + [v_stored, f_dma, halves_loaded, strips_loaded, sbias] + pbias + o_stored:
                    pool.wait_ge(q.sem, q.layer)
                pool.wait_ge(lines_sem, 96)
                pool.wait_ge(layer_over, 4)
                pool.dma_reset(layer_sems)
                pool.sem_clear(layer_sems)
                for q in go.values():
                    pool.sem_inc(q, 1)


def constants():
    con = np.zeros((P, NCONST + 1), np.float32)
    p = np.arange(P)
    con[:, C_ID:C_ID + P] = np.eye(P)
    con[:, C_TRI:C_TRI + P] = np.where(p[None, :] <= p[:, None], 0, NEG)
    con[:, C_CM + P:C_CM + 2 * P] = np.where(p[None, :] // 64 <= p[:, None] // 64, 0, NEG)
    r, h, i = p // 64, p // STEPS % H, p % STEPS
    for base, causal in ((C_FULL, False), (C_CAUS, True)):
        w = np.full((P, 224), NEG, np.float32)
        for step in range(STEPS):
            ok = (step <= i) | (not causal)
            w[p[ok], 96 + STEPS * r[ok] + step] = 0
        con[:, base:base + 224] = w
    con[:, C_SELT:C_SELT + P] = (p[:, None] % 32 == (STEPS * r + i)[None, :])
    con[:, C_SEL:C_SEL + 32] = ((STEPS * r + i)[:, None] == np.arange(32)[None, :])
    con[:, C_PM:C_PM + 4] = (p[:, None] // 32 == np.arange(4)[None, :])
    con[:, C_HM:C_HM + 4] = (h[:, None] == np.arange(4)[None, :])
    inv = np.float32(500000.0) ** (-np.arange(ROT, dtype=np.float32) / np.float32(ROT))
    for t in TILES:
        pos = (t * P + p if t < NT else PAST + p % STEPS).astype(np.float32)
        ang = (pos[:, None] * inv[None, :].astype(np.float32)).astype(np.float32)
        con[:, C_ROPE + 16 * t:C_ROPE + 16 * t + 8] = np.cos(ang.astype(np.float64))
        con[:, C_ROPE + 16 * t + 8:C_ROPE + 16 * t + 16] = np.sin(ang.astype(np.float64))
    con[:, NCONST] = EPS
    tmask = np.where(p[:, None] // STEPS == p[None, :] // STEPS, 0, NEG).astype(np.float32)
    return con, tmask


def lay_out(x_prompt, x_sample, cache_a_k, cache_a_v, cache_a_kidx, cache_b_k, cache_b_v, cache_b_logf,
            cache_c_k, cache_c_v, cache_mem_k, cache_mem_v, mem_prompt, w_in, w_out, g_norm, b_f, c_bias,
            g_mem, w_mem_kv, g_final):
    a = np.ascontiguousarray
    off, cols = 0, {}
    for name, n in (("a_q", W), ("a_k", HD), ("a_v", HD), ("a_qi", W), ("a_ki", HD), ("a_wi", H), ("a_g", W), ("b_q", W),
                    ("b_k", W), ("b_v", W), ("b_f", H), ("b_g", W), ("c_q", W), ("c_k", W), ("c_v", W), ("c_g", W),
                    ("m_q", W), ("m_g", W)):
        cols[name] = w_in[:, :, off:off + n]
        off += n
    join = lambda *names: np.concatenate([cols[n] for n in names], -1)
    a1 = join("a_qi", "a_ki", "a_k", "a_v", "a_wi", "b_f")
    a1 = np.concatenate([a1, np.zeros(a1.shape[:2] + (512 - a1.shape[2],), a1.dtype)], -1)
    chunks = {"A1": a1, "mm": w_mem_kv, "B1": join("b_q", "b_k"), "B2": join("b_v", "b_g"), "C1": join("c_q", "c_k"),
              "C2": join("c_v", "c_g"), "M1": join("m_q", "m_g"), "A2": join("a_q", "a_g"),
              "O0": w_out[:, :, :512], "O1": w_out[:, :, 512:]}
    w = np.stack([chunks[c] for c in CHUNKS], 1)
    w = w.reshape(DEPTH, len(CHUNKS), KT, P, 512).transpose(0, 1, 3, 2, 4)
    shared_k = lambda c: a(c.reshape(DEPTH, PAIRS, 2, PAST, HD).transpose(0, 1, 4, 2, 3).reshape(-1, 2 * PAST))
    heads_k = lambda c: a(c.reshape(DEPTH, PAIRS, 2, -1, 2, 2, HD).transpose(0, 1, 5, 6, 2, 4, 3).reshape(
        DEPTH * PAIRS * P, -1))
    values = lambda c: a(c.reshape(DEPTH, PAIRS, 2, c.shape[2] // P, P, -1).transpose(0, 1, 4, 2, 3, 5).reshape(
        DEPTH * PAIRS * P, -1))
    con, tmask = constants()
    return {
        "x": a(np.concatenate([x_prompt.reshape(SEQ, D), x_sample.reshape(P, D)])),
        "mem": a(mem_prompt.reshape(MEM, D)),
        "w": a(w.reshape(-1, KT * 512)),
        "gain": a(np.concatenate([np.stack([g_norm, g_mem], 1).reshape(2 * DEPTH, D), g_final[None]])),
        "bf": a(b_f),
        "cb": a(c_bias[:, :, ::-1].reshape(DEPTH * H, -1)),
        "blf": a(cache_b_logf.transpose(0, 3, 1, 2).reshape(DEPTH * H * R, PAST)),
        "kI": shared_k(cache_a_kidx), "kA": shared_k(cache_a_k), "vA": values(cache_a_v),
        "kB": heads_k(cache_b_k), "vB": values(cache_b_v), "kC": heads_k(cache_c_k), "vC": values(cache_c_v),
        "kM": heads_k(cache_mem_k), "vM": values(cache_mem_v),
        "const": con, "tmask": tmask,
    }


_OUTS = {"y": (TOK, D), "pa_k": (DEPTH * SEQ, HD), "pa_v": (DEPTH * SEQ, HD), "pa_ki": (DEPTH * SEQ, HD),
         "pb_k": (DEPTH * SEQ, W), "pb_v": (DEPTH * SEQ, W), "pb_lf": (DEPTH * SEQ, H),
         "pc_k": (DEPTH * 512, W), "pc_v": (DEPTH * 512, W), "pm_k": (DEPTH * MEM, W), "pm_v": (DEPTH * MEM, W),
         "sa_k": (DEPTH * P, HD), "sa_v": (DEPTH * P, HD), "sa_ki": (DEPTH * P, HD),
         "sb_k": (DEPTH * P, W), "sb_v": (DEPTH * P, W), "sb_lf": (DEPTH * P, H),
         "sc_k": (DEPTH * P, W), "sc_v": (DEPTH * P, W)}
_SCRATCH = {"xres": (TOK, D), "oscr": (TOK, 3 * W), "lfnat": (TOK, H), "fp": (H, SEQ), "fs": (H * R, SKEYS), "xl": (H, XL),
            "xr": (H * P, XL)}


def kernel(**inputs):
    import concourse.bacc as bacc
    from concourse.bass_utils import run_bass_kernel_spmd

    arrays = lay_out(**{k: np.asarray(v) for k, v in inputs.items()})
    nc = bacc.Bacc("TRN2", target_bir_lowering=False, num_devices=1)
    d = {n: nc.dram_tensor(f"in_{n}", a.shape, F32, kind="ExternalInput").ap() for n, a in arrays.items()}
    d |= {n: nc.dram_tensor(f"out_{n}", s, F32, kind="ExternalOutput").ap() for n, s in _OUTS.items()}
    d |= {n: nc.dram_tensor(f"scratch_{n}", s, F32, kind="Internal").ap() for n, s in _SCRATCH.items()}
    encoder(nc, d)
    r = run_bass_kernel_spmd(nc, [{f"in_{n}": a for n, a in arrays.items()}], core_ids=[0]).results[0]
    o = {n: r[f"out_{n}"] for n in _OUTS}
    res = [o["y"][:SEQ].reshape(1, SEQ, D), o["y"][SEQ:].reshape(R, STEPS, D)]
    for n in list(_OUTS)[1:]:
        tail = (H, HD) if n[1] in "bcm" and n[-2:] != "lf" else (_OUTS[n][1],)
        lead = (DEPTH, 1, _OUTS[n][0] // DEPTH) if n[0] == "p" else (DEPTH, R, STEPS)
        res.append(o[n].reshape(lead + tail))
    return tuple(res)
```
